# Optimizing a Trainium2 kernel written in Bass

```python
import jax, jax.numpy as jnp
from jax import lax
import numpy as np

D_MODEL = 2048
BATCH = 1
SEQ = 256
DEPTH = 1

EPS = 1e-6
ROPE_THETA = 500000.0
GLA_HEADS = 4
GLA_DK = 128
GLA_DV = 256
GLA_LOWRANK = 16
GLA_TAU = 16.0
GLA_CHUNK = 64
NSA_HEADS = 16
NSA_GROUPS = 4
NSA_HPG = NSA_HEADS // NSA_GROUPS
NSA_DH = 128
ROPE_DIM = NSA_DH // 4
CMP_BLOCK = 32
CMP_STRIDE = 16
SLC_BLOCK = 64
SLC_TOPN = 16
WINDOW = 512
NSA_QCHUNK = 64
PEER_HEADS = 8
PEER_NKEYS = 128
PEER_EXPERTS = PEER_NKEYS * PEER_NKEYS
PEER_DKEY = 128
PEER_TOPK = 16
PEER_CHUNK = 128
NSA_Q_COLS = NSA_HEADS * NSA_DH
NSA_KV_COLS = NSA_GROUPS * NSA_DH
NSA_GATE_COLS = NSA_HEADS * 3
GLA_QK_COLS = GLA_HEADS * GLA_DK
GLA_V_COLS = GLA_HEADS * GLA_DV
MERGE_COLS = D_MODEL
IN_COLS = NSA_Q_COLS + 6 * NSA_KV_COLS + NSA_GATE_COLS + 2 * GLA_QK_COLS + 2 * GLA_V_COLS + GLA_LOWRANK + 2 * MERGE_COLS

kernel_name = "hybrid_gla_nsa_peer_block"

def rmsnorm(x, g):
    xf = x.astype(jnp.float32)
    y = xf * lax.rsqrt(jnp.mean(xf * xf, axis=-1, keepdims=True) + EPS)
    return (y * g.astype(jnp.float32)).astype(x.dtype)

def partial_rope(x, positions):
    half = ROPE_DIM // 2
    inv = jnp.power(ROPE_THETA, -(jnp.arange(0, ROPE_DIM, 2, dtype=jnp.float32) / ROPE_DIM))
    ang = positions.astype(jnp.float32)[..., None] * inv
    cos = jnp.cos(ang)[:, :, None, :]
    sin = jnp.sin(ang)[:, :, None, :]
    xr = x[..., :ROPE_DIM].astype(jnp.float32)
    x1, x2 = xr[..., :half], xr[..., half:]
    rot = jnp.concatenate([x1 * cos - x2 * sin, x2 * cos + x1 * sin], axis=-1).astype(x.dtype)
    return jnp.concatenate([rot, x[..., ROPE_DIM:]], axis=-1)

def masked_softmax(s, mask):
    s = jnp.where(mask, s, -jnp.inf)
    m = jnp.max(s, axis=-1, keepdims=True)
    m = jnp.where(jnp.isfinite(m), m, 0.0)
    p = jnp.where(mask, jnp.exp(s - m), 0.0)
    return p / jnp.maximum(jnp.sum(p, axis=-1, keepdims=True), 1e-30)

def gla_mixer(q, k, v, log_a, r, norm_g):
    B, S, H, _ = q.shape
    C = GLA_CHUNK
    nc = S // C

    def to_chunks(t):
        return t.astype(jnp.float32).reshape(B, nc, C, H, t.shape[-1]).transpose(1, 0, 3, 2, 4)

    qc = to_chunks(q * (GLA_DK ** -0.5))
    kc, vc, gc = to_chunks(k), to_chunks(v), to_chunks(log_a)
    causal = jnp.tril(jnp.ones((C, C), dtype=bool))

    def step(state, inp):
        qi, ki, vi, gi = inp
        b = jnp.cumsum(gi, axis=2)
        diff = b[:, :, :, None, :] - b[:, :, None, :, :]
        decay = jnp.exp(jnp.where(causal[:, :, None], diff, -jnp.inf))
        attn = jnp.einsum('bhtd,bhsd,bhtsd->bhts', qi, ki, decay)
        o = jnp.einsum('bhts,bhse->bhte', attn, vi) + jnp.einsum('bhtd,bhde->bhte', qi * jnp.exp(b), state)
        b_last = b[:, :, -1:, :]
        new_state = jnp.exp(b_last[:, :, 0, :])[..., None] * state + jnp.einsum('bhsd,bhse->bhde', ki * jnp.exp(b_last - b), vi)
        return new_state, o

    state0 = jnp.zeros((B, H, GLA_DK, GLA_DV), jnp.float32)
    _, o = lax.scan(step, state0, (qc, kc, vc, gc))
    o = o.transpose(1, 0, 3, 2, 4).reshape(B, S, H, GLA_DV)
    o = rmsnorm(o, norm_g).reshape(B, S, H * GLA_DV)
    return (o * jax.nn.silu(r.astype(jnp.float32))).astype(r.dtype)

def nsa_mixer(q, k_cmp, v_cmp, k_slc, v_slc, k_win, v_win, gates, pos_k, pos_v, k_w1, k_w2, v_w1, v_w2):
    B, S, H, dh = q.shape
    G = NSA_GROUPS
    dtype = q.dtype
    scale = dh ** -0.5
    qg = q.reshape(B, S, G, NSA_HPG, dh).transpose(0, 2, 3, 1, 4)

    def grp(t):
        return t.transpose(0, 2, 1, 3)

    n_cmp = (S - CMP_BLOCK) // CMP_STRIDE + 1
    blk_idx = jnp.arange(n_cmp)[:, None] * CMP_STRIDE + jnp.arange(CMP_BLOCK)[None, :]

    def compress(t, pos, w1, w2):
        blocks = t[:, :, blk_idx] + pos
        hid = jax.nn.gelu(blocks.reshape(B, G, n_cmp, CMP_BLOCK * dh) @ w1)
        return hid @ w2

    kc = compress(grp(k_cmp), pos_k, k_w1, k_w2)
    vc = compress(grp(v_cmp), pos_v, v_w1, v_w2)
    t_pos = jnp.arange(S)
    cmp_end = jnp.arange(n_cmp) * CMP_STRIDE + CMP_BLOCK - 1
    cmask = cmp_end[None, :] <= t_pos[:, None]
    s_cmp = jnp.einsum('bghsd,bgnd->bghsn', qg, kc).astype(jnp.float32) * scale
    p_cmp = masked_softmax(s_cmp, cmask)
    o_cmp = jnp.einsum('bghsn,bgnd->bghsd', p_cmp.astype(dtype), vc)

    n_slc = S // SLC_BLOCK
    top_n = min(SLC_TOPN, n_slc)
    ratio = SLC_BLOCK // CMP_STRIDE
    nrep = CMP_BLOCK // CMP_STRIDE
    p_grp = jnp.sum(p_cmp, axis=2)
    padded = jnp.pad(p_grp, ((0, 0), (0, 0), (0, 0), (nrep - 1, nrep - 1)))
    imp = jnp.zeros(p_grp.shape[:-1] + (n_slc,), jnp.float32)
    for m in range(ratio):
        for n in range(nrep):
            start = m - n + nrep - 1
            imp = imp + padded[..., start::ratio][..., :n_slc]
    blk_t = t_pos // SLC_BLOCK
    j = jnp.arange(n_slc)
    forced = (j[None, :] == 0) | (j[None, :] == blk_t[:, None]) | (j[None, :] == blk_t[:, None] - 1)
    future = j[None, :] > blk_t[:, None]
    imp = jnp.where(forced, 1e9, jnp.where(future, -1e9, imp))
    _, sel = lax.top_k(imp, top_n)

    k_blocks = grp(k_slc).reshape(B, G, n_slc, SLC_BLOCK, dh)
    v_blocks = grp(v_slc).reshape(B, G, n_slc, SLC_BLOCK, dh)
    kw_pad = jnp.pad(grp(k_win), ((0, 0), (0, 0), (WINDOW, 0), (0, 0)))
    vw_pad = jnp.pad(grp(v_win), ((0, 0), (0, 0), (WINDOW, 0), (0, 0)))
    QC = NSA_QCHUNK
    nq = S // QC
    q_chunks = qg.reshape(B, G, NSA_HPG, nq, QC, dh).transpose(3, 0, 1, 2, 4, 5)
    sel_chunks = sel.reshape(B, G, nq, QC, top_n).transpose(2, 0, 1, 3, 4)
    starts = jnp.arange(nq, dtype=jnp.int32) * QC
    bi = jnp.arange(B)[:, None, None, None]
    gi = jnp.arange(G)[None, :, None, None]

    def sweep(args):
        qc, sc, c0 = args
        tq = c0 + jnp.arange(QC)
        ks = k_blocks[bi, gi, sc].reshape(B, G, QC, top_n * SLC_BLOCK, dh)
        vs = v_blocks[bi, gi, sc].reshape(B, G, QC, top_n * SLC_BLOCK, dh)
        kpos = (sc[..., None] * SLC_BLOCK + jnp.arange(SLC_BLOCK)).reshape(B, G, QC, top_n * SLC_BLOCK)
        smask = (kpos <= tq[None, None, :, None])[:, :, None]
        s = jnp.einsum('bghqd,bgqkd->bghqk', qc, ks).astype(jnp.float32) * scale
        o_s = jnp.einsum('bghqk,bgqkd->bghqd', masked_softmax(s, smask).astype(dtype), vs)
        kw = lax.dynamic_slice_in_dim(kw_pad, c0, QC + WINDOW, axis=2)
        vw = lax.dynamic_slice_in_dim(vw_pad, c0, QC + WINDOW, axis=2)
        ppos = c0 + jnp.arange(QC + WINDOW)
        wmask = (ppos[None, :] > tq[:, None]) & (ppos[None, :] <= tq[:, None] + WINDOW) & (ppos[None, :] >= WINDOW)
        s = jnp.einsum('bghqd,bgkd->bghqk', qc, kw).astype(jnp.float32) * scale
        o_w = jnp.einsum('bghqk,bgkd->bghqd', masked_softmax(s, wmask).astype(dtype), vw)
        return o_s, o_w

    o_slc, o_win = lax.map(sweep, (q_chunks, sel_chunks, starts))
    o_slc = o_slc.transpose(1, 2, 3, 0, 4, 5).reshape(B, G, NSA_HPG, S, dh)
    o_win = o_win.transpose(1, 2, 3, 0, 4, 5).reshape(B, G, NSA_HPG, S, dh)

    g = jax.nn.sigmoid(gates.astype(jnp.float32)).reshape(B, S, G, NSA_HPG, 3).transpose(0, 2, 3, 1, 4)
    o = g[..., 0:1] * o_cmp + g[..., 1:2] * o_slc + g[..., 2:3] * o_win
    return o.transpose(0, 3, 1, 2, 4).reshape(B, S, H * dh).astype(dtype)

def peer(xn, w_q, sub_k1, sub_k2, u_tab, v_tab):
    B, S, D = xn.shape
    T = B * S
    xt = xn.reshape(T, D)
    qp = (xt @ w_q).reshape(T, PEER_HEADS, PEER_DKEY)
    half = PEER_DKEY // 2
    s1 = jnp.einsum('thd,hnd->thn', qp[..., :half], sub_k1).astype(jnp.float32)
    s2 = jnp.einsum('thd,hnd->thn', qp[..., half:], sub_k2).astype(jnp.float32)
    v1, i1 = lax.top_k(s1, PEER_TOPK)
    v2, i2 = lax.top_k(s2, PEER_TOPK)
    cand = (v1[..., :, None] + v2[..., None, :]).reshape(T, PEER_HEADS, PEER_TOPK * PEER_TOPK)
    vals, flat = lax.top_k(cand, PEER_TOPK)
    e1 = jnp.take_along_axis(i1, flat // PEER_TOPK, axis=-1)
    e2 = jnp.take_along_axis(i2, flat % PEER_TOPK, axis=-1)
    experts = e1 * PEER_NKEYS + e2
    gates = jax.nn.softmax(vals, axis=-1)
    nchunk = T // PEER_CHUNK

    def expert_chunk(args):
        xc, ec, gc = args
        hid = jax.nn.gelu(jnp.einsum('cd,chkd->chk', xc, u_tab[ec]).astype(jnp.float32))
        return jnp.einsum('chk,chkd->cd', (gc * hid).astype(xc.dtype), v_tab[ec])

    out = lax.map(expert_chunk, (xt.reshape(nchunk, PEER_CHUNK, D),
                                 experts.reshape(nchunk, PEER_CHUNK, PEER_HEADS, PEER_TOPK),
                                 gates.reshape(nchunk, PEER_CHUNK, PEER_HEADS, PEER_TOPK)))
    return out.reshape(B, S, D)

def setup_inputs(seed: int = 0) -> dict:
    key = jax.random.key(seed)
    ks = jax.random.split(key, 24)
    f32 = jnp.float32
    L, D = DEPTH, D_MODEL

    def nrm(k, shape, scale):
        return jax.random.normal(k, shape, f32) * scale

    offs = jax.random.randint(ks[1], (BATCH, 1), 0, 1024, dtype=jnp.int32)
    positions = offs + jnp.arange(SEQ, dtype=jnp.int32)[None, :]
    return {
        "x": nrm(ks[0], (BATCH, SEQ, D), 1.0),
        "positions": positions,
        "norm1_g": 1.0 + nrm(ks[2], (L, D), 0.02),
        "w_in": nrm(ks[3], (L, D, IN_COLS), D ** -0.5),
        "gla_w_decay": nrm(ks[4], (L, GLA_LOWRANK, GLA_QK_COLS), GLA_LOWRANK ** -0.5),
        "gla_b_decay": nrm(ks[5], (L, GLA_QK_COLS), 0.1),
        "gla_norm_g": 1.0 + nrm(ks[6], (L, GLA_DV), 0.02),
        "nsa_cmp_pos_k": nrm(ks[7], (L, CMP_BLOCK, NSA_DH), 0.02),
        "nsa_cmp_pos_v": nrm(ks[8], (L, CMP_BLOCK, NSA_DH), 0.02),
        "nsa_cmp_k_w1": nrm(ks[9], (L, CMP_BLOCK * NSA_DH, NSA_DH), (CMP_BLOCK * NSA_DH) ** -0.5),
        "nsa_cmp_k_w2": nrm(ks[10], (L, NSA_DH, NSA_DH), NSA_DH ** -0.5),
        "nsa_cmp_v_w1": nrm(ks[11], (L, CMP_BLOCK * NSA_DH, NSA_DH), (CMP_BLOCK * NSA_DH) ** -0.5),
        "nsa_cmp_v_w2": nrm(ks[12], (L, NSA_DH, NSA_DH), NSA_DH ** -0.5),
        "w_up_gla": nrm(ks[13], (L, GLA_V_COLS, D), GLA_V_COLS ** -0.5),
        "w_up_nsa": nrm(ks[14], (L, NSA_Q_COLS, D), NSA_Q_COLS ** -0.5),
        "w_out": nrm(ks[15], (L, D, D), D ** -0.5),
        "norm2_g": 1.0 + nrm(ks[16], (L, D), 0.02),
        "peer_w_q": nrm(ks[17], (L, D, PEER_HEADS * PEER_DKEY), D ** -0.5),
        "peer_sub_k1": nrm(ks[18], (L, PEER_HEADS, PEER_NKEYS, PEER_DKEY // 2), (PEER_DKEY // 2) ** -0.5),
        "peer_sub_k2": nrm(ks[19], (L, PEER_HEADS, PEER_NKEYS, PEER_DKEY // 2), (PEER_DKEY // 2) ** -0.5),
        "peer_u": nrm(ks[20], (L, PEER_EXPERTS, D), D ** -0.5),
        "peer_v": nrm(ks[21], (L, PEER_EXPERTS, D), PEER_HEADS ** -0.5),
        "final_g": 1.0 + nrm(ks[22], (D,), 0.02),
    }

def reference(x, positions, norm1_g, w_in, gla_w_decay, gla_b_decay, gla_norm_g, nsa_cmp_pos_k, nsa_cmp_pos_v,
              nsa_cmp_k_w1, nsa_cmp_k_w2, nsa_cmp_v_w1, nsa_cmp_v_w2, w_up_gla, w_up_nsa, w_out, norm2_g,
              peer_w_q, peer_sub_k1, peer_sub_k2, peer_u, peer_v, final_g):
    B, S, D = x.shape
    widths = [NSA_Q_COLS] + [NSA_KV_COLS] * 6 + [NSA_GATE_COLS, GLA_QK_COLS, GLA_QK_COLS, GLA_V_COLS,
                                                 GLA_LOWRANK, GLA_V_COLS, MERGE_COLS, MERGE_COLS]
    offsets = np.cumsum(widths)[:-1].tolist()
    for l in range(DEPTH):
        h = rmsnorm(x, norm1_g[l])
        proj = h @ w_in[l]
        (nq, kcm, vcm, ksl, vsl, kwn, vwn, ngate, gq, gk, gv, glr, gr, gate_a, gate_b) = jnp.split(proj, offsets, axis=-1)

        log_a = jax.nn.log_sigmoid((glr @ gla_w_decay[l] + gla_b_decay[l]).astype(jnp.float32)) / GLA_TAU
        y_gla = gla_mixer(gq.reshape(B, S, GLA_HEADS, GLA_DK), gk.reshape(B, S, GLA_HEADS, GLA_DK),
                          gv.reshape(B, S, GLA_HEADS, GLA_DV), log_a.reshape(B, S, GLA_HEADS, GLA_DK),
                          gr, gla_norm_g[l])

        def kv(t):
            return t.reshape(B, S, NSA_GROUPS, NSA_DH)
        q_n = partial_rope(nq.reshape(B, S, NSA_HEADS, NSA_DH), positions)
        y_nsa = nsa_mixer(q_n, partial_rope(kv(kcm), positions), kv(vcm), partial_rope(kv(ksl), positions), kv(vsl),
                          partial_rope(kv(kwn), positions), kv(vwn), ngate,
                          nsa_cmp_pos_k[l], nsa_cmp_pos_v[l], nsa_cmp_k_w1[l], nsa_cmp_k_w2[l],
                          nsa_cmp_v_w1[l], nsa_cmp_v_w2[l])

        ga = jax.nn.sigmoid(gate_a.astype(jnp.float32))
        gb = jax.nn.sigmoid(gate_b.astype(jnp.float32))
        merged = (ga * (y_gla @ w_up_gla[l]) + gb * (y_nsa @ w_up_nsa[l])).astype(x.dtype)
        x = x + merged @ w_out[l]

        h2 = rmsnorm(x, norm2_g[l])
        x = x + peer(h2, peer_w_q[l], peer_sub_k1[l], peer_sub_k2[l], peer_u[l], peer_v[l])
    return rmsnorm(x, final_g)


_drawn_inputs = setup_inputs


def setup_inputs(seed=0):
    import zlib

    import numpy as np

    out = dict(_drawn_inputs(seed))
    spreads = {}
    factors = {'gla_norm_g': 3.463,
     'nsa_cmp_pos_k': 64.0,
     'nsa_cmp_pos_v': 18.763,
     'final_g': 8.01,
     'norm2_g': 3.212}
    for name, (base, spread) in spreads.items():
        noise = np.random.default_rng([zlib.crc32(name.encode()), seed]).standard_normal(out[name].shape)
        drawn = base * np.exp(spread * noise) if base else spread * noise
        out[name] = __import__('jax').numpy.asarray(drawn.astype(out[name].dtype))
    for name, factor in factors.items():
        out[name] = (out[name] * factor).astype(out[name].dtype)
    return out
```

```python
from contextlib import ExitStack

import concourse.bass as bass
import numpy as np
from concourse import mybir

F32 = mybir.dt.float32
F32R = mybir.dt.float32r
BF16 = mybir.dt.bfloat16
I32 = mybir.dt.int32
U32 = mybir.dt.uint32
ALU = mybir.AluOpType
ACT = mybir.ActivationFunctionType
AX = mybir.AxisListType
ds = bass.ds

P = 128
D = 2048
S = 256
NT = S // P
KC = D // P
NB = 512
CU = 4
UW = CU * NB
EPS = 1e-6

GLA_H, GLA_DK, GLA_DV, GLA_LR, GLA_TAU = 4, 128, 256, 16, 16.0
NSA_G, NSA_HPG, DH = 4, 4, 128
NSA_H = NSA_G * NSA_HPG
ROT = DH // 4
HALF = ROT // 2
ROPE_THETA = 500000.0
CMP_BLOCK, CMP_STRIDE = 32, 16
NCMP = (S - CMP_BLOCK) // CMP_STRIDE + 1
PEER_H, PEER_NK, PEER_DK, TOPK = 8, 128, 128, 16
SCALE = float(DH) ** -0.5
MASKED = -1e30
MASKED_MAX = -1e29

B_KCM, B_VCM, B_KSL, B_VSL, B_KWN, B_VWN, B_GQ, B_GK, B_GV, B_GR, B_NQ, B_GA, B_GB = 0, 1, 2, 3, 4, 5, 6, 7, 8, 10, 12, 16, 20
PROJ_BLOCKS = 24
A_BLOCKS = 12
UPB = KC // CU
UPG = GLA_H * GLA_DV // P // CU
UNITS = PROJ_BLOCKS * UPB + 4 * (UPG + UPB) + 4 * UPB + 2 * UPB
RAW = 4
SPLIT = 2

LEVELS = [64, 32, 16, 8, 4, 2, 1]
NL = len(LEVELS) + 2
L128, LDIAG = len(LEVELS), len(LEVELS) + 1

RING = 8
UNITS_P = NT * PEER_H


def hybrid_block(nc, io):
    ctx = ExitStack()
    with ctx:
        def sem(name):
            return ctx.enter_context(nc.semaphore(name))

        def place(stack, name, shape, dt=F32):
            return stack.enter_context(nc.sbuf_tensor(name, shape, dt))

        KB = 1024
        buf = {}

        def region(offset, limit, *specs):
            with ExitStack() as stack:
                if offset:
                    stack.enter_context(nc.sbuf_tensor(f"below_{specs[0][0]}", [P, offset], mybir.dt.uint8))
                size = 0
                for name, shape, *dt in specs:
                    dt = dt[0] if dt else F32
                    buf[name] = stack.enter_context(nc.sbuf_tensor(name, shape, dt))
                    size += int(np.prod(shape[1:])) * (2 if dt == BF16 else 4)
                assert offset + size <= limit, (specs[0][0], offset + size, limit)

        AT_W, AT_EVAC, AT_YG, AT_MIX, AT_YN, AT_NSA, AT_X, END = (n * KB - 256 for n in (1, 65, 73, 89, 130, 162, 192, 208))
        nlev = len(LEVELS) + 1
        region(0, AT_W, ("ident", [P, P]), ("rstd1", [P, NT]), ("rstd2", [P, NT]), ("stat", [P, 16]), ("newton", [P, NT]), ("sq_x1", [P, NT, 4]))
        region(AT_W, AT_EVAC, ("w_raw", [P, RAW, UW]), ("w_hi", [P, SPLIT, UW], F32R), ("w_lo", [P, SPLIT, UW], F32R))
        region(AT_EVAC, AT_YG, ("evac", [P, 2, NT, NB]))
        region(AT_YG, AT_MIX, ("ygT_hi", [P, 2 * GLA_H, S], F32R), ("ygT_lo", [P, 2 * GLA_H, S], F32R))
        region(AT_YN, AT_NSA, ("ynT_hi", [P, NSA_H, S], F32R), ("ynT_lo", [P, NSA_H, S], F32R))
        region(AT_X, END, ("x_nat", [P, NT, D]))
        region(AT_MIX, AT_YN, ("hT_hi", [P, KC, S], F32R), ("hT_lo", [P, KC, S], F32R), ("gates", [P, NT, 3 * NSA_H]),
               ("cos_t", [P, NT, HALF]), ("sin_t", [P, NT, HALF]), ("kcT", [P, NSA_G * NCMP]), ("vc", [NCMP, NSA_G, DH]),
               ("tri", [P, S]), ("cmask", [P, NT, NCMP]), ("bT", [P, GLA_H, S]), ("glr", [P, NT, GLA_LR]))
        region(AT_YN, AT_X, ("xgT", [P, KC, S]), ("g1", [P, KC]), ("w_small", [P, KC, 64]), ("pos_i", [P, NT], I32),
               ("pos_f", [P, NT]), ("inv_f", [P, HALF]), ("ang", [P, NT, HALF]), ("turns", [P, NT, HALF]), ("sq_junk", [P, D]))
        region(AT_YN, AT_X, ("glrT", [GLA_LR, S]), ("w_decay", [GLA_LR, GLA_H * GLA_DK]), ("b_decay", [P, GLA_H]),
               ("kv_c", [P, 2, NT, NSA_G * DH]), ("rot_c", [P, 4, NT, NSA_G, HALF]), ("kvT_c", [P, 2, NSA_G, S]),
               ("blk_c", [P, 2, CMP_BLOCK, NSA_G, NCMP]), ("posT", [P, 2, CMP_BLOCK]), ("w1", [P, 2, CMP_BLOCK // 4, DH]),
               ("w2", [P, 2, DH]), ("hid_c", [P, 2, NSA_G * NCMP]))
        region(AT_YN, AT_X, ("masks", [P, nlev, P]), ("gnorm", [P, GLA_DV]), ("qk_g", [P, 2, NT, GLA_DK]), ("v_g", [P, NT, GLA_DV]),
               ("r_g", [P, NT, GLA_DV]), ("sig_g", [P, NT, GLA_DV]), ("qT_g", [P, S]), ("kT_g", [P, S]), ("dec", [P, NL, S]),
               ("qL", [P, NL, S]), ("kL", [P, NL, S]), ("att_m", [P, nlev, P]), ("att_T", [P, 3, P]), ("y_g", [P, NT, GLA_DV]), ("gst", [P, 8]))
        region(AT_NSA, AT_X, ("qk_n", [P, NT, NSA_HPG + 2, DH]), ("rot_n", [P, 4, NT, NSA_HPG + 2, HALF]), ("v_n", [P, 2, NT, DH]),
               ("qkT", [P, NSA_HPG + 2, S]), ("g_n", [P, NT, 3 * NSA_HPG]), ("vc_n", [NCMP, DH]), ("sm", [P, 2, 3 * S]),
               ("smc", [P, 2, NT, NCMP]), ("mx", [P, 2, NT, 3]), ("nmx", [P, 2, NT, 3]), ("sums", [P, 2, NT, 3]), ("wts", [P, 2, NT, 3]),
               ("pT", [P, 4, S]), ("pcT", [NCMP, S]))
        region(AT_MIX, AT_YN, ("mT_hi", [P, KC, S], F32R), ("mT_lo", [P, KC, S], F32R), ("g2", [P, D]))
        region(AT_NSA, AT_X, ("gab", [P, 2, NT, NB]))
        region(AT_MIX, AT_YN, ("qp", [P, NT, PEER_H * PEER_DK]), ("qpT", [P, PEER_H, S]), ("keys", [P, PEER_H, 2 * PEER_NK]))
        region(AT_W, AT_EVAC, ("h2", [P, NT, D]), ("sc", [P, NT * PEER_H, 2 * PEER_NK]))
        region(AT_W + 32 * KB, AT_X, ("ring", [P, RING, 2 * D]), ("junk", [P, 2, D], BF16), ("gf", [P, D]), ("diag", [P, 4, P]),
               ("iota16", [P, TOPK]), ("s_now", [P, 2, PEER_NK]), ("s_cut", [P, 2, PEER_NK]), ("v_top", [P, 2, TOPK]),
               ("i_top", [P, 2, TOPK], U32), ("if_top", [P, 2, TOPK]), ("cand", [P, TOPK, TOPK]), ("cand_cut", [P, TOPK, TOPK]),
               ("vals", [P, TOPK]), ("flat", [P, TOPK], U32), ("ab", [P, 2, TOPK], U32), ("abf", [P, 2, TOPK]),
               ("hot", [P, 2, TOPK, TOPK]), ("e12", [P, 2, TOPK]), ("rexp", [P, TOPK]), ("rst", [P, 4]), ("e_idx", [P, 2, TOPK], I32),
               ("e_gate", [P, 2, TOPK]), ("hid", [P, 2, TOPK]), ("act_h", [P, 2, TOPK]), ("zeros", [P, P]))
        ident, rstd1, rstd2, stat, sq_x1, w_raw, w_hi, w_lo, evac = (buf["ident"], buf["rstd1"], buf["rstd2"], buf["stat"], buf["sq_x1"], buf["w_raw"], buf["w_hi"], buf["w_lo"], buf["evac"])
        ygT_hi, ygT_lo, ynT_hi, ynT_lo, x_nat, hT_hi, hT_lo, gates, cos_t = (buf["ygT_hi"], buf["ygT_lo"], buf["ynT_hi"], buf["ynT_lo"], buf["x_nat"], buf["hT_hi"], buf["hT_lo"], buf["gates"], buf["cos_t"])
        sin_t, kcT, vc, tri, cmask, bT, xgT, g1, w_small = (buf["sin_t"], buf["kcT"], buf["vc"], buf["tri"], buf["cmask"], buf["bT"], buf["xgT"], buf["g1"], buf["w_small"])
        pos_i, pos_f, inv_f, ang, turns, sq_junk, glrT, w_decay, b_decay = (buf["pos_i"], buf["pos_f"], buf["inv_f"], buf["ang"], buf["turns"], buf["sq_junk"], buf["glrT"], buf["w_decay"], buf["b_decay"])
        kv_c, rot_c, kvT_c, blk_c, posT, w1, w2, hid_c, masks = (buf["kv_c"], buf["rot_c"], buf["kvT_c"], buf["blk_c"], buf["posT"], buf["w1"], buf["w2"], buf["hid_c"], buf["masks"])
        gnorm, qk_g, v_g, r_g, sig_g, qT_g, kT_g, dec, qL = (buf["gnorm"], buf["qk_g"], buf["v_g"], buf["r_g"], buf["sig_g"], buf["qT_g"], buf["kT_g"], buf["dec"], buf["qL"])
        kL, att_m, att_T, y_g, gst, qk_n, rot_n, v_n, qkT = (buf["kL"], buf["att_m"], buf["att_T"], buf["y_g"], buf["gst"], buf["qk_n"], buf["rot_n"], buf["v_n"], buf["qkT"])
        g_n, vc_n, sm, smc, mx, nmx, sums, wts, pT = (buf["g_n"], buf["vc_n"], buf["sm"], buf["smc"], buf["mx"], buf["nmx"], buf["sums"], buf["wts"], buf["pT"])
        pcT, mT_hi, mT_lo, g2, gab, qp, qpT, keys, h2 = (buf["pcT"], buf["mT_hi"], buf["mT_lo"], buf["g2"], buf["gab"], buf["qp"], buf["qpT"], buf["keys"], buf["h2"])
        sc, ring, junk, gf, diag, iota16, s_now, s_cut, v_top = (buf["sc"], buf["ring"], buf["junk"], buf["gf"], buf["diag"], buf["iota16"], buf["s_now"], buf["s_cut"], buf["v_top"])
        i_top, if_top, cand, cand_cut, vals, flat, ab, abf, hot = (buf["i_top"], buf["if_top"], buf["cand"], buf["cand_cut"], buf["vals"], buf["flat"], buf["ab"], buf["abf"], buf["hot"])
        e12, rexp, rst, e_idx, e_gate, hid, act_h, zeros = (buf["e12"], buf["rexp"], buf["rst"], buf["e_idx"], buf["e_gate"], buf["hid"], buf["act_h"], buf["zeros"])
        glr, newton = buf["glr"], buf["newton"]
        mrg = evac
        h2T_hi, h2T_lo = ynT_hi, ynT_lo
        zT = kv_c[:, 0, :, :].rearrange("p t n -> p (t n)")
        zA = kv_c[:, 1, :, :].rearrange("p t n -> p (t n)")

        psum = ctx.enter_context(nc.psum_tensor("psum", [P, 8, NB], F32))
        proj = nc.dram_tensor("proj_scratch", [PROJ_BLOCKS, P, NT, NB], F32, kind="Internal").ap()

        def sems(*names):
            return [sem(n) for n in names]

        xT_in, xn_in, const_in, small_in, ssq1, ms1_done, sq1_done, rs1_done = sems(
            "xT_in", "xn_in", "const_in", "small_in", "ssq1", "ms1_done", "sq1_done", "rs1_done")
        xg_done, h_hi, h_lo, ang_ready, trig_done, small_done, small_out = sems(
            "xg_done", "h_hi", "h_lo", "ang_ready", "trig_done", "small_done", "small_out")
        v_step, a_step = sems("v_step", "a_step")
        w_in_s = sems(*(f"w_landed{k}" for k in range(RAW)))
        hi_done, lo_done, unit_done, evac_done = sems("hi_done", "lo_done", "unit_done", "evac_done")
        stored = sems("stored0", "stored1")
        prep_in, kvc_in, w1_used, pe_prep, act_prep, dve_prep = sems("prep_in", "kvc_in", "w1_used", "pe_prep", "act_prep", "dve_prep")
        w1_in = sems("w1_in0", "w1_in1")
        g_msk, g_in, g_qkt, g_qe, g_ke, g_dec, g_exp, g_ql, g_kl = sems(
            "g_consts_in", "g_in", "g_turned", "g_q_out", "g_k_out", "g_decay", "g_exp", "g_q_scaled", "g_k_scaled")
        g_lev, g_att, g_a01, g_o, g_rn, g_sig, g_y, g_yt, g_yhi, g_ylo = sems(
            "g_levels", "g_att", "g_att01", "g_out", "g_rnorm", "g_sig", "g_y", "g_y_turned", "g_y_hi", "g_y_lo")
        nqk_in, nv_in, roped, qkt_done, qkt_a, qkt_v, vcn_done = sems(
            "n_qk_in", "n_v_in", "n_roped", "n_qk_turned", "n_qk_out_act", "n_qk_out_dve", "n_vc_ready")
        s_done, mx_done, exp_done, p_done, pt_done, pt_a, pt_v, pv_done, o_hi, o_lo = sems(
            "scores_done", "max_done", "exp_done", "probs_done", "probs_turned", "pT_out_act", "pT_out_dve", "pv_done", "o_hi", "o_lo")
        gab_in, gab_sig, m_done, mt_done, m_hi, m_lo, g2_in = sems(
            "gates_in", "gates_sig", "merge_read", "merged_turned", "m_hi", "m_lo", "g2_in")
        x1_done, sq2, xg2_done, xt_done, x_hi, x_lo, ms2_done, sq2_done, rs2_done, h2_done = sems(
            "x1_done", "sq2", "xg2_done", "xg2_turned", "x_hi", "x_lo", "ms2_done", "sq2_done", "rs2_done", "h2_done")
        qp_done, qpt_done, qpt_out, sc_done, sc_out, keys_in, gf_in = sems(
            "query_out", "query_turned", "queryT_out", "sc_done", "sc_out", "keys_in", "gf_in")
        routed, r_vals, r_exp = sems("routed", "r_vals", "r_exp")
        landed = sems(*(f"row_landed{k}" for k in range(RING)))
        dot_done, act_done, diag_done, acc_done, zero_done = sems("dot_done", "act_done", "diag_done", "acc_done", "zero_done")
        x2_done, fsq, fms, frs, out_done, out_st = sems("x2_done", "fsq", "fms", "frs", "out_done", "out_stored")

        block = ctx.enter_context(nc.Block())

        def wait_alone(eng, s, value):
            eng.wait_ge(s, value)
            eng.nop(nofuse=True)

        class Steps:

            def __init__(self, eng, s):
                self.eng, self.s, self.n, self.base = eng, s, 0, 0

            def __call__(self, ins, alone=False):
                self.n += 1
                ins.then_inc(self.s, 1)
                self.eng.wait_ge(self.s, self.base + self.n)
                if alone:
                    self.eng.nop(nofuse=True)

            def enter(self, i, first, per):
                self.start, self.per = self.n, per
                self.base, self.first = (i - first) * per, first

            def leave(self, count):
                assert self.n - self.start == self.per, (self.n - self.start, self.per)
                self.n = self.start + self.per * count
                self.base = 0

        @block.sync
        def _(sp):
            for q in range(4):
                sp.dma_start(xgT[:, 4 * q:4 * q + 4, :], io["xT"][:, 4 * q:4 * q + 4, :]).then_inc(xT_in, 16)
            sp.dma_start(w_small[:, :, :], io["w_small"]).then_inc(small_in, 16)
            for s in range(RAW):
                sp.dma_start(w_raw[:, s, :], io["w_units"][s]).then_inc(w_in_s[s], 16)
            with sp.Fori(1, UNITS // RAW) as i:
                for s in range(RAW):
                    sp.wait_ge(hi_done, i * RAW + (s - RAW + 1))
                    sp.wait_ge(lo_done, i * RAW + (s - RAW + 1))
                    sp.dma_start(w_raw[:, s, :], io["w_units"][ds(i * RAW + s, 1), :, :].rearrange("a p n -> p (a n)")).then_inc(w_in_s[s], 16)
            for t in range(NT):
                sp.wait_ge(out_done, t + 1)
                sp.dma_start(io["out"][t * P:(t + 1) * P, :], h2[:, t, :]).then_inc(out_st, 16)
            sp.wait_ge(out_st, 16 * NT)

        @block.gpsimd
        def _(pool):
            pool.wait_ge(small_done, 1)
            pool.wait_ge(h_lo, 4)
            pool.wait_ge(trig_done, 2)
            for dst, name in ((w_decay[:, :], "w_decay"), (b_decay[:, :], "b_decay"), (posT[:, :, :], "posT"), (w2[:, :, :], "w2")):
                pool.dma_start(dst, io[name]).then_inc(prep_in, 16)
            pool.wait_ge(stored[0], 16)
            pool.wait_ge(stored[1], 16)
            pool.wait_ge(dve_prep, 9)
            for a, b in ((0, B_KCM), (1, B_VCM)):
                pool.dma_start(kv_c[:, a, :, :], proj[b]).then_inc(kvc_in, 16)
            for n in range(8):
                if n >= 2:
                    pool.wait_ge(w1_used, n - 1)
                pool.dma_start(w1[:, n % 2, :, :], io["w1"][n]).then_inc(w1_in[n % 2], 16)

            pool.wait_ge(pe_prep, 5)
            pool.wait_ge(act_prep, 8)
            pool.wait_ge(dve_prep, 11)
            pool.dma_start(masks[:, :, :], io["gla_masks"]).then_inc(g_msk, 16)
            pool.dma_start(gnorm[:, :], io["gla_g"].partition_broadcast(P)).then_inc(g_msk, 16)
            for k in range(2):
                pool.wait_ge(stored[k], 16 * A_BLOCKS // 2)
            with pool.Fori(0, GLA_H // 2) as i:
                for hp in range(2):
                    h = i * 2 + hp
                    wait_alone(pool, g_y, h)
                    wait_alone(pool, g_o, h)
                    wait_alone(pool, g_sig, h)
                    for a, b in ((0, B_GQ), (1, B_GK)):
                        pool.dma_start(qk_g[:, a, :, :], proj[b][:, :, ds(h * GLA_DK, GLA_DK)]).then_inc(g_in, 16)
                    for dst, b in ((v_g, B_GV), (r_g, B_GR)):
                        pool.dma_start(dst[:, :, :], proj[ds(i + b, 1), :, :, hp * GLA_DV:(hp + 1) * GLA_DV].rearrange("a p t n -> p (a t) n")).then_inc(g_in, 16)
                    wait_alone(pool, g_exp, h + 1)
                    wait_alone(pool, g_ke, h + 1)
                    pool.tensor_tensor(kL[:, :, :], dec[:, :, :], kT_g[:, None, :].to_broadcast([P, NL, S]), ALU.mult).then_inc(g_kl, 1)

            pool.wait_ge(g_ylo, GLA_H)
            pool.wait_ge(g_yhi, GLA_H)
            pool.wait_ge(stored[0], 16 * (A_BLOCKS + 4) // 2)
            pool.wait_ge(stored[1], 16 * (A_BLOCKS + 4) // 2)
            with pool.Fori(0, NSA_G) as g:
                wait_alone(pool, qkt_done, g)
                wait_alone(pool, pv_done, g * NSA_HPG)
                pool.dma_start(qk_n[:, :, 0:NSA_HPG, :], proj[ds(g + B_NQ, 1), :, :, :].rearrange("a p t (h d) -> p (a t) h d", d=DH)).then_inc(nqk_in, 16)
                for a, b in ((NSA_HPG, B_KSL), (NSA_HPG + 1, B_KWN)):
                    pool.dma_start(qk_n[:, :, a, :], proj[b][:, :, ds(g * DH, DH)]).then_inc(nqk_in, 16)
                for a, b in ((0, B_VSL), (1, B_VWN)):
                    pool.dma_start(v_n[:, a, :, :], proj[b][:, :, ds(g * DH, DH)]).then_inc(nv_in, 16)

            pool.wait_ge(pv_done, NSA_H)
            pool.wait_ge(o_lo, NSA_H)
            pool.wait_ge(unit_done, PROJ_BLOCKS * UPB)
            pool.wait_ge(stored[0], 16 * PROJ_BLOCKS // 2)
            pool.wait_ge(stored[1], 16 * PROJ_BLOCKS // 2)
            pool.dma_start(g2[:, :], io["g2"].partition_broadcast(P)).then_inc(g2_in, 16)
            with pool.Fori(0, 4) as nb:
                wait_alone(pool, m_done, nb * 2)
                for a, b in ((0, B_GA), (1, B_GB)):
                    pool.dma_start(gab[:, a, :, :], proj[ds(nb + b, 1), :, :, :].rearrange("a p t n -> p (a t) n")).then_inc(gab_in, 16)

            pool.wait_ge(unit_done, UNITS)
            pool.wait_ge(x_lo, 4)
            pool.dma_start(keys[:, :, :], io["keys"]).then_inc(keys_in, 16)
            pool.wait_ge(sc_out, 2)
            pool.wait_ge(h2_done, 1)
            pool.dma_start(gf[:, :], io["gf"].partition_broadcast(P)).then_inc(gf_in, 16)
            pool.dma_start(iota16[:, :], io["iota16"].partition_broadcast(P)).then_inc(gf_in, 16)

            def gather(u, par, first):
                wait_alone(pool, routed, u + 1)
                for k in range(TOPK):
                    slot = (par * TOPK + k) % RING
                    if not (first and k < RING):
                        wait_alone(pool, acc_done, u * TOPK + (k - RING + 1))
                    pool.indirect_dma_start(ring[:, slot, :], None, io["uv"],
                                            bass.IndirectOffsetOnAxis(ap=e_idx[:, par, k:k + 1], axis=0)).then_inc(landed[slot], 16)

            gather(0, 0, True)
            gather(1, 1, False)
            with pool.Fori(1, UNITS_P // 2) as i:
                gather(i * 2, 0, False)
                gather(i * 2 + 1, 1, False)

        @block.scalar
        def _(act):
            step = Steps(act, a_step)

            def hi(n, s):
                act.wait_ge(w_in_s[s % RAW], (n - s % RAW) * (16 // RAW) + 16)
                wait = n - (SPLIT - 1)
                if not (isinstance(wait, int) and wait <= 0):
                    act.wait_ge(unit_done, wait)
                act.activation(w_hi[:, s % SPLIT, :], w_raw[:, s % RAW, :], ACT.Copy).then_inc(hi_done, 1)

            def evacuate(b, par, first=False):
                act.wait_ge(unit_done, b * UPB + UPB)
                if not first:
                    act.wait_ge(stored[par], (b - par) * 8)
                for t in range(NT):
                    act.activation(evac[:, par, t, :], psum[:, 2 * par + t, :], ACT.Copy, scale=rstd1[:, t:t + 1]).then_inc(evac_done, 1)
                act.wait_ge(evac_done, b * 2 + 2)
                dst = proj[b] if isinstance(b, int) else proj[ds(b, 1), :, :, :].rearrange("a p t n -> p (a t) n")
                act.dma_start(dst, evac[:, par, :, :]).then_inc(stored[par], 16)

            act.dma_start(x_nat[:, :, :], io["x"]).then_inc(xn_in, 16)
            for dst, name in ((g1[:, :], "g1"), (ident[:, :], "ident"), (pos_i[:, :], "positions"),
                              (tri[:, :], "tri"), (cmask[:, :, :], "cmask")):
                act.dma_start(dst, io[name]).then_inc(const_in, 16)
            act.dma_start(inv_f[:, :], io["inv_f"].partition_broadcast(P)).then_inc(const_in, 16)
            act.wait_ge(xn_in, 16)
            for t in range(NT):
                act.activation(sq_junk[:, :], x_nat[:, t, :], ACT.Square,
                               accum_out=stat[:, t:t + 1]).then_inc(ssq1, 1)
                act.wait_ge(ssq1, t + 1)
            for q in range(4):
                act.wait_ge(xg_done, q + 1)
                act.activation(hT_hi[:, 4 * q:4 * q + 4, :], xgT[:, 4 * q:4 * q + 4, :], ACT.Copy).then_inc(h_hi, 1)
                if q == 0:
                    hi(0, 0)
            act.wait_ge(ms1_done, 1)
            act.activation(stat[:, 4:6], stat[:, 2:4], ACT.Sqrt).then_inc(sq1_done, 1)
            act.wait_ge(ang_ready, 1)
            act.activation(sin_t[:, :, :], ang[:, :, :], ACT.Sin).then_inc(trig_done, 1)
            act.activation(turns[:, :, :], ang[:, :, :], ACT.Sin, scale=0.5).then_inc(trig_done, 1)
            act.wait_ge(small_done, 1)
            act.wait_ge(rs1_done, 1)
            for t in range(NT):
                act.activation(glr[:, t, :], psum[:, 4, t * 64:t * 64 + GLA_LR], ACT.Copy, scale=rstd1[:, t:t + 1]).then_inc(small_out, 1)
                act.activation(gates[:, t, :], psum[:, 4, t * 64 + GLA_LR:(t + 1) * 64], ACT.Sigmoid, scale=rstd1[:, t:t + 1]).then_inc(small_out, 1)
            hi(1, 1)

            for b in range(2):
                for k in range(UPB):
                    if b * UPB + k >= 1:
                        hi(b * UPB + k + 1, (b * UPB + k + 1) % 4)
                evacuate(b, b, True)
            with act.Fori(1, A_BLOCKS // 2) as i:
                for par in range(2):
                    for k in range(UPB):
                        hi(i * 8 + (par * 4 + k + 1), k + 1)
                    evacuate(i * 2 + par, par)

            act.wait_ge(pe_prep, 1)
            act.activation(glrT[:, :], psum[0:GLA_LR, 4, 0:S], ACT.Copy).then_inc(act_prep, 1)
            act.wait_ge(dve_prep, 4)
            step(act.activation(zA, zT, ACT.Abs))
            step(act.activation(zA, zA, ACT.Exp, scale=-1.0))
            act.activation(zA, zA, ACT.Ln, bias=1.0).then_inc(act_prep, 1)
            for a in range(2):
                act.wait_ge(pe_prep, 3 + a)
                act.activation(kvT_c[:, a, :, :].rearrange("p g t -> p (g t)"), psum[:, 4 + 2 * a:6 + 2 * a, :].rearrange("p b n -> p (b n)"), ACT.Copy).then_inc(act_prep, 1)
            for a in range(2):
                act.wait_ge(w1_used, 4 * a + 4)
                act.activation(hid_c[:, a, :], psum[:, 4 + a, 0:NSA_G * NCMP], ACT.Gelu_apprx_tanh).then_inc(act_prep, 1)
            act.wait_ge(pe_prep, 5)
            act.activation(kcT[:, :], psum[:, 6, 0:NSA_G * NCMP], ACT.Copy).then_inc(act_prep, 1)
            act.activation(vc[:, :, :].rearrange("n g d -> n (g d)"), psum[0:NCMP, 7, :], ACT.Copy).then_inc(act_prep, 1)

            def gla_slot(h, k):
                if k == 0:
                    act.wait_ge(g_qkt, h + 1)
                    act.activation(qT_g[:, :], psum[:, 4, 0:S], ACT.Copy, scale=GLA_DK ** -0.5).then_inc(g_qe, 1)
                    act.wait_ge(g_dec, h + 1)
                    act.activation(dec[:, 0:LDIAG, :], dec[:, 0:LDIAG, :], ACT.Exp, scale=-1.0 / GLA_TAU).then_inc(g_exp, 1)
                    act.wait_ge(g_in, h * 64 + 64)
                    act.activation(sig_g[:, :, :], r_g[:, :, :], ACT.Exp, scale=-1.0).then_inc(g_sig, 1)
                if k == 3:
                    act.wait_ge(g_o, h + 1)
                    for t in range(NT):
                        step(act.activation(y_g[:, t, :], psum[:, 7, t * GLA_DV:(t + 1) * GLA_DV], ACT.Square, accum_out=gst[:, t:t + 1]))
                    step(act.activation(gst[:, 2:4], gst[:, 0:2], ACT.Ln, scale=1.0 / GLA_DV, bias=eps_ap))
                    act.activation(gst[:, 4:6], gst[:, 2:4], ACT.Exp, scale=-0.5).then_inc(g_rn, 1)
                    act.wait_ge(g_yt, h + 1)
                    act.activation(ygT_hi[:, ds(h * 2, 2), :].rearrange("p c t -> p (c t)"), psum[:, 4, :], ACT.Copy).then_inc(g_yhi, 1)

            eps_ap = stat[:, 12:13]
            act.wait_ge(g_msk, 32)
            base = A_BLOCKS * UPB
            with act.Fori(0, GLA_H // 2) as i:
                step.enter(i, 0, 2 * 3)
                for hp in range(2):
                    for k in range(UPB):
                        hi(i * 8 + (base + hp * 4 + k + 1), k + 1)
                        gla_slot(i * 2 + hp, k)
                    evacuate(i * 2 + (A_BLOCKS + hp), hp)
                step.leave(GLA_H // 2)

            base = (A_BLOCKS + 4) * UPB
            with act.Fori(0, NSA_G) as g:
                for k in range(8):
                    hi(g * 8 + (base + k + 1), k + 1)
                    if k == 0:
                        act.wait_ge(pv_done, g * NSA_HPG)
                        act.activation(vc_n[:, :], vc[:, ds(g, 1), :].rearrange("n a d -> n (a d)"), ACT.Copy).then_inc(vcn_done, 1)
                    if k == 1:
                        act.wait_ge(qkt_done, g + 1)
                        for b in range(2):
                            act.activation(qkT[:, 2 * b:2 * b + 2, :].rearrange("p h t -> p (h t)"), psum[:, 4 + b, :], ACT.Copy).then_inc(qkt_a, 1)
                    j = k - 4
                    if 0 <= j < NSA_HPG:
                        act.wait_ge(pv_done, g * NSA_HPG + j + 1)
                        act.activation(ynT_hi[:, ds(g * NSA_HPG + j, 1), :].rearrange("p a t -> p (a t)"), psum[:, 6, S:2 * S], ACT.Copy).then_inc(o_hi, 1)
                    j = k - 3
                    if 0 <= j < NSA_HPG:
                        act.wait_ge(pt_done, g * NSA_HPG + j + 1)
                        act.activation(pT[:, 0:2, 0:P], psum[:, 6, 0:S].rearrange("p (a t) -> p a t", a=2), ACT.Copy).then_inc(pt_a, 1)
                        act.activation(pcT[:, :], psum[0:NCMP, 6, S:2 * S], ACT.Copy).then_inc(pt_a, 1)
                    j = k - 2
                    if 0 <= j < NSA_HPG:
                        q = j % 2
                        act.wait_ge(mx_done, g * NSA_HPG + j + 1)
                        for t in range(NT):
                            for b in (2, 0, 1):
                                w = (b + 1) % 3
                                src = smc[:, q, t, :] if b == 2 else sm[:, q, 2 * P * t + b * (t + 1) * P:2 * P * t + (b + 1) * (t + 1) * P]
                                act.activation(src, src, ACT.Exp, scale=SCALE, bias=nmx[:, q, t, w:w + 1],
                                               accum_out=sums[:, q, t, w:w + 1]).then_inc(exp_done, 1)
                    if k % 4 == 3:
                        evacuate(g * 2 + (A_BLOCKS + 4 + k // 4), k // 4)

            base = PROJ_BLOCKS * UPB
            act.wait_ge(stored[0], 16 * PROJ_BLOCKS // 2)
            act.wait_ge(stored[1], 16 * PROJ_BLOCKS // 2)
            with act.Fori(0, 2) as i:
                for nbp in range(2):
                    nb = i * 2 + nbp
                    for k in range(6):
                        hi(i * 12 + (base + nbp * 6 + k + 1), nbp * 6 + k + 1)
                        if k == 0:
                            act.wait_ge(gab_in, nb * 32 + 32)
                            act.activation(gab[:, :, :, :], gab[:, :, :, :], ACT.Sigmoid).then_inc(gab_sig, 1)
                    act.wait_ge(mt_done, nb + 1)
                    act.activation(mT_hi[:, ds(nb * 4, 4), :].rearrange("p c t -> p (c t)"), psum[:, 4:6, :].rearrange("p b n -> p (b n)"), ACT.Copy).then_inc(m_hi, 1)

            base = PROJ_BLOCKS * UPB + 4 * (UPG + UPB)
            with act.Fori(0, 2) as i:
                for par in range(2):
                    b = i * 2 + par
                    for k in range(UPB):
                        hi(i * 8 + (base + par * 4 + k + 1), k + 1)
                    act.wait_ge(x1_done, b + 1)
                    for t in range(NT):
                        act.activation(gab[:, t, 0, :], x_nat[:, t, ds(b * NB, NB)], ACT.Square, accum_out=sq_x1[:, t, ds(b, 1)]).then_inc(sq2, 1)
                        act.wait_ge(sq2, b * 2 + t + 1)
                    act.wait_ge(xt_done, b + 1)
                    act.activation(h2T_hi[:, ds(b * 4, 4), :].rearrange("p c t -> p (c t)"), psum[:, 4:6, :].rearrange("p b n -> p (b n)"), ACT.Copy).then_inc(x_hi, 1)

            base = PROJ_BLOCKS * UPB + 4 * (UPG + UPB) + 4 * UPB
            act.wait_ge(ms2_done, 1)
            act.activation(stat[:, 10:12], stat[:, 8:10], ACT.Sqrt).then_inc(sq2_done, 1)
            for par in range(2):
                for k in range(UPB):
                    n = base + par * 4 + k + 1
                    if n < UNITS:
                        hi(n, n % 4)
            act.wait_ge(rs2_done, 1)
            for par in range(2):
                act.wait_ge(unit_done, base + par * UPB + UPB)
                for t in range(NT):
                    act.activation(qp[:, t, par * NB:(par + 1) * NB], psum[:, 2 * par + t, :], ACT.Copy, scale=rstd2[:, t:t + 1]).then_inc(qp_done, 1)
            act.wait_ge(qpt_done, 1)
            act.activation(qpT[:, :, :].rearrange("p h t -> p (h t)"), psum[:, 4:8, :].rearrange("p b n -> p (b n)"), ACT.Copy).then_inc(qpt_out, 1)
            for t in range(NT):
                act.wait_ge(sc_done, t + 1)
                act.activation(sc[:, t * PEER_H:(t + 1) * PEER_H, :].rearrange("p h n -> p (h n)"), psum[:, 4 * t:4 * t + 4, :].rearrange("p b n -> p (b n)"), ACT.Copy).then_inc(sc_out, 1)

            def route_exp(u):
                act.wait_ge(r_vals, u + 1)
                act.activation(rexp[:, :], vals[:, :], ACT.Exp, bias=rst[:, 0:1], accum_out=rst[:, 1:2]).then_inc(r_exp, 1)

            def picks(u, par, route):
                for k in range(TOPK):
                    act.wait_ge(dot_done, u * TOPK + k + 1)
                    act.activation(act_h[:, par, k:k + 1], hid[:, par, k:k + 1], ACT.Gelu_apprx_tanh).then_inc(act_done, 1)
                    if k == 2 and route:
                        route_exp(u + 1)

            def norm_out(t):
                act.wait_ge(x2_done, t + 1)
                act.activation(ring_free(t), x_nat[:, t, :], ACT.Square, accum_out=stat[:, t:t + 1]).then_inc(fsq, 1)
                act.wait_ge(fms, t + 1)
                act.activation(stat[:, 4 + t:5 + t], stat[:, 2 + t:3 + t], ACT.Sqrt).then_inc(frs, 1)

            def ring_free(t):
                return sc[:, 0:PEER_H, :].rearrange("p h n -> p (h n)")

            route_exp(0)
            with act.Fori(0, PEER_H // 2) as i:
                picks(i * 2, 0, True)
                picks(i * 2 + 1, 1, True)
            norm_out(0)
            with act.Fori(PEER_H // 2, PEER_H - 1) as i:
                picks(i * 2, 0, True)
                picks(i * 2 + 1, 1, True)
            picks(UNITS_P - 2, 0, True)
            picks(UNITS_P - 1, 1, False)
            norm_out(1)

        @block.tensor
        def _(pe):
            def unit(n, k4, par, xh, xl, kc0, first, last, free, half=None):
                s = k4 % SPLIT
                if half in (None, 0):
                    pe.wait_ge(hi_done, n + 1)
                    pe.wait_ge(lo_done, n + 1)
                    if first and free is not None:
                        pe.wait_ge(*free)
                cs = range(CU) if half is None else range(half * 2, half * 2 + 2)
                for c in cs:
                    rh, rl = w_hi[:, s, c * NB:(c + 1) * NB], w_lo[:, s, c * NB:(c + 1) * NB]
                    for t in range(NT):
                        ts = slice(t * P, (t + 1) * P)
                        out = psum[:, 2 * par + t, :]
                        st, en = first and c == 0, last and c == CU - 1
                        pe.matmul(out, xh[:, kc0 + c, ts], rh, start=st, stop=False, skip_group_check=True)
                        pe.matmul(out, xh[:, kc0 + c, ts], rl, start=False, stop=False, skip_group_check=True)
                        ins = pe.matmul(out, xl[:, kc0 + c, ts], rh, start=False, stop=en, skip_group_check=True)
                if half in (None, 1):
                    ins.then_inc(unit_done, 1)

            def proj_unit(n, k, par, b, half=None):
                free = None if isinstance(b, int) and b < 2 else (evac_done, b * 2 - 2)
                unit(n, k, par, hT_hi, hT_lo, 4 * k, k == 0, k == UPB - 1, free, half)

            pe.wait_ge(small_in, 16)
            pe.wait_ge(xg_done, 4)
            for t in range(NT):
                for c in range(KC):
                    ins = pe.matmul(psum[:, 4, t * 64:(t + 1) * 64], xgT[:, c, t * P:(t + 1) * P], w_small[:, c, :],
                                    start=c == 0, stop=c == KC - 1, skip_group_check=True)
            ins.then_inc(small_done, 1)
            pe.wait_ge(h_hi, 4)
            pe.wait_ge(h_lo, 4)
            for b in range(2):
                for k in range(UPB):
                    proj_unit(b * UPB + k, k, b, b)
            with pe.Fori(1, A_BLOCKS // 2) as i:
                for par in range(2):
                    for k in range(UPB):
                        proj_unit(i * 8 + (par * 4 + k), k, par, i * 2 + par)

            pe.wait_ge(small_out, 4)
            pe.wait_ge(const_in, 96)
            for t in range(NT):
                ins = pe.transpose(psum[0:GLA_LR, 4, t * P:(t + 1) * P], glr[:, t, :], ident[:, :])
            ins.then_inc(pe_prep, 1)
            pe.wait_ge(act_prep, 1)
            pe.wait_ge(prep_in, 64)
            for h in range(GLA_H):
                ins = pe.matmul(psum[:, 4 + h // 2, (h % 2) * S:(h % 2 + 1) * S], w_decay[:, h * GLA_DK:(h + 1) * GLA_DK], glrT[:, :],
                                start=True, stop=True, skip_group_check=True)
            ins.then_inc(pe_prep, 1)
            for a in range(2):
                if a == 0:
                    pe.wait_ge(dve_prep, 10)
                for g in range(NSA_G):
                    for t in range(NT):
                        ins = pe.transpose(psum[:, 4 + 2 * a + g // 2, (g % 2) * S + t * P:(g % 2) * S + (t + 1) * P],
                                           kv_c[:, a, t, g * DH:(g + 1) * DH], ident[:, :])
                ins.then_inc(pe_prep, 1)
            for a in range(2):
                pe.wait_ge(dve_prep, 11)
                for q in range(4):
                    pe.wait_ge(w1_in[q % 2], 16 * (a * 2 + q // 2 + 1))
                    for i in range(CMP_BLOCK // 4):
                        c = q * (CMP_BLOCK // 4) + i
                        ins = pe.matmul(psum[:, 4 + a, 0:NSA_G * NCMP], w1[:, q % 2, i, :], blk_c[:, a, c, :, :].rearrange("p g n -> p (g n)"),
                                        start=c == 0, stop=c == CMP_BLOCK - 1, skip_group_check=True)
                    ins.then_inc(w1_used, 1)
            pe.wait_ge(act_prep, 6)
            pe.matmul(psum[:, 6, 0:NSA_G * NCMP], w2[:, 0, :], hid_c[:, 0, :], start=True, stop=True, skip_group_check=True)
            for g in range(NSA_G):
                ins = pe.matmul(psum[0:NCMP, 7, g * DH:(g + 1) * DH], hid_c[:, 1, g * NCMP:(g + 1) * NCMP], w2[:, 1, :],
                                start=True, stop=True, skip_group_check=True)
            ins.then_inc(pe_prep, 1)

            def gla_part(h, k, half):
                if (k, half) == (0, 0):
                    pe.wait_ge(g_in, h * 64 + 64)
                    pe.wait_ge(g_yhi, h)
                    pe.wait_ge(g_ylo, h)
                    for a in range(2):
                        for t in range(NT):
                            ins = pe.transpose(psum[:, 4, a * S + t * P:a * S + (t + 1) * P], qk_g[:, a, t, :], ident[:, :])
                    ins.then_inc(g_qkt, 1)
                if (k, half) in ((2, 0), (2, 1)):
                    t = half
                    if t == 0:
                        pe.wait_ge(g_ql, h + 1)
                        pe.wait_ge(g_kl, h + 1)
                        pe.wait_ge(g_att, h * 2)
                    else:
                        pe.wait_ge(g_att, h * 2 + 1)
                    ts = slice(t * P, (t + 1) * P)
                    for n, lev in enumerate([*range(len(LEVELS)), LDIAG]):
                        ins = pe.matmul(psum[:, 5 + n // 4, (n % 4) * P:(n % 4 + 1) * P], kL[:, lev, ts], qL[:, lev, ts],
                                        start=True, stop=True, skip_group_check=True)
                    if t == 0:
                        ins = pe.matmul(psum[:, 4, 0:P], kL[:, L128, 0:P], qL[:, L128, P:S], start=True, stop=True, skip_group_check=True)
                    ins.then_inc(g_lev, 1)
                if (k, half) == (3, 0):
                    pe.wait_ge(g_att, h * 2 + 2)
                    pe.wait_ge(g_a01, h + 1)
                    pe.matmul(psum[:, 7, 0:GLA_DV], att_T[:, 0, :], v_g[:, 0, :], start=True, stop=True, skip_group_check=True)
                    pe.matmul(psum[:, 7, GLA_DV:2 * GLA_DV], att_T[:, 2, :], v_g[:, 0, :], start=True, stop=False, skip_group_check=True)
                    pe.matmul(psum[:, 7, GLA_DV:2 * GLA_DV], att_T[:, 1, :], v_g[:, 1, :], start=False, stop=True,
                              skip_group_check=True).then_inc(g_o, 1)
                if (k, half) == (3, 1):
                    pe.wait_ge(g_y, h + 1)
                    for c in range(2):
                        for t in range(NT):
                            ins = pe.transpose(psum[:, 4, c * S + t * P:c * S + (t + 1) * P], y_g[:, t, c * P:(c + 1) * P], ident[:, :])
                    ins.then_inc(g_yt, 1)

            pe.wait_ge(act_prep, 8)
            base = A_BLOCKS * UPB
            with pe.Fori(0, GLA_H // 2) as i:
                for hp in range(2):
                    for k in range(UPB):
                        for half in range(2):
                            proj_unit(i * 8 + (base + hp * 4 + k), k, hp, i * 2 + (A_BLOCKS + hp), half)
                            gla_part(i * 2 + hp, k, half)

            def scores(g, j):
                h = g * NSA_HPG + j
                pe.wait_ge(mx_done, h)
                if j == 0:
                    pe.wait_ge(qkt_a, g * 2 + 2)
                    pe.wait_ge(qkt_v, g + 1)
                for t in range(NT):
                    q = qkT[:, j, t * P:(t + 1) * P]
                    n = (t + 1) * P
                    for b in range(2):
                        pe.matmul(psum[:, 4 + t, b * n:(b + 1) * n], q, qkT[:, NSA_HPG + b, 0:n], start=True, stop=True, skip_group_check=True)
                    ins = pe.matmul(psum[:, 4, S + t * 16:S + t * 16 + NCMP], q, kcT[:, ds(g * NCMP, NCMP)], start=True, stop=True, skip_group_check=True)
                ins.then_inc(s_done, 1)

            def turn(g, j):
                h = g * NSA_HPG + j
                q = j % 2
                pe.wait_ge(p_done, h + 1)
                pe.wait_ge(o_hi, h)
                pe.wait_ge(o_lo, h)
                pe.wait_ge(pt_a, h * 2)
                pe.wait_ge(pt_v, h)
                for b in range(2):
                    pe.transpose(psum[:, 6, b * P:(b + 1) * P], sm[:, q, b * P:(b + 1) * P], ident[:, :])
                for t in range(NT):
                    pe.transpose(psum[0:NCMP, 6, S + t * P:S + (t + 1) * P], smc[:, q, t, :], ident[:, :])
                for b in range(2):
                    for kt in range(2):
                        o = (kt * 2 + b) * P
                        ins = pe.transpose(psum[:, 7, o:o + P], sm[:, q, 2 * P + b * S + kt * P:2 * P + b * S + (kt + 1) * P], ident[:, :])
                ins.then_inc(pt_done, 1)

            def values(g, j):
                h = g * NSA_HPG + j
                pe.wait_ge(pt_a, h * 2 + 2)
                pe.wait_ge(pt_v, h + 1)
                if j == 0:
                    pe.wait_ge(nv_in, g * 32 + 32)
                    pe.wait_ge(vcn_done, g + 1)
                out = psum[:, 6, S:2 * S]
                pe.matmul(out, v_n[:, 0, 0, :], pT[:, 0, :], start=True, stop=False, skip_group_check=True)
                pe.matmul(out, v_n[:, 1, 0, :], pT[:, 1, :], start=False, stop=False, skip_group_check=True)
                pe.matmul(out, vc_n[:, :], pcT[:, :], start=False, stop=False, skip_group_check=True)
                out = psum[:, 6, S + P:2 * S]
                pe.matmul(out, v_n[:, 0, 1, :], pT[:, 2, P:S], start=False, stop=False, skip_group_check=True)
                pe.matmul(out, v_n[:, 1, 1, :], pT[:, 3, P:S], start=False, stop=True, skip_group_check=True).then_inc(pv_done, 1)

            pe.wait_ge(g_yhi, GLA_H)
            pe.wait_ge(g_ylo, GLA_H)
            base = (A_BLOCKS + 4) * UPB
            with pe.Fori(0, NSA_G) as g:
                for k in range(8):
                    proj_unit(g * 8 + (base + k), k % 4, k // 4, g * 2 + (A_BLOCKS + 4 + k // 4))
                    if k == 1:
                        pe.wait_ge(roped, g + 1)
                        pe.wait_ge(mx_done, g * NSA_HPG)
                        pe.wait_ge(o_hi, g * NSA_HPG)
                        pe.wait_ge(o_lo, g * NSA_HPG)
                        for a in range(NSA_HPG + 2):
                            for t in range(NT):
                                ins = pe.transpose(psum[:, 4 + a // 2, (a % 2) * S + t * P:(a % 2) * S + (t + 1) * P], qk_n[:, t, a, :], ident[:, :])
                        ins.then_inc(qkt_done, 1)
                    if 0 <= k - 4 < NSA_HPG:
                        values(g, k - 4)
                    if 0 <= k - 2 < NSA_HPG:
                        scores(g, k - 2)
                    if 0 <= k - 3 < NSA_HPG:
                        turn(g, k - 3)

            base = PROJ_BLOCKS * UPB
            pe.wait_ge(o_hi, NSA_H)
            pe.wait_ge(o_lo, NSA_H)
            pe.wait_ge(evac_done, 2 * PROJ_BLOCKS)
            with pe.Fori(0, 2) as i:
                for nbp in range(2):
                    nb = i * 2 + nbp
                    for k in range(UPG):
                        unit(i * 12 + (base + nbp * 6 + k), nbp * 6 + k, 0, ygT_hi, ygT_lo, 4 * k, k == 0, k == UPG - 1, (m_done, nb * 2))
                    for k in range(UPB):
                        unit(i * 12 + (base + nbp * 6 + UPG + k), nbp * 6 + UPG + k, 1, ynT_hi, ynT_lo, 4 * k, k == 0, k == UPB - 1, (m_done, nb * 2))
                    pe.wait_ge(m_done, nb * 2 + 2)
                    pe.wait_ge(m_hi, nb)
                    pe.wait_ge(m_lo, nb)
                    for c in range(4):
                        for t in range(NT):
                            ins = pe.transpose(psum[:, 4 + c // 2, (c % 2) * S + t * P:(c % 2) * S + (t + 1) * P], mrg[:, 1, t, c * P:(c + 1) * P], ident[:, :])
                    ins.then_inc(mt_done, 1)

            base = PROJ_BLOCKS * UPB + 4 * (UPG + UPB)
            pe.wait_ge(m_hi, 4)
            pe.wait_ge(m_lo, 4)
            with pe.Fori(0, 2) as i:
                for par in range(2):
                    b = i * 2 + par
                    for k in range(UPB):
                        unit(i * 8 + (base + par * 4 + k), k, par, mT_hi, mT_lo, 4 * k, k == 0, k == UPB - 1, (x1_done, b))
                    pe.wait_ge(xg2_done, b + 1)
                    pe.wait_ge(x_hi, b)
                    pe.wait_ge(x_lo, b)
                    for c in range(4):
                        for t in range(NT):
                            ins = pe.transpose(psum[:, 4 + c // 2, (c % 2) * S + t * P:(c % 2) * S + (t + 1) * P], mrg[:, 1, t, c * P:(c + 1) * P], ident[:, :])
                    ins.then_inc(xt_done, 1)

            base = PROJ_BLOCKS * UPB + 4 * (UPG + UPB) + 4 * UPB
            pe.wait_ge(x_hi, 4)
            pe.wait_ge(x_lo, 4)
            for par in range(2):
                for k in range(UPB):
                    unit(base + par * 4 + k, k, par, h2T_hi, h2T_lo, 4 * k, k == 0, k == UPB - 1, (x1_done, 4))
            pe.wait_ge(qp_done, 4)
            for h in range(PEER_H):
                for t in range(NT):
                    ins = pe.transpose(psum[:, 4 + h // 2, (h % 2) * S + t * P:(h % 2) * S + (t + 1) * P], qp[:, t, h * PEER_DK:(h + 1) * PEER_DK], ident[:, :])
            ins.then_inc(qpt_done, 1)
            pe.wait_ge(qpt_out, 1)
            pe.wait_ge(keys_in, 16)
            for t in range(NT):
                for h in range(PEER_H):
                    ins = pe.matmul(psum[:, 4 * t + h // 2, (h % 2) * S:(h % 2 + 1) * S], qpT[:, h, t * P:(t + 1) * P], keys[:, h, :],
                                    start=True, stop=True, skip_group_check=True)
                ins.then_inc(sc_done, 1)

            pe.wait_ge(zero_done, 1)
            for t in range(NT):
                pe.wait_ge(sc_out, t + 1)
                for q in range(4):
                    pe.matmul(psum[:, 4 * t + q, :], zeros[:, :], zeros[:, None, :].to_broadcast([P, 4, P]), start=True, stop=False, skip_group_check=True)
            for t in range(NT):
                with pe.Fori(t * PEER_H // 2, (t + 1) * PEER_H // 2) as i:
                    for par in range(2):
                        for k in range(TOPK):
                            pe.wait_ge(diag_done, (i * 2 + par) * TOPK + k + 1)
                            slot = (par * TOPK + k) % RING
                            for q in range(4):
                                ins = pe.matmul(psum[:, 4 * t + q, :], diag[:, k % 4, :], ring[:, slot, D + q * NB:D + (q + 1) * NB],
                                                start=False, stop=False, skip_group_check=True)
                            ins.then_inc(acc_done, 1)


        @block.vector
        def _(dve):
            step = Steps(dve, v_step)

            def lo(n, s):
                dve.wait_ge(hi_done, n + 1)
                wait = n - (SPLIT - 1)
                if not (isinstance(wait, int) and wait <= 0):
                    dve.wait_ge(unit_done, wait)
                dve.tensor_tensor(w_lo[:, s % SPLIT, :], w_raw[:, s % RAW, :], w_hi[:, s % SPLIT, :].bitcast(F32), ALU.subtract).then_inc(lo_done, 1)

            def lower(dst, src, up, n, s, value):
                dve.wait_ge(s, value)
                return dve.tensor_tensor(dst, src, up.bitcast(F32), ALU.subtract)

            def rope(x, rot, n):
                cs = cos_t[:, :, None, :].to_broadcast([P, NT, n, HALF])
                sn = sin_t[:, :, None, :].to_broadcast([P, NT, n, HALF])
                x1, x2 = x[:, :, 0:n, 0:HALF], x[:, :, 0:n, HALF:ROT]
                dve.tensor_tensor(rot[:, 0], x1, cs, ALU.mult)
                dve.tensor_tensor(rot[:, 1], x2, sn, ALU.mult)
                dve.tensor_tensor(rot[:, 2], x2, cs, ALU.mult)
                step(dve.tensor_tensor(rot[:, 3], x1, sn, ALU.mult))
                dve.tensor_tensor(x1, rot[:, 0], rot[:, 1], ALU.subtract)
                return dve.tensor_tensor(x2, rot[:, 2], rot[:, 3], ALU.add)

            def refine(r, v, n=NT):
                t = newton[:, 0:n]
                step(dve.tensor_tensor(t, r, r, ALU.mult))
                step(dve.tensor_tensor(t, t, v, ALU.mult))
                step(dve.tensor_scalar(t, t, -0.5, 1.5, ALU.mult, ALU.add))
                return dve.tensor_tensor(r, r, t, ALU.mult)

            dve.memset(stat[:, 12:13], EPS)
            dve.wait_ge(xT_in, 64)
            dve.wait_ge(const_in, 96)
            for q in range(4):
                c = slice(4 * q, 4 * q + 4)
                dve.tensor_tensor(xgT[:, c, :], xgT[:, c, :], g1[:, c, None].to_broadcast([P, 4, S]), ALU.mult).then_inc(xg_done, 1)
            for q in range(4):
                c = slice(4 * q, 4 * q + 4)
                dve.wait_ge(h_hi, q + 1)
                dve.tensor_tensor(hT_lo[:, c, :], xgT[:, c, :], hT_hi[:, c, :].bitcast(F32), ALU.subtract).then_inc(h_lo, 1)
            lo(0, 0)
            dve.wait_ge(ssq1, 2)
            dve.tensor_scalar(stat[:, 2:4], stat[:, 0:2], 1.0 / D, EPS, ALU.mult, ALU.add).then_inc(ms1_done, 1)
            step(dve.tensor_copy(pos_f[:, :], pos_i[:, :]))
            for t in range(NT):
                ins = dve.tensor_scalar(ang[:, t, :], inv_f[:, :], pos_f[:, t:t + 1], None, ALU.mult)
            step(ins)
            step(dve.tensor_scalar(turns[:, :, :], ang[:, :, :], float(1 / (2 * np.pi)), None, ALU.mult))
            step(dve.tensor_scalar(turns[:, :, :], turns[:, :, :], ROUND, None, ALU.add))
            step(dve.tensor_scalar(turns[:, :, :], turns[:, :, :], ROUND, None, ALU.subtract))
            for part in TWO_PI:
                step(dve.scalar_tensor_tensor(ang[:, :, :], turns[:, :, :], -part, ang[:, :, :], ALU.mult, ALU.add))
            dve.tensor_scalar(ang[:, :, :], ang[:, :, :], 3.1415925, -3.1415925, ALU.min, ALU.max).then_inc(ang_ready, 1)
            dve.wait_ge(sq1_done, 1)
            step(dve.reciprocal(rstd1[:, :], stat[:, 4:6]))
            refine(rstd1[:, :], stat[:, 2:4]).then_inc(rs1_done, 1)
            dve.wait_ge(trig_done, 2)
            step(dve.tensor_tensor(cos_t[:, :, :], turns[:, :, :], turns[:, :, :], ALU.mult))
            step(dve.tensor_scalar(cos_t[:, :, :], cos_t[:, :, :], -2.0, 1.0, ALU.mult, ALU.add))
            lo(1, 1)

            for n in range(1, 2 * UPB):
                lo(n + 1, (n + 1) % 4)
            with dve.Fori(1, A_BLOCKS // 2) as i:
                for k in range(2 * UPB):
                    lo(i * 8 + (k + 1), k + 1)

            dve.wait_ge(pe_prep, 2)
            dve.wait_ge(prep_in, 64)
            for h in range(GLA_H):
                dve.tensor_scalar(zT[:, h * S:(h + 1) * S], psum[:, 4 + h // 2, (h % 2) * S:(h % 2 + 1) * S], b_decay[:, h:h + 1], None,
                                  ALU.add).then_inc(dve_prep, 1)
            dve.wait_ge(act_prep, 2)
            dve.scalar_tensor_tensor(zT, zT, 0.0, zA, ALU.min, ALU.subtract).then_inc(dve_prep, 1)
            dve.wait_ge(dve_prep, 5)
            for h in range(GLA_H):
                dve.tensor_tensor_scan(bT[:, h, :], zT[:, h * S:(h + 1) * S], zT[:, h * S:(h + 1) * S], 0.0, ALU.add, ALU.bypass).then_inc(dve_prep, 1)
            dve.wait_ge(kvc_in, 32)
            rope(kv_c[:, 0, :, :].rearrange("p t (g d) -> p t g d", d=DH), rot_c, NSA_G).then_inc(dve_prep, 1)
            dve.wait_ge(act_prep, 4)
            for a in range(2):
                for half in range(CMP_BLOCK // CMP_STRIDE):
                    o = half * CMP_STRIDE
                    ins = dve.tensor_tensor(blk_c[:, a, o:o + CMP_STRIDE, :, :],
                                            kvT_c[:, a, :, o:o + NCMP * CMP_STRIDE].rearrange("p g (n b) -> p b g n", b=CMP_STRIDE),
                                            posT[:, a, o:o + CMP_STRIDE, None, None].to_broadcast([P, CMP_STRIDE, NSA_G, NCMP]), ALU.add)
            ins.then_inc(dve_prep, 1)

            def gla_slot(h, k):
                if k == 0:
                    if not isinstance(h, int):
                        dve.wait_ge(g_kl, h)
                    for n, m in enumerate([*LEVELS, P]):
                        b = bT[:, ds(h, 1), :].rearrange("p a (n m) -> p (a n) m", m=2 * m)
                        ins = dve.tensor_tensor(dec[:, n, :].rearrange("p (n m) -> p n m", m=2 * m), b,
                                                b[:, :, m - 1:m].to_broadcast([P, S // (2 * m), 2 * m]), ALU.subtract)
                    step(ins)
                    dve.scalar_tensor_tensor(dec[:, 0:LDIAG, :], dec[:, 0:LDIAG, :], -1.0, dec[:, 0:LDIAG, :], ALU.mult, ALU.max).then_inc(g_dec, 1)
                    dve.wait_ge(g_qe, h + 1)
                    dve.tensor_copy(kT_g[:, :], psum[:, 4, S:2 * S]).then_inc(g_ke, 1)
                if k == 1:
                    dve.wait_ge(g_exp, h + 1)
                    dve.wait_ge(g_qe, h + 1)
                    dve.tensor_tensor(qL[:, :, :], dec[:, :, :], qT_g[:, None, :].to_broadcast([P, NL, S]), ALU.mult).then_inc(g_ql, 1)
                    dve.wait_ge(g_sig, h + 1)
                    step(dve.tensor_scalar(sig_g[:, :, :], sig_g[:, :, :], 1.0, None, ALU.add))
                    step(dve.reciprocal(sig_g[:, :, :], sig_g[:, :, :]))
                    step(dve.tensor_tensor(sig_g[:, :, :], sig_g[:, :, :], r_g[:, :, :], ALU.mult))
                if k == 2:
                    for t in range(NT):
                        dve.wait_ge(g_lev, h * 2 + (t + 1))
                        step(dve.tensor_tensor(att_m[:, :, :], psum[:, 5:7, :].rearrange("p b (l t) -> p (b l) t", t=P), masks[:, :, :], ALU.mult))
                        dve.tensor_reduce(att_T[:, t, :], att_m[:, :, :].rearrange("p l t -> p t l"), AX.X, ALU.add).then_inc(g_att, 1)
                        dve.wait_ge(g_att, h * 2 + (t + 1))
                        if t == 0:
                            dve.tensor_copy(att_T[:, 2, :], psum[:, 4, 0:P]).then_inc(g_a01, 1)
                if k == 3:
                    dve.wait_ge(g_rn, h + 1)
                    step(dve.tensor_scalar(gst[:, 6:8], gst[:, 0:2], 1.0 / GLA_DV, EPS, ALU.mult, ALU.add))
                    step(refine(gst[:, 4:6], gst[:, 6:8]))
                    for t in range(NT):
                        ins = dve.scalar_tensor_tensor(y_g[:, t, :], psum[:, 7, t * GLA_DV:(t + 1) * GLA_DV], gst[:, 4 + t:5 + t], gnorm[:, :], ALU.mult, ALU.mult)
                    step(ins)
                    dve.tensor_tensor(y_g[:, :, :], y_g[:, :, :], sig_g[:, :, :], ALU.mult).then_inc(g_y, 1)
                    up = ygT_hi[:, ds(h * 2, 2), :].rearrange("p c t -> p (c t)")
                    dve.wait_ge(g_yhi, h + 1)
                    dve.tensor_tensor(ygT_lo[:, ds(h * 2, 2), :].rearrange("p c t -> p (c t)"), psum[:, 4, :], up.bitcast(F32), ALU.subtract).then_inc(g_ylo, 1)

            dve.wait_ge(g_msk, 32)
            step(dve.memset(dec[:, LDIAG, :], 1.0))
            base = A_BLOCKS * UPB
            with dve.Fori(0, GLA_H // 2) as i:
                step.enter(i, 0, 2 * 12)
                for hp in range(2):
                    for k in range(UPB):
                        lo(i * 8 + (base + hp * 4 + k + 1), k + 1)
                        gla_slot(i * 2 + hp, k)
                step.leave(GLA_H // 2)

            def scores_max(h, j):
                q = j % 2
                wait_alone(dve, s_done, h + 1)
                for t in range(NT):
                    n = (t + 1) * P
                    for b in range(2):
                        o = 2 * P * t + b * n
                        dve.tensor_tensor_reduce(sm[:, q, o:o + n], psum[:, 4 + t, b * n:(b + 1) * n], tri[:, S - n:S], 1.0, -3e38,
                                                 ALU.add, ALU.max, mx[:, q, t, b + 1:b + 2])
                    ins = dve.tensor_tensor_reduce(smc[:, q, t, :], psum[:, 4, S + 16 * t:S + 16 * t + NCMP], cmask[:, t, :], 1.0, -3e38,
                                                   ALU.add, ALU.max, mx[:, q, t, 0:1])
                step(ins)
                dve.tensor_scalar(nmx[:, q, :, :], mx[:, q, :, :], MASKED_MAX, -SCALE, ALU.max, ALU.mult).then_inc(mx_done, 1)

            def probs(h, j):
                q = j % 2
                dve.wait_ge(exp_done, h * 6 + 6)
                step(dve.tensor_scalar(wts[:, q, :, :], sums[:, q, :, :], 1e-30, None, ALU.max))
                step(dve.reciprocal(wts[:, q, :, :], wts[:, q, :, :]))
                step(dve.tensor_tensor(wts[:, q, :, :], wts[:, q, :, :], g_n[:, :, 3 * j:3 * j + 3], ALU.mult))
                for t in range(NT):
                    for b in range(3):
                        n = (t + 1) * P
                        o = 2 * P * t + b * n
                        w = (b + 1) % 3
                        x = smc[:, q, t, :] if b == 2 else sm[:, q, o:o + n]
                        ins = dve.tensor_scalar(x, x, wts[:, q, t, w:w + 1], None, ALU.mult)
                ins.then_inc(p_done, 1)

            base = (A_BLOCKS + 4) * UPB
            with dve.Fori(0, NSA_G) as g:
                step.enter(g, 0, 2 + 4 * 4)
                for k in range(8):
                    lo(g * 8 + (base + k + 1), k + 1)
                    if k == 0:
                        step(dve.tensor_copy(g_n[:, :, :], gates[:, :, ds(g * 3 * NSA_HPG, 3 * NSA_HPG)]))
                        dve.wait_ge(nqk_in, g * 48 + 48)
                        rope(qk_n, rot_n, NSA_HPG + 2).then_inc(roped, 1)
                    if k == 1:
                        dve.wait_ge(qkt_done, g + 1)
                        dve.tensor_copy(qkT[:, 4:6, :].rearrange("p h t -> p (h t)"), psum[:, 6, :]).then_inc(qkt_v, 1)
                    if 0 <= k - 4 < NSA_HPG:
                        h = g * NSA_HPG + (k - 4)
                        up = ynT_hi[:, ds(h, 1), :].rearrange("p a t -> p (a t)")
                        dve.wait_ge(o_hi, h + 1)
                        dve.tensor_tensor(ynT_lo[:, ds(h, 1), :].rearrange("p a t -> p (a t)"), psum[:, 6, S:2 * S], up.bitcast(F32), ALU.subtract).then_inc(o_lo, 1)
                    if 0 <= k - 3 < NSA_HPG:
                        probs(g * NSA_HPG + (k - 3), k - 3)
                    if 0 <= k - 2 < NSA_HPG:
                        scores_max(g * NSA_HPG + (k - 2), k - 2)
                    if 0 <= k - 3 < NSA_HPG:
                        dve.wait_ge(pt_done, g * NSA_HPG + (k - 3) + 1)
                        dve.tensor_copy(pT[:, :, P:S], psum[:, 7, :].rearrange("p (a t) -> p a t", t=P)).then_inc(pt_v, 1)
                step.leave(NSA_G)

            base = PROJ_BLOCKS * UPB
            dve.wait_ge(stored[0], 16 * PROJ_BLOCKS // 2)
            dve.wait_ge(stored[1], 16 * PROJ_BLOCKS // 2)
            with dve.Fori(0, 2) as i:
                step.enter(i, 0, 2)
                for nbp in range(2):
                    nb = i * 2 + nbp
                    for k in range(6):
                        n = i * 12 + (base + nbp * 6 + k + 1)
                        lo(n, nbp * 6 + k + 1)
                        if k == UPG - 1:
                            dve.wait_ge(gab_sig, nb + 1)
                            dve.wait_ge(unit_done, n)
                            dve.tensor_tensor(mrg[:, 0, :, :], psum[:, 0:2, :], gab[:, 0, :, :], ALU.mult).then_inc(m_done, 1)
                    dve.wait_ge(unit_done, n)
                    step(dve.tensor_tensor(mrg[:, 1, :, :], psum[:, 2:4, :], gab[:, 1, :, :], ALU.mult))
                    dve.tensor_tensor(mrg[:, 1, :, :], mrg[:, 1, :, :], mrg[:, 0, :, :], ALU.add).then_inc(m_done, 1)
                    dve.wait_ge(m_hi, nb + 1)
                    dve.tensor_tensor(mT_lo[:, ds(nb * 4, 4), :].rearrange("p c t -> p (c t)"), psum[:, 4:6, :].rearrange("p b n -> p (b n)"),
                                      mT_hi[:, ds(nb * 4, 4), :].rearrange("p c t -> p (c t)").bitcast(F32), ALU.subtract).then_inc(m_lo, 1)
                step.leave(2)

            base = PROJ_BLOCKS * UPB + 4 * (UPG + UPB)
            dve.wait_ge(xn_in, 16)
            dve.wait_ge(g2_in, 16)
            with dve.Fori(0, 2) as i:
                for par in range(2):
                    b = i * 2 + par
                    for k in range(UPB):
                        n = i * 8 + (base + par * 4 + k + 1)
                        lo(n, k + 1)
                    dve.wait_ge(unit_done, n)
                    x = x_nat[:, :, ds(b * NB, NB)]
                    dve.tensor_tensor(x, x, psum[:, 2 * par:2 * par + 2, :], ALU.add).then_inc(x1_done, 1)
                    dve.wait_ge(x1_done, b + 1)
                    for t in range(NT):
                        ins = dve.tensor_tensor(mrg[:, 1, t, :], x_nat[:, t, ds(b * NB, NB)], g2[:, ds(b * NB, NB)], ALU.mult)
                    ins.then_inc(xg2_done, 1)
                    dve.wait_ge(x_hi, b + 1)
                    dve.tensor_tensor(h2T_lo[:, ds(b * 4, 4), :].rearrange("p c t -> p (c t)"), psum[:, 4:6, :].rearrange("p b n -> p (b n)"),
                                      h2T_hi[:, ds(b * 4, 4), :].rearrange("p c t -> p (c t)").bitcast(F32), ALU.subtract).then_inc(x_lo, 1)

            base = PROJ_BLOCKS * UPB + 4 * (UPG + UPB) + 4 * UPB
            dve.wait_ge(sq2, 8)
            step(dve.tensor_reduce(stat[:, 6:8], sq_x1[:, :, :], AX.X, ALU.add))
            dve.tensor_scalar(stat[:, 8:10], stat[:, 6:8], 1.0 / D, EPS, ALU.mult, ALU.add).then_inc(ms2_done, 1)
            dve.wait_ge(sq2_done, 1)
            step(dve.reciprocal(rstd2[:, :], stat[:, 10:12]))
            refine(rstd2[:, :], stat[:, 8:10]).then_inc(rs2_done, 1)
            for n in range(base + 1, UNITS):
                lo(n, n % 4)
            dve.wait_ge(unit_done, UNITS)
            dve.wait_ge(rs2_done, 1)
            for t in range(NT):
                ins = dve.scalar_tensor_tensor(h2[:, t, :], x_nat[:, t, :], rstd2[:, t:t + 1], g2[:, :], ALU.mult, ALU.mult)
            ins.then_inc(h2_done, 1)

            def top16(values, cut, top, index):
                step(dve.max(top[:, 0:8], values), alone=True)
                dve.max_index(index[:, 0:8], top[:, 0:8], values)
                step(dve.match_replace(cut, top[:, 0:8], values, -3e38), alone=True)
                step(dve.max(top[:, 8:16], cut), alone=True)
                step(dve.max_index(index[:, 8:16], top[:, 8:16], cut), alone=True)

            def route(u, par):
                step(dve.tensor_copy(s_now[:, :, :].rearrange("p a n -> p (a n)"), sc[:, ds(u, 1), :].rearrange("p a n -> p (a n)")), alone=True)
                for a in range(2):
                    top16(s_now[:, a, :], s_cut[:, a, :], v_top[:, a, :], i_top[:, a, :])
                dve.tensor_copy(if_top[:, :, :], i_top[:, :, :])
                step(dve.tensor_tensor(cand[:, :, :], v_top[:, 0, :, None].to_broadcast([P, TOPK, TOPK]),
                                       v_top[:, 1, None, :].to_broadcast([P, TOPK, TOPK]), ALU.add), alone=True)
                top16(cand[:, :, :].rearrange("p a b -> p (a b)"), cand_cut[:, :, :].rearrange("p a b -> p (a b)"), vals[:, :], flat[:, :])
                dve.tensor_scalar(rst[:, 0:1], vals[:, 0:1], -1.0, None, ALU.mult).then_inc(r_vals, 1)
                dve.tensor_scalar(ab[:, 0, :], flat[:, :], 4, None, ALU.logical_shift_right)
                step(dve.tensor_scalar(ab[:, 1, :], flat[:, :], TOPK - 1, None, ALU.bitwise_and))
                step(dve.tensor_copy(abf[:, :, :], ab[:, :, :]))
                for a in range(2):
                    ins = dve.tensor_tensor(hot[:, a, :, :], abf[:, a, :, None].to_broadcast([P, TOPK, TOPK]),
                                            iota16[:, None, :].to_broadcast([P, TOPK, TOPK]), ALU.is_equal)
                step(ins)
                for a in range(2):
                    ins = dve.tensor_tensor(hot[:, a, :, :], hot[:, a, :, :], if_top[:, a, None, :].to_broadcast([P, TOPK, TOPK]), ALU.mult)
                step(ins)
                step(dve.tensor_reduce(e12[:, :, :], hot[:, :, :, :], AX.X, ALU.add))
                dve.scalar_tensor_tensor(e_idx[:, par, :], e12[:, 0, :], float(PEER_NK), e12[:, 1, :], ALU.mult, ALU.add).then_inc(routed, 1)
                dve.wait_ge(r_exp, u + 1)
                step(dve.reciprocal(rst[:, 2:3], rst[:, 1:2]))
                step(dve.tensor_scalar(e_gate[:, par, :], rexp[:, :], rst[:, 2:3], None, ALU.mult))

            def weigh(u, par, k, first):
                if not (first and k < 4):
                    dve.wait_ge(acc_done, u * TOPK + (k - 3))
                dve.wait_ge(act_done, u * TOPK + k + 1)
                dve.tensor_scalar(diag[:, k % 4, :], ident[:, :], act_h[:, par, k:k + 1], e_gate[:, par, k:k + 1],
                                  ALU.mult, ALU.mult).then_inc(diag_done, 1)

            def picks(u, par, t, more=True, first=False):
                for k in range(TOPK):
                    n = par * TOPK + k
                    wait_alone(dve, landed[n % RING], (u - par) * (16 * TOPK // RING) + 16 * (n // RING + 1))
                    dve.tensor_tensor_reduce(junk[:, k % 2, :], ring[:, n % RING, 0:D], h2[:, t, :], 1.0, 0.0, ALU.mult, ALU.add,
                                             hid[:, par, k:k + 1]).then_inc(dot_done, 1)
                    if k >= 1:
                        weigh(u, par, k - 1, first)
                    if k == 3 and more:
                        route(u + 1, 1 - par)
                weigh(u, par, TOPK - 1, first)

            def norm_out(t):
                dve.wait_ge(acc_done, (t + 1) * PEER_H * TOPK)
                dve.tensor_tensor(x_nat[:, t, :], x_nat[:, t, :], psum[:, 4 * t:4 * t + 4, :].rearrange("p b n -> p (b n)"), ALU.add).then_inc(x2_done, 1)
                dve.wait_ge(fsq, t + 1)
                dve.tensor_scalar(stat[:, 2 + t:3 + t], stat[:, t:t + 1], 1.0 / D, EPS, ALU.mult, ALU.add).then_inc(fms, 1)
                dve.wait_ge(frs, t + 1)
                step(dve.reciprocal(stat[:, 6 + t:7 + t], stat[:, 4 + t:5 + t]))
                step(refine(stat[:, 6 + t:7 + t], stat[:, 2 + t:3 + t], 1))
                dve.scalar_tensor_tensor(h2[:, t, :], x_nat[:, t, :], stat[:, 6 + t:7 + t], gf[:, :], ALU.mult, ALU.mult).then_inc(out_done, 1)

            dve.wait_ge(gf_in, 32)
            dve.memset(zeros[:, :], 0.0).then_inc(zero_done, 1)
            ROUTE = 21
            route(0, 0)
            picks(0, 0, 0, first=True)
            picks(1, 1, 0)
            with dve.Fori(1, PEER_H // 2) as i:
                step.enter(i, 1, 2 * ROUTE)
                picks(i * 2, 0, 0)
                picks(i * 2 + 1, 1, 0)
                step.leave(PEER_H // 2 - 1)
            norm_out(0)
            with dve.Fori(PEER_H // 2, PEER_H - 1) as i:
                step.enter(i, PEER_H // 2, 2 * ROUTE)
                picks(i * 2, 0, 1)
                picks(i * 2 + 1, 1, 1)
                step.leave(PEER_H // 2 - 1)
            picks(UNITS_P - 2, 0, 1)
            picks(UNITS_P - 1, 1, 1, more=False)
            norm_out(1)


ROUND = float(3 << 22)
TWO_PI = (6.28125, 0.0019350051879882812, float(2 * np.pi - 6.28125 - 0.0019350051879882812))


def _gla_masks():
    s, t = np.arange(P)[:, None], np.arange(P)[None, :]
    levels = [(s // (2 * m) == t // (2 * m)) & (s % (2 * m) < m) & (t % (2 * m) >= m) for m in LEVELS]
    return np.stack([*levels, s == t], axis=1).astype(np.float32)


def _shape_constants():
    t = np.arange(S)
    tri = np.zeros((P, S), np.float32)
    tri[:, P:] = np.where(np.arange(P)[None, :] <= np.arange(P)[:, None], 0.0, MASKED)
    end = np.arange(NCMP) * CMP_STRIDE + CMP_BLOCK - 1
    cmask = np.where(end[None, :] <= t[:, None], 0.0, MASKED).astype(np.float32)
    inv = np.power(np.float32(ROPE_THETA), -(np.arange(0, ROT, 2, dtype=np.float32) / np.float32(ROT)))
    return {
        "ident": np.eye(P, dtype=np.float32), "tri": tri, "cmask": cmask.reshape(NT, P, NCMP).transpose(1, 0, 2),
        "inv_f": inv.astype(np.float32)[None, :], "gla_masks": _gla_masks(),
        "iota16": np.arange(TOPK, dtype=np.float32)[None, :],
    }


def _blocks(w):
    k, n = w.shape
    return w.reshape(k // (CU * P), CU, P, n // NB, NB).transpose(3, 0, 2, 1, 4).reshape(n // NB, k // (CU * P), P, UW)


def _layout(a):
    w = a["w_in"][0]
    kv = slice(2048, 5120)
    gate, gqk, glr, gr, ga = 5120, 5168, 7216, 7232, 8256
    order = np.concatenate([w[:, kv], w[:, gqk:glr], w[:, gr:ga], w[:, 0:2048], w[:, ga:]], axis=1)
    gla, nsa = _blocks(a["w_up_gla"][0]), _blocks(a["w_up_nsa"][0])
    merge = np.concatenate([gla, nsa], axis=1)
    units = np.concatenate([x.reshape(-1, P, UW) for x in (_blocks(order), merge, _blocks(a["w_out"][0]), _blocks(a["peer_w_q"][0]))])
    small = np.concatenate([w[:, glr:gr], w[:, gate:gqk]], axis=1).reshape(KC, P, 64).transpose(1, 0, 2)
    x = a["x"][0]
    keys = np.zeros((P, PEER_H, 2 * PEER_NK), np.float32)
    keys[:PEER_DK // 2, :, :PEER_NK] = a["peer_sub_k1"][0].transpose(2, 0, 1)
    keys[PEER_DK // 2:, :, PEER_NK:] = a["peer_sub_k2"][0].transpose(2, 0, 1)
    w1 = np.stack([a["nsa_cmp_k_w1"][0], a["nsa_cmp_v_w1"][0]]).reshape(2, 4, CMP_BLOCK // 4, DH, DH)
    return {
        "x": x.reshape(NT, P, D).transpose(1, 0, 2), "xT": x.T.reshape(KC, P, S).transpose(1, 0, 2),
        "positions": a["positions"].reshape(NT, P).T, "g1": a["norm1_g"][0].reshape(KC, P).T,
        "w_small": small, "w_units": units, "w_decay": a["gla_w_decay"][0], "b_decay": a["gla_b_decay"][0].reshape(GLA_H, P).T,
        "posT": np.stack([a["nsa_cmp_pos_k"][0], a["nsa_cmp_pos_v"][0]]).transpose(2, 0, 1),
        "w1": w1.transpose(0, 1, 3, 2, 4).reshape(8, DH, CMP_BLOCK // 4, DH),
        "w2": np.stack([a["nsa_cmp_k_w2"][0], a["nsa_cmp_v_w2"][0]], axis=1),
        "gla_g": a["gla_norm_g"], "g2": a["norm2_g"], "gf": a["final_g"][None, :], "keys": keys,
        "uv": np.concatenate([a["peer_u"][0], a["peer_v"][0]], axis=1),
    }


def kernel(**inputs):
    import concourse.bacc as bacc
    from concourse.bass_utils import run_bass_kernel_spmd as run

    nc = bacc.Bacc("TRN2", target_bir_lowering=False, num_devices=1)
    laid = {**_layout({k: np.asarray(v) for k, v in inputs.items()}), **_shape_constants()}
    arrays = {f"in_{name}": np.ascontiguousarray(a) for name, a in laid.items()}
    io = {name: nc.dram_tensor(f"in_{name}", arrays[f"in_{name}"].shape, mybir.dt.from_np(arrays[f"in_{name}"].dtype), kind="ExternalInput").ap()
          for name in laid}
    io["out"] = nc.dram_tensor("out_0", (S, D), F32, kind="ExternalOutput").ap()
    hybrid_block(nc, io)
    r = run(nc, [arrays], core_ids=[0])
    return r.results[0]["out_0"].reshape(1, S, D)
```

```python
from contextlib import ExitStack

import concourse.bass as bass
import numpy as np
from concourse import mybir

F32 = mybir.dt.float32
F32R = mybir.dt.float32r
BF16 = mybir.dt.bfloat16
I32 = mybir.dt.int32
U32 = mybir.dt.uint32
ALU = mybir.AluOpType
ACT = mybir.ActivationFunctionType
AX = mybir.AxisListType
ds = bass.ds

P = 128
D = 2048
S = 256
NT = S // P
KC = D // P
NB = 512
CU = 4
UW = CU * NB
EPS = 1e-6

GLA_H, GLA_DK, GLA_DV, GLA_LR, GLA_TAU = 4, 128, 256, 16, 16.0
NSA_G, NSA_HPG, DH = 4, 4, 128
NSA_H = NSA_G * NSA_HPG
W1_SLOTS = 6
ROT = DH // 4
HALF = ROT // 2
ROPE_THETA = 500000.0
CMP_BLOCK, CMP_STRIDE = 32, 16
NCMP = (S - CMP_BLOCK) // CMP_STRIDE + 1
PEER_H, PEER_NK, PEER_DK, TOPK = 8, 128, 128, 16
SCALE = float(DH) ** -0.5
MASKED = -1e30
MASKED_MAX = -1e29

B_KCM, B_VCM, B_GQ, B_GK, B_GV, B_GR, B_KSL, B_VSL, B_KWN, B_VWN, B_NQ, B_GA, B_GB = 0, 1, 2, 3, 4, 6, 8, 9, 10, 11, 12, 16, 20
PROJ_BLOCKS = 24
A_BLOCKS = 12
UPB = KC // CU
UPG = GLA_H * GLA_DV // P // CU
U0 = PROJ_BLOCKS * UPB + 4 * (UPG + UPB) + 4 * UPB + 2 * UPB
V0 = U0 + PEER_NK
UNITS = V0 + PEER_NK
RAW = 2
SPLIT = 4
AHEAD = SPLIT - 1

LEVELS = [64, 32, 16, 8, 4, 2, 1]
NL = len(LEVELS) + 2
KL_POOL = 5
L128, LDIAG = len(LEVELS), len(LEVELS) + 1

ROUTES = NT * PEER_H
PICKS = PEER_H * TOPK
TB = 16
VB = 4


def hybrid_block(nc, io):
    ctx = ExitStack()
    with ctx:
        def sem(name):
            return ctx.enter_context(nc.semaphore(name))

        def place(stack, name, shape, dt=F32):
            return stack.enter_context(nc.sbuf_tensor(name, shape, dt))

        KB = 1024
        buf = {}

        def region(offset, limit, *specs):
            with ExitStack() as stack:
                if offset:
                    stack.enter_context(nc.sbuf_tensor(f"below_{specs[0][0]}", [P, offset], mybir.dt.uint8))
                size = 0
                for name, shape, *dt in specs:
                    dt = dt[0] if dt else F32
                    buf[name] = stack.enter_context(nc.sbuf_tensor(name, shape, dt))
                    size += -(-int(np.prod(shape[1:])) * (2 if dt == BF16 else 4) // 32) * 32
                assert offset + size <= limit, (specs[0][0], offset + size, limit)

        AT_W, AT_EVAC, AT_MIX, AT_YN, AT_NSA, AT_X, END = (n * KB - 192 for n in (1, 81, 89, 130, 162, 192, 208))
        nlev = len(LEVELS) + 1
        region(0, AT_W, ("ident", [P, P]), ("rstd1", [P, NT]), ("rstd2", [P, NT]), ("stat", [P, 16]), ("newton", [P, NT]), ("sq_x1", [P, NT, 4]), ("glr", [P, NT, GLA_LR]))
        region(AT_W, AT_EVAC, ("w_raw", [P, RAW, UW]), ("w_hi", [P, SPLIT, UW], F32R), ("w_lo", [P, SPLIT, UW], F32R))
        region(AT_EVAC, AT_MIX, ("evac", [P, 2, NT, NB]))
        region(AT_X, END, ("ygT_hi", [P, 2 * GLA_H, S], F32R), ("ygT_lo", [P, 2 * GLA_H, S], F32R))
        region(AT_YN, AT_NSA, ("ynT_hi", [P, NSA_H, S], F32R), ("ynT_lo", [P, NSA_H, S], F32R))
        region(AT_X, END, ("x_nat", [P, NT, D]))
        region(AT_MIX, AT_YN, ("hT_hi", [P, KC, S], F32R), ("hT_lo", [P, KC, S], F32R), ("gates", [P, NT, 3 * NSA_H]),
               ("cos_t", [P, NT, HALF]), ("sin_t", [P, NT, HALF]), ("kcT", [P, NSA_G * NCMP]), ("vc", [NCMP, NSA_G, DH]),
               ("tri", [P, S]), ("cmask", [P, NT, NCMP]), ("bT", [P, GLA_H + 1, S]))
        region(AT_YN, AT_X, ("xgT", [P, KC, S]), ("g1", [P, KC]), ("w_small", [P, KC, 64]), ("pos_i", [P, NT], I32),
               ("pos_f", [P, NT]), ("inv_f", [P, HALF]), ("ang", [P, NT, HALF]), ("turns", [P, NT, HALF]), ("sq_junk", [P, D]))
        region(AT_YN, AT_X, ("glrT", [GLA_LR, S]), ("w_decay", [GLA_LR, GLA_H * GLA_DK]), ("b_decay", [P, GLA_H]),
               ("kv_c", [P, 2, NT, NSA_G * DH]), ("rot_c", [P, 4, NT, NSA_G, HALF]), ("kvT_c", [P, 2, NSA_G, S]),
               ("blk_c", [P, 2, CMP_BLOCK, NSA_G, NCMP]), ("posT", [P, 2, CMP_BLOCK]), ("w1", [P, W1_SLOTS, CMP_BLOCK // 4, DH]),
               ("w2", [P, 2, DH]), ("hid_c", [P, 2, NSA_G * NCMP]))
        region(AT_YN, AT_X, ("masks", [P, nlev, P]), ("gnorm", [P, GLA_DV]), ("qk_g", [P, 2, NT, GLA_DK]), ("v_g", [P, NT, GLA_DV]),
               ("r_g", [P, NT, GLA_DV]), ("sig_g", [P, NT, GLA_DV]), ("qT_g", [P, S]), ("kT_g", [P, S]), ("dec", [P, NL, S]),
               ("qL", [P, NL, S]), ("kL", [P, NL, S]), ("att_m", [P, nlev, P]), ("att_T", [P, 3, P]), ("y_g", [P, NT, GLA_DV]), ("gst", [P, 8]))
        region(AT_NSA, AT_X, ("qk_n", [P, NT, NSA_HPG + 2, DH]), ("rot_n", [P, 4, NT, NSA_HPG + 2, HALF]), ("v_n", [P, 2, NT, DH]),
               ("qkT", [P, NSA_HPG + 2, S]), ("g_n", [P, NT, 3 * NSA_HPG]), ("vc_n", [NCMP, DH]), ("sm", [P, 2, 3 * S]),
               ("smc", [P, 2, NT, NCMP]), ("mx", [P, 2, NT, 3]), ("nmx", [P, 2, NT, 3]), ("sums", [P, 2, NT, 3]), ("wts", [P, 2, NT, 3]),
               ("pT", [P, 4, S]), ("pcT", [NCMP, S]))
        region(AT_MIX, AT_YN, ("mT_hi", [P, KC, S], F32R), ("mT_lo", [P, KC, S], F32R), ("g2", [P, D]))
        region(AT_NSA, AT_X, ("gab", [P, 2, NT, NB]))
        region(AT_EVAC, AT_MIX, ("keys", [P, PEER_H, 2 * PEER_NK]))
        region(AT_MIX, AT_MIX + 16 * KB, ("sc", [P, ROUTES, 2 * PEER_NK]))
        region(AT_NSA, AT_NSA + 8 * KB, ("qpT", [P, PEER_H, S]))
        region(AT_MIX + 16 * KB, AT_YN, ("hst", [P, 2, 4 * S]), ("hs", [P, 2, 2 * S]), ("rs_row", [P, S]), ("rt", [P, 3, ROUTES, TOPK]),
               ("gate_b", [P, TB, PEER_NK]))
        region(AT_NSA + 16 * KB, AT_X, ("rtT", [P, 3, S]), ("rt16", [P, 3, TB]),
               ("iota", [P, PEER_NK]), ("s_now", [P, 2, PEER_NK]), ("s_cut", [P, 2, PEER_NK]), ("v_top", [P, 2, TOPK]),
               ("i_top", [P, 2, TOPK], U32), ("if_top", [P, 2, TOPK]), ("cand", [P, TOPK, TOPK]), ("cand_cut", [P, TOPK, TOPK]),
               ("vals", [P, TOPK]), ("flat", [P, TOPK], U32), ("ab", [P, 2, TOPK], U32), ("abf", [P, 2, TOPK]),
               ("ones", [P, P]), ("rs_diag", [P, NT, P]), ("hot", [P, 2, TOPK, TOPK]), ("e12", [P, 2, TOPK]), ("rexp", [P, TOPK]), ("rst", [P, 4]), ("zeros", [P, P]))
        region(AT_NSA, AT_NSA + 16 * KB, ("hot1a", [P, TB, PEER_NK]), ("hot2a", [P, TB, PEER_NK]))
        region(AT_MIX, AT_MIX + 16 * KB, ("hot1b", [P, TB, PEER_NK]), ("hot2b", [P, TB, PEER_NK]))
        region(AT_EVAC, AT_MIX, ("gate_a", [P, TB, PEER_NK]))
        region(AT_YN, AT_NSA, ("h_in", [P, 2, VB, S]), ("g_tab", [P, S // TB, 2 * VB, TB]), ("w_up", [P, 2, VB, S], F32R), ("w_low", [P, 2, VB, S], F32R))
        region(AT_MIX, AT_MIX + 16 * KB, ("out_t", [P, NT, D]))
        region(AT_MIX + 16 * KB, AT_YN, ("gf", [P, D]), ("sq_last", [P, D]))
        ident, rstd1, rstd2, stat, sq_x1, w_raw, w_hi, w_lo, evac = (buf["ident"], buf["rstd1"], buf["rstd2"], buf["stat"], buf["sq_x1"], buf["w_raw"], buf["w_hi"], buf["w_lo"], buf["evac"])
        ygT_hi, ygT_lo, ynT_hi, ynT_lo, x_nat, hT_hi, hT_lo, gates, cos_t = (buf["ygT_hi"], buf["ygT_lo"], buf["ynT_hi"], buf["ynT_lo"], buf["x_nat"], buf["hT_hi"], buf["hT_lo"], buf["gates"], buf["cos_t"])
        sin_t, kcT, vc, tri, cmask, bT, xgT, g1, w_small = (buf["sin_t"], buf["kcT"], buf["vc"], buf["tri"], buf["cmask"], buf["bT"], buf["xgT"], buf["g1"], buf["w_small"])
        pos_i, pos_f, inv_f, ang, turns, sq_junk, glrT, w_decay, b_decay = (buf["pos_i"], buf["pos_f"], buf["inv_f"], buf["ang"], buf["turns"], buf["sq_junk"], buf["glrT"], buf["w_decay"], buf["b_decay"])
        kv_c, rot_c, kvT_c, blk_c, posT, w1, w2, hid_c, masks = (buf["kv_c"], buf["rot_c"], buf["kvT_c"], buf["blk_c"], buf["posT"], buf["w1"], buf["w2"], buf["hid_c"], buf["masks"])
        gnorm, qk_g, v_g, r_g, sig_g, qT_g, kT_g, dec, qL = (buf["gnorm"], buf["qk_g"], buf["v_g"], buf["r_g"], buf["sig_g"], buf["qT_g"], buf["kT_g"], buf["dec"], buf["qL"])
        kL, att_m, att_T, y_g, gst, qk_n, rot_n, v_n, qkT = (buf["kL"], buf["att_m"], buf["att_T"], buf["y_g"], buf["gst"], buf["qk_n"], buf["rot_n"], buf["v_n"], buf["qkT"])
        g_n, vc_n, sm, smc, mx, nmx, sums, wts, pT = (buf["g_n"], buf["vc_n"], buf["sm"], buf["smc"], buf["mx"], buf["nmx"], buf["sums"], buf["wts"], buf["pT"])
        pcT, mT_hi, mT_lo, g2, gab, qpT, keys, sc, hst = (buf["pcT"], buf["mT_hi"], buf["mT_lo"], buf["g2"], buf["gab"], buf["qpT"], buf["keys"], buf["sc"], buf["hst"])
        hs, rs_row, rt, gate_a, gate_b, rtT, rt16, iota, s_now = (buf["hs"], buf["rs_row"], buf["rt"], buf["gate_a"], buf["gate_b"], buf["rtT"], buf["rt16"], buf["iota"], buf["s_now"])
        s_cut, v_top, i_top, if_top, cand, cand_cut, vals, flat, ab = (buf["s_cut"], buf["v_top"], buf["i_top"], buf["if_top"], buf["cand"], buf["cand_cut"], buf["vals"], buf["flat"], buf["ab"])
        abf, hot, e12, rexp, rst, zeros, hot1a, hot2a, hot1b, hot2b, h_in = (buf["abf"], buf["hot"], buf["e12"], buf["rexp"], buf["rst"], buf["zeros"], buf["hot1a"], buf["hot2a"], buf["hot1b"], buf["hot2b"], buf["h_in"])
        g_tab, w_up, w_low, out_t, gf, sq_last = (buf["g_tab"], buf["w_up"], buf["w_low"], buf["out_t"], buf["gf"], buf["sq_last"])
        hots = ((hot1a, hot2a), (hot1b, hot2b))
        glr, newton, ones, rs_diag = buf["glr"], buf["newton"], buf["ones"], buf["rs_diag"]
        mrg = evac
        h2T_hi, h2T_lo = ynT_hi, ynT_lo
        zT = kvT_c[:, 0, :, :].rearrange("p g t -> p (g t)")
        zA = kvT_c[:, 1, :, :].rearrange("p g t -> p (g t)")

        psum = ctx.enter_context(nc.psum_tensor("psum", [P, 8, NB], F32))
        hid = nc.dram_tensor("hid_scratch", [PEER_NK // 4, P, 4 * S], F32, kind="Internal").ap()
        tab = nc.dram_tensor("tab_scratch", [S // TB, P, PEER_NK, TB], F32, kind="Internal").ap()
        proj = nc.dram_tensor("proj_scratch", [PROJ_BLOCKS, P, NT, NB], F32, kind="Internal").ap()

        def sems(*names):
            return [sem(n) for n in names]

        xT_in = sems(*(f"xT_landed{q}" for q in range(4)))
        xn_in, const_in, small_in, ssq1, ms1_done, sq1_done, rs1_done = sems(
            "xn_in", "const_in", "small_in", "ssq1", "ms1_done", "sq1_done", "rs1_done")
        xg_done, h_hi, h_lo, ang_ready, trig_done, small_done, small_out = sems(
            "xg_done", "h_hi", "h_lo", "ang_ready", "trig_done", "small_done", "small_out")
        v_step, a_step = sems("v_step", "a_step")
        w_in_s = sems(*(f"w_landed{k}" for k in range(RAW)))
        hi_done, lo_done, unit_done, evac_done = sems("hi_done", "lo_done", "unit_done", "evac_done")
        stored = sems("stored0", "stored1")
        prep_in, kvc_in, w1_used, pe_prep, act_prep, dve_prep = sems("prep_in", "kvc_in", "w1_used", "pe_prep", "act_prep", "dve_prep")
        w1_in = sems(*(f"w1_landed{k}" for k in range(W1_SLOTS)))
        g_msk, g_one, g_in, g_vr_in, g_silu, g_qkt, g_qe, g_ke, g_dec, g_exp, g_ql, g_kl = sems(
            "g_consts_in", "g_ones", "g_qk_in", "g_vr_in", "g_silu", "g_turned", "g_q_out", "g_k_out", "g_decay", "g_exp", "g_q_scaled", "g_k_scaled")
        g_lev, g_att, g_a01, g_o, g_rn, g_sig, g_y, g_yt, g_yhi, g_ylo = sems(
            "g_levels", "g_att", "g_att01", "g_out", "g_rnorm", "g_sig", "g_y", "g_y_turned", "g_y_hi", "g_y_lo")
        nqk_in, nv_in, roped, qkt_done, qkt_a, qkt_v, vcn_done = sems(
            "n_qk_in", "n_v_in", "n_roped", "n_qk_turned", "n_qk_out_act", "n_qk_out_dve", "n_vc_ready")
        s_done, mx_done, exp_done, p_done, pt_done, pt_a, pt_v, pv_done, o_hi, o_lo = sems(
            "scores_done", "max_done", "exp_done", "probs_done", "probs_turned", "pT_out_act", "pT_out_dve", "pv_done", "o_hi", "o_lo")
        gab_in, gab_sig, m_done, mt_done, m_hi, m_lo, g2_in = sems(
            "gates_in", "gates_sig", "merge_read", "merged_turned", "m_hi", "m_lo", "g2_in")
        x1_done, sq2, xg2_done, xt_done, x_hi, x_lo, ms2_done, sq2_done, rs2_done, h2_done = sems(
            "x1_done", "sq2", "xg2_done", "xg2_turned", "x_hi", "x_lo", "ms2_done", "sq2_done", "rs2_done", "h2_done")
        qpt_out, sc_done, sc_out, keys_in, iota_in, gf_in = sems("queryT_out", "sc_done", "sc_out", "keys_in", "iota_in", "gf_in")
        rsd_done, rs_row_done, rs_row_out, zero_done, r_vals, r_exp, routed = sems(
            "rs_diag_done", "rs_row_done", "rs_row_out", "zero_done", "r_vals", "r_exp", "routed")
        hid_scaled, hid_gelu = sems("hid_scaled", "hid_gelu")
        hid_st = sems("hid_stored0", "hid_stored1")
        rt_turned, rt_out, rt16_done, hot1_done, hot2_done, tab_done, tab_out = sems(
            "rt_turned", "rt_out", "rt16_done", "hot1_done", "hot2_done", "tab_done", "tab_out")
        tab_st = sems("tab_stored0", "tab_stored1")
        v_in, prod_done, wup_done, wlow_done, acc_done = sems("v_operands_in", "prod_done", "w_up_done", "w_low_done", "acc_done")
        x2_done, fsq, fms, frs, out_done, out_st = sems("x2_done", "fsq", "fms", "frs", "out_done", "out_stored")

        block = ctx.enter_context(nc.Block())

        def wait_alone(eng, s, value):
            eng.wait_ge(s, value)
            eng.nop(nofuse=True)

        class Steps:

            def __init__(self, eng, s):
                self.eng, self.s, self.n, self.base = eng, s, 0, 0

            def __call__(self, ins, alone=False):
                self.n += 1
                ins.then_inc(self.s, 1)
                self.eng.wait_ge(self.s, self.base + self.n)
                if alone:
                    self.eng.nop(nofuse=True)

            def enter(self, i, first, per):
                self.start, self.per = self.n, per
                self.base, self.first = (i - first) * per, first

            def leave(self, count):
                assert self.n - self.start == self.per, (self.n - self.start, self.per)
                self.n = self.start + self.per * count
                self.base = 0

        @block.sync
        def _(sp):
            for q in range(4):
                sp.dma_start(xgT[:, 4 * q:4 * q + 4, :], io["xT"][:, 4 * q:4 * q + 4, :]).then_inc(xT_in[q], 16)
                if q < RAW:
                    sp.dma_start(w_raw[:, q, :], io["w_units"][q]).then_inc(w_in_s[q], 16)
            with sp.Fori(1, UNITS // RAW) as i:
                for s in range(RAW):
                    sp.wait_ge(hi_done, i * RAW + (s - RAW + 1))
                    sp.wait_ge(lo_done, i * RAW + (s - RAW + 1))
                    sp.dma_start(w_raw[:, s, :], io["w_units"][ds(i * RAW + s, 1), :, :].rearrange("a p n -> p (a n)")).then_inc(w_in_s[s], 16)
            for t in range(NT):
                sp.wait_ge(out_done, t + 1)
                sp.dma_start(io["out"][t * P:(t + 1) * P, :], out_t[:, t, :]).then_inc(out_st, 16)
            sp.wait_ge(out_st, 16 * NT)

        @block.gpsimd
        def _(pool):
            pool.wait_ge(xT_in[3], 16)
            pool.dma_start(x_nat[:, :, :], io["x"]).then_inc(xn_in, 16)
            pool.dma_start(w_small[:, :, :], io["w_small"]).then_inc(small_in, 16)
            pool.wait_ge(small_done, 1)
            pool.wait_ge(h_lo, 4)
            pool.wait_ge(trig_done, 2)
            for dst, name in ((w_decay[:, :], "w_decay"), (b_decay[:, :], "b_decay"), (posT[:, :, :], "posT"), (w2[:, :, :], "w2")):
                pool.dma_start(dst, io[name]).then_inc(prep_in, 16)
            pool.wait_ge(stored[0], 16)
            pool.wait_ge(stored[1], 16)
            for a, b in ((0, B_KCM), (1, B_VCM)):
                pool.dma_start(kv_c[:, a, :, :], proj[b]).then_inc(kvc_in, 16)
            for n in range(8):
                if n >= W1_SLOTS:
                    pool.wait_ge(w1_used, n - W1_SLOTS + 1)
                pool.dma_start(w1[:, n % W1_SLOTS, :, :], io["w1"][n]).then_inc(w1_in[n % W1_SLOTS], 16)

            pool.wait_ge(pe_prep, 5)
            pool.wait_ge(act_prep, 8)
            pool.wait_ge(dve_prep, 11)
            pool.dma_start(masks[:, :, :], io["gla_masks"]).then_inc(g_msk, 16)
            pool.dma_start(gnorm[:, :], io["gla_g"].partition_broadcast(P)).then_inc(g_msk, 16)
            for k in range(2):
                pool.wait_ge(stored[k], 16 * B_KSL // 2)
            def distances(h):
                for n, m in enumerate([*LEVELS, P]):
                    b = bT[:, ds(h, 1), :].rearrange("p a (n m) -> p (a n) m", m=2 * m)
                    ins = pool.tensor_tensor(dec[:, n, :].rearrange("p (n m) -> p n m", m=2 * m), b,
                                             b[:, :, m - 1:m].to_broadcast([P, S // (2 * m), 2 * m]), ALU.subtract)
                ins.then_inc(g_dec, 1)

            distances(0)
            pool.wait_ge(g_one, 1)
            with pool.Fori(0, GLA_H // 2) as i:
                for hp in range(2):
                    h = i * 2 + hp
                    wait_alone(pool, g_qkt, h)
                    for a, b in ((0, B_GQ), (1, B_GK)):
                        pool.dma_start(qk_g[:, a, :, :], proj[b][:, :, ds(h * GLA_DK, GLA_DK)]).then_inc(g_in, 16)
                    wait_alone(pool, g_o, h)
                    wait_alone(pool, g_y, h)
                    wait_alone(pool, g_sig, h)
                    for dst, b in ((v_g, B_GV), (r_g, B_GR)):
                        pool.dma_start(dst[:, :, :], proj[ds(i + b, 1), :, :, hp * GLA_DV:(hp + 1) * GLA_DV].rearrange("a p t n -> p (a t) n")).then_inc(g_vr_in, 16)
                    wait_alone(pool, g_exp, h + 1)
                    wait_alone(pool, g_ke, h + 1)
                    pool.tensor_tensor(kL[:, 0:KL_POOL, :], dec[:, 0:KL_POOL, :], kT_g[:, None, :].to_broadcast([P, KL_POOL, S]), ALU.mult).then_inc(g_kl, 1)
                    wait_alone(pool, g_sig, h + 1)
                    pool.tensor_tensor(sig_g[:, :, :], sig_g[:, :, :], r_g[:, :, :], ALU.mult).then_inc(g_silu, 1)
                    wait_alone(pool, g_kl, h + 1)
                    wait_alone(pool, g_ql, h + 1)
                    distances(h + 1)

            pool.wait_ge(g_ylo, GLA_H)
            pool.wait_ge(g_yhi, GLA_H)
            pool.wait_ge(stored[0], 16 * (A_BLOCKS + 4) // 2)
            pool.wait_ge(stored[1], 16 * (A_BLOCKS + 4) // 2)
            with pool.Fori(0, NSA_G) as g:
                wait_alone(pool, qkt_done, g)
                pool.dma_start(qk_n[:, :, 0:NSA_HPG, :], proj[ds(g + B_NQ, 1), :, :, :].rearrange("a p t (h d) -> p (a t) h d", d=DH)).then_inc(nqk_in, 16)
                for a, b in ((NSA_HPG, B_KSL), (NSA_HPG + 1, B_KWN)):
                    pool.dma_start(qk_n[:, :, a, :], proj[b][:, :, ds(g * DH, DH)]).then_inc(nqk_in, 16)
                wait_alone(pool, pv_done, g * NSA_HPG)
                for a, b in ((0, B_VSL), (1, B_VWN)):
                    pool.dma_start(v_n[:, a, :, :], proj[b][:, :, ds(g * DH, DH)]).then_inc(nv_in, 16)

            pool.wait_ge(pv_done, NSA_H)
            pool.wait_ge(o_lo, NSA_H)
            pool.wait_ge(unit_done, PROJ_BLOCKS * UPB)
            pool.wait_ge(stored[0], 16 * PROJ_BLOCKS // 2)
            pool.wait_ge(stored[1], 16 * PROJ_BLOCKS // 2)
            pool.dma_start(g2[:, :], io["g2"].partition_broadcast(P)).then_inc(g2_in, 16)
            with pool.Fori(0, 4) as nb:
                wait_alone(pool, m_done, nb * 2)
                for a, b in ((0, B_GA), (1, B_GB)):
                    pool.dma_start(gab[:, a, :, :], proj[ds(nb + b, 1), :, :, :].rearrange("a p t n -> p (a t) n")).then_inc(gab_in, 16)

            pool.wait_ge(unit_done, PROJ_BLOCKS * UPB + 3 * (UPG + UPB) + UPG)
            pool.dma_start(x_nat[:, :, :], io["x"]).then_inc(xn_in, 16)

            pool.wait_ge(xt_done, 4)
            pool.dma_start(keys[:, :, :], io["keys"]).then_inc(keys_in, 16)
            pool.dma_start(iota[:, :], io["iota"].partition_broadcast(P)).then_inc(iota_in, 16)

            def v_load(i):
                pool.dma_start(h_in[:, :, :, :].rearrange("p a c t -> p a (c t)"),
                               hid[ds(i * 2, 2), :, :].rearrange("a p n -> p a n")).then_inc(v_in, 16)
                pool.dma_start(g_tab[:, :, :, :], tab[:, :, ds(i * 2 * VB, 2 * VB), :].rearrange("b p c t -> p b c t")).then_inc(v_in, 16)

            pool.wait_ge(unit_done, V0)
            for half in range(2):
                pool.wait_ge(hid_st[half], 16 * PEER_NK // 8)
                pool.wait_ge(tab_st[half], 16 * (S // TB - 4) if half == 0 else 16 * 4)
            v_load(0)
            pool.dma_start(gf[:, :], io["gf"].partition_broadcast(P)).then_inc(gf_in, 16)
            with pool.Fori(1, PEER_NK // (2 * VB)) as i:
                wait_alone(pool, wlow_done, i * 2)
                v_load(i)

        @block.scalar
        def _(act):
            step = Steps(act, a_step)

            def hi(n, s):
                act.wait_ge(w_in_s[s % RAW], (n - s % RAW) * (16 // RAW) + 16)
                wait = n - (SPLIT - 1)
                if not (isinstance(wait, int) and wait <= 0):
                    act.wait_ge(unit_done, wait)
                act.activation(w_hi[:, s % SPLIT, :], w_raw[:, s % RAW, :], ACT.Copy).then_inc(hi_done, 1)

            def evacuate(b, par, first=False):
                act.wait_ge(unit_done, b * UPB + UPB)
                if not first:
                    act.wait_ge(stored[par], (b - par) * 8)
                for t in range(NT):
                    act.activation(evac[:, par, t, :], psum[:, 2 * par + t, :], ACT.Copy, scale=rstd1[:, t:t + 1]).then_inc(evac_done, 1)
                act.wait_ge(evac_done, b * 2 + 2)
                dst = proj[b] if isinstance(b, int) else proj[ds(b, 1), :, :, :].rearrange("a p t n -> p (a t) n")
                act.dma_start(dst, evac[:, par, :, :]).then_inc(stored[par], 16)

            for dst, name in ((g1[:, :], "g1"), (ident[:, :], "ident"), (pos_i[:, :], "positions"),
                              (tri[:, :], "tri"), (cmask[:, :, :], "cmask")):
                act.dma_start(dst, io[name]).then_inc(const_in, 16)
            act.dma_start(inv_f[:, :], io["inv_f"].partition_broadcast(P)).then_inc(const_in, 16)
            for q in range(4):
                act.wait_ge(xg_done, q + 1)
                act.activation(hT_hi[:, 4 * q:4 * q + 4, :], xgT[:, 4 * q:4 * q + 4, :], ACT.Copy).then_inc(h_hi, 1)
                if q < AHEAD:
                    hi(q, q)

            for k in range(UPB):
                hi(k + AHEAD, k + AHEAD)
                if k == 1:
                    act.wait_ge(xn_in, 16)
                    for t in range(NT):
                        act.activation(sq_junk[:, :], x_nat[:, t, :], ACT.Square, accum_out=stat[:, t:t + 1]).then_inc(ssq1, 1)
                        act.wait_ge(ssq1, t + 1)
                if k == 2:
                    act.wait_ge(ms1_done, 1)
                    act.activation(stat[:, 4:6], stat[:, 2:4], ACT.Sqrt).then_inc(sq1_done, 1)
                    act.wait_ge(ang_ready, 1)
                    act.activation(sin_t[:, :, :], ang[:, :, :], ACT.Sin).then_inc(trig_done, 1)
                    act.activation(turns[:, :, :], ang[:, :, :], ACT.Sin, scale=0.5).then_inc(trig_done, 1)
            act.wait_ge(small_done, 1)
            act.wait_ge(rs1_done, 1)
            for t in range(NT):
                act.activation(glr[:, t, :], psum[:, 4, t * 64:t * 64 + GLA_LR], ACT.Copy, scale=rstd1[:, t:t + 1]).then_inc(small_out, 1)
                act.activation(gates[:, t, :], psum[:, 4, t * 64 + GLA_LR:(t + 1) * 64], ACT.Sigmoid, scale=rstd1[:, t:t + 1]).then_inc(small_out, 1)
            evacuate(0, 0, True)
            for k in range(UPB):
                hi(UPB + k + AHEAD, k + AHEAD)
            evacuate(1, 1, True)
            for k in range(2 * UPB):
                hi(2 * UPB + k + AHEAD, k + AHEAD)
                if k == 0:
                    act.wait_ge(pe_prep, 1)
                    act.activation(glrT[:, :], psum[0:GLA_LR, 4, 0:S], ACT.Copy).then_inc(act_prep, 1)
                if k == 1:
                    act.wait_ge(dve_prep, 4)
                    step(act.activation(zA, zT, ACT.Abs))
                    step(act.activation(zA, zA, ACT.Exp, scale=-1.0))
                    act.activation(zA, zA, ACT.Ln, bias=1.0).then_inc(act_prep, 1)
                if k in (3, 4):
                    a = k - 3
                    act.wait_ge(pe_prep, 3 + a)
                    act.activation(kvT_c[:, a, :, :].rearrange("p g t -> p (g t)"), psum[:, 4 + 2 * a:6 + 2 * a, :].rearrange("p b n -> p (b n)"), ACT.Copy).then_inc(act_prep, 1)
                if k in (5, 6):
                    a = k - 5
                    act.wait_ge(w1_used, 4 * a + 4)
                    act.activation(hid_c[:, a, :], psum[:, 4 + a, 0:NSA_G * NCMP], ACT.Gelu_apprx_tanh).then_inc(act_prep, 1)
                if k == 7:
                    act.wait_ge(pe_prep, 5)
                    act.activation(kcT[:, :], psum[:, 6, 0:NSA_G * NCMP], ACT.Copy).then_inc(act_prep, 1)
                    act.activation(vc[:, :, :].rearrange("n g d -> n (g d)"), psum[0:NCMP, 7, :], ACT.Copy).then_inc(act_prep, 1)
                if k % UPB == UPB - 1:
                    evacuate(2 + k // UPB, k // UPB)
            with act.Fori(2, A_BLOCKS // 2) as i:
                for par in range(2):
                    for k in range(UPB):
                        hi(i * 8 + (par * 4 + k + AHEAD), k + AHEAD)
                    evacuate(i * 2 + par, par)

            def decays(h):
                act.wait_ge(g_dec, h + 1)
                step(act.activation(dec[:, 0:LDIAG, :], dec[:, 0:LDIAG, :], ACT.Abs))
                act.activation(dec[:, 0:LDIAG, :], dec[:, 0:LDIAG, :], ACT.Exp, scale=-1.0 / GLA_TAU).then_inc(g_exp, 1)

            def gla_slot(h, k):
                if k == 0:
                    act.wait_ge(g_qkt, h + 1)
                    act.activation(qT_g[:, :], psum[:, 4, 0:S], ACT.Copy, scale=GLA_DK ** -0.5).then_inc(g_qe, 1)
                    act.wait_ge(g_vr_in, h * 32 + 32)
                    act.activation(sig_g[:, :, :], r_g[:, :, :], ACT.Sigmoid).then_inc(g_sig, 1)
                if k == 2:
                    act.wait_ge(g_o, h + 1)
                    for t in range(NT):
                        step(act.activation(y_g[:, t, :], psum[:, 7, t * GLA_DV:(t + 1) * GLA_DV], ACT.Square, accum_out=gst[:, t:t + 1]))
                    act.activation(gst[:, 2:4], gst[:, 0:2], ACT.Sqrt, scale=1.0 / GLA_DV, bias=eps_ap).then_inc(g_rn, 1)
                if k == 3:
                    decays(h + 1)
                    act.wait_ge(g_yt, h + 1)
                    act.activation(ygT_hi[:, ds(h * 2, 2), :].rearrange("p c t -> p (c t)"), psum[:, 4, :], ACT.Copy).then_inc(g_yhi, 1)

            eps_ap = stat[:, 12:13]
            act.wait_ge(g_msk, 32)
            decays(0)
            base = A_BLOCKS * UPB
            with act.Fori(0, GLA_H // 2) as i:
                step.enter(i, 0, 2 * 3)
                for hp in range(2):
                    for k in range(UPB):
                        hi(i * 8 + (base + hp * 4 + k + AHEAD), k + AHEAD)
                        gla_slot(i * 2 + hp, k)
                    evacuate(i * 2 + (A_BLOCKS + hp), hp)
                step.leave(GLA_H // 2)

            base = (A_BLOCKS + 4) * UPB
            with act.Fori(0, NSA_G) as g:
                for k in range(8):
                    hi(g * 8 + (base + k + AHEAD), k + AHEAD)
                    if k == 0:
                        act.wait_ge(pv_done, g * NSA_HPG)
                        act.activation(vc_n[:, :], vc[:, ds(g, 1), :].rearrange("n a d -> n (a d)"), ACT.Copy).then_inc(vcn_done, 1)
                    if k == 1:
                        act.wait_ge(qkt_done, g + 1)
                        for b in range(2):
                            act.activation(qkT[:, 2 * b:2 * b + 2, :].rearrange("p h t -> p (h t)"), psum[:, 4 + b, :], ACT.Copy).then_inc(qkt_a, 1)
                    j = k - 4
                    if 0 <= j < NSA_HPG:
                        act.wait_ge(pv_done, g * NSA_HPG + j + 1)
                        act.activation(ynT_hi[:, ds(g * NSA_HPG + j, 1), :].rearrange("p a t -> p (a t)"), psum[:, 6, S:2 * S], ACT.Copy).then_inc(o_hi, 1)
                    j = k - 3
                    if 0 <= j < NSA_HPG:
                        act.wait_ge(pt_done, g * NSA_HPG + j + 1)
                        act.activation(pT[:, 0:2, 0:P], psum[:, 6, 0:S].rearrange("p (a t) -> p a t", a=2), ACT.Copy).then_inc(pt_a, 1)
                        act.activation(pcT[:, :], psum[0:NCMP, 6, S:2 * S], ACT.Copy).then_inc(pt_a, 1)
                    j = k - 2
                    if 0 <= j < NSA_HPG:
                        q = j % 2
                        act.wait_ge(mx_done, g * NSA_HPG + j + 1)
                        for t in range(NT):
                            for b in (2, 0, 1):
                                w = (b + 1) % 3
                                src = smc[:, q, t, :] if b == 2 else sm[:, q, 2 * P * t + b * (t + 1) * P:2 * P * t + (b + 1) * (t + 1) * P]
                                act.activation(src, src, ACT.Exp, scale=SCALE, bias=nmx[:, q, t, w:w + 1],
                                               accum_out=sums[:, q, t, w:w + 1]).then_inc(exp_done, 1)
                    if k % 4 == 3:
                        evacuate(g * 2 + (A_BLOCKS + 4 + k // 4), k // 4)

            base = PROJ_BLOCKS * UPB
            act.wait_ge(stored[0], 16 * PROJ_BLOCKS // 2)
            act.wait_ge(stored[1], 16 * PROJ_BLOCKS // 2)
            with act.Fori(0, 2) as i:
                for nbp in range(2):
                    nb = i * 2 + nbp
                    for k in range(6):
                        hi(i * 12 + (base + nbp * 6 + k + AHEAD), nbp * 6 + k + AHEAD)
                        if k == 0:
                            act.wait_ge(gab_in, nb * 32 + 32)
                            act.activation(gab[:, :, :, :], gab[:, :, :, :], ACT.Sigmoid).then_inc(gab_sig, 1)
                        if (nbp, k) in ((1, 0), (1, 5)):
                            m = nb - 1 if k == 0 else nb
                            act.wait_ge(mt_done, m + 1)
                            act.activation(mT_hi[:, ds(m * 4, 4), :].rearrange("p c t -> p (c t)"), psum[:, 4:6, :].rearrange("p b n -> p (b n)"), ACT.Copy).then_inc(m_hi, 1)

            def x_upper(b):
                act.wait_ge(xt_done, b + 1)
                act.activation(h2T_hi[:, ds(b * 4, 4), :].rearrange("p c t -> p (c t)"), psum[:, 4:6, :].rearrange("p b n -> p (b n)"), ACT.Copy).then_inc(x_hi, 1)

            base = PROJ_BLOCKS * UPB + 4 * (UPG + UPB)
            with act.Fori(0, 2) as i:
                for par in range(2):
                    b = i * 2 + par
                    for k in range(UPB):
                        hi(i * 8 + (base + par * 4 + k + AHEAD), k + AHEAD)
                        if (par, k) == (1, 0):
                            x_upper(b - 1)
                    act.wait_ge(x1_done, b + 1)
                    for t in range(NT):
                        act.activation(gab[:, t, 0, :], x_nat[:, t, ds(b * NB, NB)], ACT.Square, accum_out=sq_x1[:, t, ds(b, 1)]).then_inc(sq2, 1)
                        act.wait_ge(sq2, b * 2 + t + 1)
                x_upper(b)

            base = PROJ_BLOCKS * UPB + 4 * (UPG + UPB) + 4 * UPB
            def scores_out(par):
                act.wait_ge(rs2_done, 1)
                act.wait_ge(sc_done, par + 1)
                for t in range(NT):
                    act.activation(sc[:, t * PEER_H + 4 * par:t * PEER_H + 4 * par + 4, :].rearrange("p h n -> p (h n)"),
                                   psum[:, 4 + 2 * t:6 + 2 * t, :].rearrange("p b n -> p (b n)"), ACT.Copy, scale=rstd2[:, t:t + 1]).then_inc(sc_out, 1)

            act.wait_ge(ms2_done, 1)
            act.activation(stat[:, 10:12], stat[:, 8:10], ACT.Sqrt).then_inc(sq2_done, 1)
            for par in range(2):
                for k in range(UPB):
                    n = base + par * 4 + k + AHEAD
                    hi(n, n % 4)
                    if (par, k) == (1, 0):
                        scores_out(0)
                act.wait_ge(unit_done, base + par * UPB + UPB)
                act.activation(qpT[:, 4 * par:4 * par + 4, :].rearrange("p h t -> p (h t)"), psum[:, 2 * par:2 * par + 2, :].rearrange("p b n -> p (b n)"), ACT.Copy).then_inc(qpt_out, 1)
            scores_out(1)

            def route_exp(u):
                act.wait_ge(r_vals, u + 1)
                act.activation(rexp[:, :], vals[:, :], ACT.Exp, bias=rst[:, 0:1], accum_out=rst[:, 1:2]).then_inc(r_exp, 1)

            def table_out(tb, half, prior):
                act.wait_ge(tab_done, tb + 1)
                if prior is not None:
                    act.wait_ge(tab_st[half], 16 * prior)
                dst = (gate_a, gate_b)[half]
                src = psum[:, 4:8, :] if half == 0 else psum[:, 0:4, :]
                act.activation(dst[:, :, :].rearrange("p a b -> p (a b)").rearrange("p (c t) -> p t c", t=TB),
                               src.rearrange("p b (t c) -> p (b t) c", c=PEER_NK), ACT.Copy).then_inc(tab_out, 1)
                act.wait_ge(tab_out, tb + 1)
                dram = tab[tb] if isinstance(tb, int) else tab[ds(tb, 1), :, :, :].rearrange("a p c t -> p (a c) t")
                act.dma_start(dram, dst[:, :, :].rearrange("p a b -> p (a b)").rearrange("p (c t) -> p c t", t=TB)).then_inc(tab_st[half], 16)

            def hidden(i, table):
                for k in range(8):
                    hi(i * 8 + (U0 + k + AHEAD), k + AHEAD)
                    if k == 5:
                        route_exp(i)
                    if k % 2 == 1:
                        m, half = i * 4 + k // 2, k // 4
                        act.wait_ge(hid_scaled, m + 1)
                        if k % 4 == 1 and not (isinstance(i, int) and i == 0):
                            act.wait_ge(hid_st[half], i * 16)
                        o = (k // 2 % 2) * 2 * S
                        act.activation(hst[:, half, o:o + 2 * S], hs[:, k // 2 % 2, :], ACT.Gelu_apprx_tanh).then_inc(hid_gelu, 1)
                        if k % 4 == 3:
                            act.wait_ge(hid_gelu, m + 1)
                            dst = hid[2 * i + half] if isinstance(i, int) else hid[ds(i * 2 + half, 1), :, :].rearrange("a p n -> p (a n)")
                            act.dma_start(dst, hst[:, half, :]).then_inc(hid_st[half], 16)
                    if k == 6 and table:
                        table_out(i - PEER_H, 0, None if isinstance(i, int) else i - PEER_H)

            def picks_out(t):
                act.wait_ge(rt_turned, t + 1)
                act.activation(rtT[:, :, t * P:(t + 1) * P], psum[:, 4, 0:3 * P].rearrange("p (w n) -> p w n", w=3), ACT.Copy).then_inc(rt_out, 1)

            hidden(0, False)
            with act.Fori(1, PEER_H) as i:
                hidden(i, False)
            picks_out(0)
            hidden(PEER_H, True)
            with act.Fori(PEER_H + 1, 2 * PEER_H) as i:
                hidden(i, True)
            picks_out(1)
            for half in range(2):
                table_out(PEER_H + half, half, (PEER_H, None)[half])
            with act.Fori(PEER_H // 2 + 1, PEER_H) as j:
                for half in range(2):
                    table_out(j * 2 + half, half, j + (PEER_H // 2, -PEER_H // 2)[half])

            def weights_upper(m, half):
                act.wait_ge(prod_done, m + 1)
                act.activation(w_up[:, half, :, :], h_in[:, half, :, :], ACT.Copy).then_inc(wup_done, 1)

            def experts_out(i, last=False):
                for k in range(8):
                    if not (last and k + AHEAD >= 8):
                        hi(i * 8 + (V0 + k + AHEAD), k + AHEAD)
                    if k == 0:
                        weights_upper(i * 2 + 1, 1)
                    if k == 4 and not last:
                        weights_upper(i * 2 + 2, 0)

            weights_upper(0, 0)
            experts_out(0)
            with act.Fori(1, PEER_NK // 8 - 1) as i:
                experts_out(i)
            experts_out(PEER_NK // 8 - 1, True)
            for t in range(NT):
                act.wait_ge(x2_done, t + 1)
                act.activation(sq_last[:, :], x_nat[:, t, :], ACT.Square, accum_out=stat[:, t:t + 1]).then_inc(fsq, 1)
                act.wait_ge(fms, t + 1)
                act.activation(stat[:, 4 + t:5 + t], stat[:, 2 + t:3 + t], ACT.Sqrt).then_inc(frs, 1)

        @block.tensor
        def _(pe):
            def unit(n, k4, par, xh, xl, kc0, first, last, free, half=None):
                s = k4 % SPLIT
                if half in (None, 0):
                    pe.wait_ge(hi_done, n + 1)
                    pe.wait_ge(lo_done, n + 1)
                    if first and free is not None:
                        pe.wait_ge(*free)
                cs = range(CU) if half is None else range(half * 2, half * 2 + 2)
                for c in cs:
                    rh, rl = w_hi[:, s, c * NB:(c + 1) * NB], w_lo[:, s, c * NB:(c + 1) * NB]
                    for t in range(NT):
                        ts = slice(t * P, (t + 1) * P)
                        out = psum[:, 2 * par + t, :]
                        st, en = first and c == 0, last and c == CU - 1
                        pe.matmul(out, xh[:, kc0 + c, ts], rh, start=st, stop=False, skip_group_check=True)
                        pe.matmul(out, xh[:, kc0 + c, ts], rl, start=False, stop=False, skip_group_check=True)
                        ins = pe.matmul(out, xl[:, kc0 + c, ts], rh, start=False, stop=en, skip_group_check=True)
                if half in (None, 1):
                    ins.then_inc(unit_done, 1)

            def proj_unit(n, k, par, b, half=None):
                free = None if isinstance(b, int) and b < 2 else (evac_done, b * 2 - 2)
                unit(n, k, par, hT_hi, hT_lo, 4 * k, k == 0, k == UPB - 1, free, half)

            for k in range(UPB):
                pe.wait_ge(h_hi, k + 1)
                pe.wait_ge(h_lo, k + 1)
                proj_unit(k, k, 0, 0)
            pe.wait_ge(small_in, 16)
            for t in range(NT):
                for c in range(KC):
                    ins = pe.matmul(psum[:, 4, t * 64:(t + 1) * 64], xgT[:, c, t * P:(t + 1) * P], w_small[:, c, :],
                                    start=c == 0, stop=c == KC - 1, skip_group_check=True)
            ins.then_inc(small_done, 1)
            for k in range(UPB):
                proj_unit(UPB + k, k, 1, 1)

            def prep_part(k):
                if k == 0:
                    pe.wait_ge(small_out, 4)
                    pe.wait_ge(const_in, 96)
                    for t in range(NT):
                        ins = pe.transpose(psum[0:GLA_LR, 4, t * P:(t + 1) * P], glr[:, t, :], ident[:, :])
                    ins.then_inc(pe_prep, 1)
                if k == 1:
                    pe.wait_ge(act_prep, 1)
                    pe.wait_ge(prep_in, 64)
                    for h in range(GLA_H):
                        ins = pe.matmul(psum[:, 4 + h // 2, (h % 2) * S:(h % 2 + 1) * S], w_decay[:, h * GLA_DK:(h + 1) * GLA_DK], glrT[:, :],
                                        start=True, stop=True, skip_group_check=True)
                    ins.then_inc(pe_prep, 1)
                if k in (3, 4):
                    a = k - 3
                    pe.wait_ge(dve_prep, 10)
                    for g in range(NSA_G):
                        for t in range(NT):
                            ins = pe.transpose(psum[:, 4 + 2 * a + g // 2, (g % 2) * S + t * P:(g % 2) * S + (t + 1) * P],
                                               kv_c[:, a, t, g * DH:(g + 1) * DH], ident[:, :])
                    ins.then_inc(pe_prep, 1)
                if k in (5, 6):
                    a = k - 5
                    pe.wait_ge(dve_prep, 11)
                    for q in range(4):
                        n = a * 4 + q
                        pe.wait_ge(w1_in[n % W1_SLOTS], 16 * (n // W1_SLOTS + 1))
                        for i in range(CMP_BLOCK // 4):
                            c = q * (CMP_BLOCK // 4) + i
                            ins = pe.matmul(psum[:, 4 + a, 0:NSA_G * NCMP], w1[:, n % W1_SLOTS, i, :], blk_c[:, a, c, :, :].rearrange("p g n -> p (g n)"),
                                            start=c == 0, stop=c == CMP_BLOCK - 1, skip_group_check=True)
                        ins.then_inc(w1_used, 1)
                if k == 7:
                    pe.wait_ge(act_prep, 6)
                    pe.matmul(psum[:, 6, 0:NSA_G * NCMP], w2[:, 0, :], hid_c[:, 0, :], start=True, stop=True, skip_group_check=True)
                    for g in range(NSA_G):
                        ins = pe.matmul(psum[0:NCMP, 7, g * DH:(g + 1) * DH], hid_c[:, 1, g * NCMP:(g + 1) * NCMP], w2[:, 1, :],
                                        start=True, stop=True, skip_group_check=True)
                    ins.then_inc(pe_prep, 1)

            for k in range(2 * UPB):
                proj_unit((2 * UPB + k), k % UPB, k // UPB, 2 + k // UPB)
                prep_part(k)
            with pe.Fori(2, A_BLOCKS // 2) as i:
                for par in range(2):
                    for k in range(UPB):
                        proj_unit(i * 8 + (par * 4 + k), k, par, i * 2 + par)

            def gla_part(h, k, half):
                if (k, half) == (0, 1):
                    pe.wait_ge(g_in, h * 32 + 32)
                    pe.wait_ge(g_yhi, h)
                    pe.wait_ge(g_ylo, h)
                    for a in range(2):
                        for t in range(NT):
                            ins = pe.transpose(psum[:, 4, a * S + t * P:a * S + (t + 1) * P], qk_g[:, a, t, :], ident[:, :])
                    ins.then_inc(g_qkt, 1)
                if (k, half) in ((1, 1), (2, 0)):
                    t = k - 1
                    if t == 0:
                        pe.wait_ge(g_ql, h + 1)
                        pe.wait_ge(g_kl, h + 1)
                        pe.wait_ge(g_att, h * 2)
                    else:
                        pe.wait_ge(g_att, h * 2 + 1)
                    ts = slice(t * P, (t + 1) * P)
                    for n, lev in enumerate([*range(len(LEVELS)), LDIAG]):
                        ins = pe.matmul(psum[:, 5 + n // 4, (n % 4) * P:(n % 4 + 1) * P], kL[:, lev, ts], qL[:, lev, ts],
                                        start=True, stop=True, skip_group_check=True)
                    if t == 0:
                        ins = pe.matmul(psum[:, 4, 0:P], kL[:, L128, 0:P], qL[:, L128, P:S], start=True, stop=True, skip_group_check=True)
                    ins.then_inc(g_lev, 1)
                if (k, half) == (2, 1):
                    pe.wait_ge(g_vr_in, h * 32 + 32)
                    pe.wait_ge(g_att, h * 2 + 2)
                    pe.wait_ge(g_a01, h + 1)
                    pe.matmul(psum[:, 7, 0:GLA_DV], att_T[:, 0, :], v_g[:, 0, :], start=True, stop=True, skip_group_check=True)
                    pe.matmul(psum[:, 7, GLA_DV:2 * GLA_DV], att_T[:, 2, :], v_g[:, 0, :], start=True, stop=False, skip_group_check=True)
                    pe.matmul(psum[:, 7, GLA_DV:2 * GLA_DV], att_T[:, 1, :], v_g[:, 1, :], start=False, stop=True,
                              skip_group_check=True).then_inc(g_o, 1)
                if (k, half) == (3, 1):
                    pe.wait_ge(g_y, h + 1)
                    for c in range(2):
                        for t in range(NT):
                            ins = pe.transpose(psum[:, 4, c * S + t * P:c * S + (t + 1) * P], y_g[:, t, c * P:(c + 1) * P], ident[:, :])
                    ins.then_inc(g_yt, 1)

            pe.wait_ge(act_prep, 8)
            base = A_BLOCKS * UPB
            with pe.Fori(0, GLA_H // 2) as i:
                for hp in range(2):
                    for k in range(UPB):
                        for half in range(2):
                            proj_unit(i * 8 + (base + hp * 4 + k), k, hp, i * 2 + (A_BLOCKS + hp), half)
                            gla_part(i * 2 + hp, k, half)

            def scores(g, j):
                h = g * NSA_HPG + j
                pe.wait_ge(mx_done, h)
                if j == 0:
                    pe.wait_ge(qkt_a, g * 2 + 2)
                    pe.wait_ge(qkt_v, g + 1)
                for t in range(NT):
                    q = qkT[:, j, t * P:(t + 1) * P]
                    n = (t + 1) * P
                    for b in range(2):
                        pe.matmul(psum[:, 4 + t, b * n:(b + 1) * n], q, qkT[:, NSA_HPG + b, 0:n], start=True, stop=True, skip_group_check=True)
                    ins = pe.matmul(psum[:, 4, S + t * 16:S + t * 16 + NCMP], q, kcT[:, ds(g * NCMP, NCMP)], start=True, stop=True, skip_group_check=True)
                ins.then_inc(s_done, 1)

            def turn(g, j):
                h = g * NSA_HPG + j
                q = j % 2
                pe.wait_ge(p_done, h + 1)
                pe.wait_ge(o_hi, h)
                pe.wait_ge(o_lo, h)
                pe.wait_ge(pt_a, h * 2)
                pe.wait_ge(pt_v, h)
                for b in range(2):
                    pe.transpose(psum[:, 6, b * P:(b + 1) * P], sm[:, q, b * P:(b + 1) * P], ident[:, :])
                for t in range(NT):
                    pe.transpose(psum[0:NCMP, 6, S + t * P:S + (t + 1) * P], smc[:, q, t, :], ident[:, :])
                for b in range(2):
                    for kt in range(2):
                        o = (kt * 2 + b) * P
                        ins = pe.transpose(psum[:, 7, o:o + P], sm[:, q, 2 * P + b * S + kt * P:2 * P + b * S + (kt + 1) * P], ident[:, :])
                ins.then_inc(pt_done, 1)

            def values(g, j):
                h = g * NSA_HPG + j
                pe.wait_ge(pt_a, h * 2 + 2)
                pe.wait_ge(pt_v, h + 1)
                if j == 0:
                    pe.wait_ge(nv_in, g * 32 + 32)
                    pe.wait_ge(vcn_done, g + 1)
                out = psum[:, 6, S:2 * S]
                pe.matmul(out, v_n[:, 0, 0, :], pT[:, 0, :], start=True, stop=False, skip_group_check=True)
                pe.matmul(out, v_n[:, 1, 0, :], pT[:, 1, :], start=False, stop=False, skip_group_check=True)
                pe.matmul(out, vc_n[:, :], pcT[:, :], start=False, stop=False, skip_group_check=True)
                out = psum[:, 6, S + P:2 * S]
                pe.matmul(out, v_n[:, 0, 1, :], pT[:, 2, P:S], start=False, stop=False, skip_group_check=True)
                pe.matmul(out, v_n[:, 1, 1, :], pT[:, 3, P:S], start=False, stop=True, skip_group_check=True).then_inc(pv_done, 1)

            pe.wait_ge(g_yhi, GLA_H)
            pe.wait_ge(g_ylo, GLA_H)
            base = (A_BLOCKS + 4) * UPB
            with pe.Fori(0, NSA_G) as g:
                for k in range(8):
                    proj_unit(g * 8 + (base + k), k % 4, k // 4, g * 2 + (A_BLOCKS + 4 + k // 4))
                    if k == 1:
                        pe.wait_ge(roped, g + 1)
                        pe.wait_ge(mx_done, g * NSA_HPG)
                        pe.wait_ge(o_hi, g * NSA_HPG)
                        pe.wait_ge(o_lo, g * NSA_HPG)
                        for a in range(NSA_HPG + 2):
                            for t in range(NT):
                                ins = pe.transpose(psum[:, 4 + a // 2, (a % 2) * S + t * P:(a % 2) * S + (t + 1) * P], qk_n[:, t, a, :], ident[:, :])
                        ins.then_inc(qkt_done, 1)
                    if 0 <= k - 4 < NSA_HPG:
                        values(g, k - 4)
                    if 0 <= k - 2 < NSA_HPG:
                        scores(g, k - 2)
                    if 0 <= k - 3 < NSA_HPG:
                        turn(g, k - 3)

            def turn_block(src, ins_done, done):
                pe.wait_ge(*ins_done)
                for c in range(4):
                    for t in range(NT):
                        ins = pe.transpose(psum[:, 4 + c // 2, (c % 2) * S + t * P:(c % 2) * S + (t + 1) * P], src[:, t, c * P:(c + 1) * P], ident[:, :])
                ins.then_inc(done, 1)

            def turn_merged(nb):
                pe.wait_ge(m_hi, nb)
                pe.wait_ge(m_lo, nb)
                turn_block(mrg[:, 1, :, :], (m_done, nb * 2 + 2), mt_done)

            def turn_x(b):
                pe.wait_ge(x_hi, b)
                pe.wait_ge(x_lo, b)
                turn_block(mrg[:, 1, :, :], (xg2_done, b + 1), xt_done)

            base = PROJ_BLOCKS * UPB
            pe.wait_ge(o_hi, NSA_H)
            pe.wait_ge(o_lo, NSA_H)
            pe.wait_ge(evac_done, 2 * PROJ_BLOCKS)
            with pe.Fori(0, 2) as i:
                for nbp in range(2):
                    nb = i * 2 + nbp
                    for k in range(UPG):
                        if nbp == 1 and k == 1:
                            turn_merged(nb - 1)
                        unit(i * 12 + (base + nbp * 6 + k), nbp * 6 + k, 0, ygT_hi, ygT_lo, 4 * k, k == 0, k == UPG - 1, (m_done, nb * 2))
                    for k in range(UPB):
                        unit(i * 12 + (base + nbp * 6 + UPG + k), nbp * 6 + UPG + k, 1, ynT_hi, ynT_lo, 4 * k, k == 0, k == UPB - 1, (m_done, nb * 2))
                turn_merged(nb)

            base = PROJ_BLOCKS * UPB + 4 * (UPG + UPB)
            pe.wait_ge(m_hi, 4)
            pe.wait_ge(m_lo, 4)
            with pe.Fori(0, 2) as i:
                for par in range(2):
                    b = i * 2 + par
                    for k in range(UPB):
                        if par == 1 and k == 1:
                            turn_x(b - 1)
                        unit(i * 8 + (base + par * 4 + k), k, par, mT_hi, mT_lo, 4 * k, k == 0, k == UPB - 1, (x1_done, b))
                turn_x(b)

            base = PROJ_BLOCKS * UPB + 4 * (UPG + UPB) + 4 * UPB

            def query_unit(par, k):
                n = base + par * UPB + k
                pe.wait_ge(hi_done, n + 1)
                pe.wait_ge(lo_done, n + 1)
                for c in range(CU):
                    kc = CU * k + c
                    for h in range(4):
                        wh, wl = w_hi[:, n % SPLIT, c * NB + h * P:c * NB + (h + 1) * P], w_lo[:, n % SPLIT, c * NB + h * P:c * NB + (h + 1) * P]
                        out = psum[:, 2 * par + h // 2, (h % 2) * S:(h % 2 + 1) * S]
                        pe.matmul(out, wh, h2T_hi[:, kc, :], start=kc == 0 and h % 2 == 0, stop=False, skip_group_check=True)
                        pe.matmul(out, wl, h2T_hi[:, kc, :], start=False, stop=False, skip_group_check=True)
                        ins = pe.matmul(out, wh, h2T_lo[:, kc, :], start=False, stop=kc == KC - 1, skip_group_check=True)
                ins.then_inc(unit_done, 1)

            def query_scores(par):
                pe.wait_ge(qpt_out, par + 1)
                pe.wait_ge(keys_in, 16)
                if par:
                    pe.wait_ge(sc_out, 2)
                for t in range(NT):
                    for h in range(4):
                        ins = pe.matmul(psum[:, 4 + 2 * t + h // 2, (h % 2) * S:(h % 2 + 1) * S], qpT[:, 4 * par + h, t * P:(t + 1) * P],
                                        keys[:, 4 * par + h, :], start=True, stop=True, skip_group_check=True)
                ins.then_inc(sc_done, 1)

            pe.wait_ge(x_hi, 4)
            pe.wait_ge(x_lo, 4)
            pe.wait_ge(x1_done, 4)
            for par in range(2):
                for k in range(UPB):
                    query_unit(par, k)
                    if (par, k) == (1, 0):
                        query_scores(0)
                    if (par, k) == (1, 1):
                        pe.wait_ge(rsd_done, 2)
                        for t in range(NT):
                            ins = pe.matmul(psum[:, 0, t * P:(t + 1) * P], ones[:, :], rs_diag[:, t, :], start=True, stop=True, skip_group_check=True)
                        ins.then_inc(rs_row_done, 1)
            query_scores(1)

            def hidden(i, table):
                for k in range(8):
                    n = i * 8 + (U0 + k)
                    m = i * 4 + k // 2
                    pe.wait_ge(hi_done, n + 1)
                    pe.wait_ge(lo_done, n + 1)
                    if k % 2 == 0 and not (isinstance(i, int) and i == 0):
                        pe.wait_ge(hid_scaled, m - 3)
                    s, out = k % SPLIT, psum[:, k // 2, (k % 2) * S:(k % 2 + 1) * S]
                    for c in range(KC):
                        uh, ul = w_hi[:, s, c * P:(c + 1) * P], w_lo[:, s, c * P:(c + 1) * P]
                        pe.matmul(out, uh, h2T_hi[:, c, :], start=c == 0, stop=False, skip_group_check=True)
                        pe.matmul(out, ul, h2T_hi[:, c, :], start=False, stop=False, skip_group_check=True)
                        ins = pe.matmul(out, uh, h2T_lo[:, c, :], start=False, stop=c == KC - 1, skip_group_check=True)
                    ins.then_inc(unit_done, 1)
                    if k == 5 and table:
                        table(i - PEER_H, 0, None if isinstance(i, int) else i - PEER_H)

            def turn_picks(t):
                pe.wait_ge(routed, PEER_H * (t + 1))
                if t:
                    pe.wait_ge(tab_out, PEER_H)
                for w in range(3):
                    ins = pe.transpose(psum[:, 4, w * P:(w + 1) * P], rt[:, w, t * PEER_H:(t + 1) * PEER_H, :].rearrange("p u k -> p (u k)"), ident[:, :])
                ins.then_inc(rt_turned, 1)

            def table(tb, half, prior):
                pe.wait_ge(hot1_done, tb + 1)
                pe.wait_ge(hot2_done, tb + 1)
                if isinstance(tb, int) and tb == PEER_H:
                    pe.wait_ge(rt_out, 2)
                elif prior is not None:
                    pe.wait_ge(tab_out, prior)
                for j in range(TB):
                    bank = (4 if half == 0 else 0) + j // 4
                    ins = pe.matmul(psum[:, bank, (j % 4) * P:(j % 4 + 1) * P], hots[half][0][:, j, :], hots[half][1][:, j, :], start=True, stop=True, skip_group_check=True)
                ins.then_inc(tab_done, 1)

            pe.wait_ge(rs_row_out, 1)
            hidden(0, None)
            with pe.Fori(1, PEER_H) as i:
                hidden(i, None)
            turn_picks(0)
            pe.wait_ge(rt_out, 1)
            hidden(PEER_H, table)
            with pe.Fori(PEER_H + 1, 2 * PEER_H) as i:
                hidden(i, table)
            turn_picks(1)
            pe.wait_ge(hid_scaled, PEER_NK // 2)
            for half in range(2):
                table(PEER_H + half, half, None)
            with pe.Fori(PEER_H // 2 + 1, PEER_H) as j:
                for half in range(2):
                    table(j * 2 + half, half, j * 2 + (half - 1))

            def experts(i):
                for k in range(8):
                    n = i * 8 + (V0 + k)
                    pe.wait_ge(hi_done, n + 1)
                    pe.wait_ge(lo_done, n + 1)
                    if k % VB == 0:
                        pe.wait_ge(wlow_done, i * 2 + (k // VB + 1))
                    s = k % SPLIT
                    for t in range(NT):
                        wh, wl = w_up[:, k // VB, k % VB, t * P:(t + 1) * P], w_low[:, k // VB, k % VB, t * P:(t + 1) * P]
                        for q in range(4):
                            vh, vl = w_hi[:, s, q * NB:(q + 1) * NB], w_lo[:, s, q * NB:(q + 1) * NB]
                            out = psum[:, 4 * t + q, :]
                            pe.matmul(out, wh, vh, start=False, stop=False, skip_group_check=True)
                            pe.matmul(out, wh, vl, start=False, stop=False, skip_group_check=True)
                            ins = pe.matmul(out, wl, vh, start=False, stop=False, skip_group_check=True)
                    ins.then_inc(unit_done, 1)

            pe.wait_ge(zero_done, 1)
            pe.wait_ge(tab_out, S // TB)
            for q in range(8):
                pe.matmul(psum[:, q, :], zeros[:, :], zeros[:, None, :].to_broadcast([P, 4, P]), start=True, stop=False, skip_group_check=True)
            experts(0)
            with pe.Fori(1, PEER_NK // 8) as i:
                experts(i)

        @block.vector
        def _(dve):
            step = Steps(dve, v_step)

            def lo(n, s):
                dve.wait_ge(hi_done, n + 1)
                wait = n - (SPLIT - 1)
                if not (isinstance(wait, int) and wait <= 0):
                    dve.wait_ge(unit_done, wait)
                dve.tensor_tensor(w_lo[:, s % SPLIT, :], w_raw[:, s % RAW, :], w_hi[:, s % SPLIT, :].bitcast(F32), ALU.subtract).then_inc(lo_done, 1)

            def lower(dst, src, up, n, s, value):
                dve.wait_ge(s, value)
                return dve.tensor_tensor(dst, src, up.bitcast(F32), ALU.subtract)

            def rope(x, rot, n):
                cs = cos_t[:, :, None, :].to_broadcast([P, NT, n, HALF])
                sn = sin_t[:, :, None, :].to_broadcast([P, NT, n, HALF])
                x1, x2 = x[:, :, 0:n, 0:HALF], x[:, :, 0:n, HALF:ROT]
                dve.tensor_tensor(rot[:, 0], x1, cs, ALU.mult)
                dve.tensor_tensor(rot[:, 1], x2, sn, ALU.mult)
                dve.tensor_tensor(rot[:, 2], x2, cs, ALU.mult)
                step(dve.tensor_tensor(rot[:, 3], x1, sn, ALU.mult))
                dve.tensor_tensor(x1, rot[:, 0], rot[:, 1], ALU.subtract)
                return dve.tensor_tensor(x2, rot[:, 2], rot[:, 3], ALU.add)

            def refine(r, v, n=NT):
                t = newton[:, 0:n]
                step(dve.tensor_tensor(t, r, r, ALU.mult))
                step(dve.tensor_tensor(t, t, v, ALU.mult))
                step(dve.tensor_scalar(t, t, -0.5, 1.5, ALU.mult, ALU.add))
                return dve.tensor_tensor(r, r, t, ALU.mult)

            dve.memset(stat[:, 12:13], EPS)
            dve.wait_ge(const_in, 96)
            for q in range(4):
                c = slice(4 * q, 4 * q + 4)
                dve.wait_ge(xT_in[q], 16)
                dve.tensor_tensor(xgT[:, c, :], xgT[:, c, :], g1[:, c, None].to_broadcast([P, 4, S]), ALU.mult).then_inc(xg_done, 1)
                dve.wait_ge(h_hi, q + 1)
                dve.tensor_tensor(hT_lo[:, c, :], xgT[:, c, :], hT_hi[:, c, :].bitcast(F32), ALU.subtract).then_inc(h_lo, 1)
                if q < AHEAD:
                    lo(q, q)
            lo(AHEAD, AHEAD)
            lo(AHEAD + 1, AHEAD + 1)
            dve.wait_ge(ssq1, 2)
            dve.tensor_scalar(stat[:, 2:4], stat[:, 0:2], 1.0 / D, EPS, ALU.mult, ALU.add).then_inc(ms1_done, 1)
            step(dve.tensor_copy(pos_f[:, :], pos_i[:, :]))
            for t in range(NT):
                ins = dve.tensor_scalar(ang[:, t, :], inv_f[:, :], pos_f[:, t:t + 1], None, ALU.mult)
            step(ins)
            step(dve.tensor_scalar(turns[:, :, :], ang[:, :, :], float(1 / (2 * np.pi)), None, ALU.mult))
            step(dve.tensor_scalar(turns[:, :, :], turns[:, :, :], ROUND, None, ALU.add))
            step(dve.tensor_scalar(turns[:, :, :], turns[:, :, :], ROUND, None, ALU.subtract))
            for part in TWO_PI:
                step(dve.scalar_tensor_tensor(ang[:, :, :], turns[:, :, :], -part, ang[:, :, :], ALU.mult, ALU.add))
            dve.tensor_scalar(ang[:, :, :], ang[:, :, :], 3.1415925, -3.1415925, ALU.min, ALU.max).then_inc(ang_ready, 1)
            lo(AHEAD + 2, AHEAD + 2)
            dve.wait_ge(sq1_done, 1)
            step(dve.reciprocal(rstd1[:, :], stat[:, 4:6]))
            refine(rstd1[:, :], stat[:, 2:4]).then_inc(rs1_done, 1)
            lo(AHEAD + 3, AHEAD + 3)
            dve.wait_ge(trig_done, 2)
            step(dve.tensor_tensor(cos_t[:, :, :], turns[:, :, :], turns[:, :, :], ALU.mult))
            step(dve.tensor_scalar(cos_t[:, :, :], cos_t[:, :, :], -2.0, 1.0, ALU.mult, ALU.add))
            for k in range(UPB):
                lo(UPB + k + AHEAD, k + AHEAD)
            for k in range(2 * UPB):
                lo(2 * UPB + k + AHEAD, k + AHEAD)
                if k == 1:
                    dve.memset(bT[:, GLA_H, :], 0.0)
                    dve.wait_ge(pe_prep, 2)
                    dve.wait_ge(prep_in, 64)
                    for h in range(GLA_H):
                        dve.tensor_scalar(zT[:, h * S:(h + 1) * S], psum[:, 4 + h // 2, (h % 2) * S:(h % 2 + 1) * S], b_decay[:, h:h + 1], None,
                                          ALU.add).then_inc(dve_prep, 1)
                    dve.wait_ge(act_prep, 2)
                    dve.scalar_tensor_tensor(zT, zT, 0.0, zA, ALU.min, ALU.subtract).then_inc(dve_prep, 1)
                    dve.wait_ge(dve_prep, 5)
                    for h in range(GLA_H):
                        dve.tensor_tensor_scan(bT[:, h, :], zT[:, h * S:(h + 1) * S], zT[:, h * S:(h + 1) * S], 0.0, ALU.add, ALU.bypass).then_inc(dve_prep, 1)
                if k == 2:
                    dve.wait_ge(kvc_in, 32)
                    rope(kv_c[:, 0, :, :].rearrange("p t (g d) -> p t g d", d=DH), rot_c, NSA_G).then_inc(dve_prep, 1)
                if k == 4:
                    dve.wait_ge(act_prep, 4)
                    for a in range(2):
                        for half in range(CMP_BLOCK // CMP_STRIDE):
                            o = half * CMP_STRIDE
                            ins = dve.tensor_tensor(blk_c[:, a, o:o + CMP_STRIDE, :, :],
                                                    kvT_c[:, a, :, o:o + NCMP * CMP_STRIDE].rearrange("p g (n b) -> p b g n", b=CMP_STRIDE),
                                                    posT[:, a, o:o + CMP_STRIDE, None, None].to_broadcast([P, CMP_STRIDE, NSA_G, NCMP]), ALU.add)
                    ins.then_inc(dve_prep, 1)
            with dve.Fori(2, A_BLOCKS // 2) as i:
                for k in range(2 * UPB):
                    lo(i * 8 + (k + AHEAD), k + AHEAD)

            def gla_slot(h, k):
                if k == 0:
                    dve.wait_ge(g_exp, h + 1)
                    dve.wait_ge(g_qe, h + 1)
                    dve.tensor_copy(kT_g[:, :], psum[:, 4, S:2 * S]).then_inc(g_ke, 1)
                    dve.wait_ge(g_ke, h + 1)
                    rest = NL - KL_POOL
                    dve.tensor_tensor(kL[:, KL_POOL:NL, :], dec[:, KL_POOL:NL, :], kT_g[:, None, :].to_broadcast([P, rest, S]), ALU.mult)
                    dve.tensor_tensor(qL[:, :, :], dec[:, :, :], qT_g[:, None, :].to_broadcast([P, NL, S]), ALU.mult).then_inc(g_ql, 1)
                if k in (1, 2):
                    t = k - 1
                    dve.wait_ge(g_lev, h * 2 + (t + 1))
                    step(dve.tensor_tensor(att_m[:, :, :], psum[:, 5:7, :].rearrange("p b (l t) -> p (b l) t", t=P), masks[:, :, :], ALU.mult))
                    dve.tensor_reduce(att_T[:, t, :], att_m[:, :, :].rearrange("p l t -> p t l"), AX.X, ALU.add).then_inc(g_att, 1)
                    dve.wait_ge(g_att, h * 2 + (t + 1))
                    if t == 0:
                        dve.tensor_copy(att_T[:, 2, :], psum[:, 4, 0:P]).then_inc(g_a01, 1)
            def gla_output(h):
                dve.wait_ge(g_rn, h + 1)
                step(dve.tensor_scalar(gst[:, 6:8], gst[:, 0:2], 1.0 / GLA_DV, EPS, ALU.mult, ALU.add))
                step(dve.reciprocal(gst[:, 4:6], gst[:, 2:4]))
                step(refine(gst[:, 4:6], gst[:, 6:8]))
                for t in range(NT):
                    ins = dve.scalar_tensor_tensor(y_g[:, t, :], psum[:, 7, t * GLA_DV:(t + 1) * GLA_DV], gst[:, 4 + t:5 + t], gnorm[:, :], ALU.mult, ALU.mult)
                step(ins)
                dve.wait_ge(g_silu, h + 1)
                dve.tensor_tensor(y_g[:, :, :], y_g[:, :, :], sig_g[:, :, :], ALU.mult).then_inc(g_y, 1)

            def gla_lower(h):
                up = ygT_hi[:, ds(h * 2, 2), :].rearrange("p c t -> p (c t)")
                dve.wait_ge(g_yhi, h + 1)
                dve.tensor_tensor(ygT_lo[:, ds(h * 2, 2), :].rearrange("p c t -> p (c t)"), psum[:, 4, :], up.bitcast(F32), ALU.subtract).then_inc(g_ylo, 1)

            dve.wait_ge(g_msk, 32)
            dve.memset(dec[:, LDIAG, :], 1.0).then_inc(g_one, 1)
            base = A_BLOCKS * UPB
            with dve.Fori(0, GLA_H // 2) as i:
                step.enter(i, 0, 2 * 9)
                for hp in range(2):
                    for k in range(UPB):
                        if k == 3:
                            gla_output(i * 2 + hp)
                        lo(i * 8 + (base + hp * 4 + k + AHEAD), k + AHEAD)
                        gla_slot(i * 2 + hp, k)
                    gla_lower(i * 2 + hp)
                step.leave(GLA_H // 2)

            def scores_max(h, j):
                q = j % 2
                wait_alone(dve, s_done, h + 1)
                for t in range(NT):
                    n = (t + 1) * P
                    for b in range(2):
                        o = 2 * P * t + b * n
                        dve.tensor_tensor_reduce(sm[:, q, o:o + n], psum[:, 4 + t, b * n:(b + 1) * n], tri[:, S - n:S], 1.0, -3e38,
                                                 ALU.add, ALU.max, mx[:, q, t, b + 1:b + 2])
                    ins = dve.tensor_tensor_reduce(smc[:, q, t, :], psum[:, 4, S + 16 * t:S + 16 * t + NCMP], cmask[:, t, :], 1.0, -3e38,
                                                   ALU.add, ALU.max, mx[:, q, t, 0:1])
                step(ins)
                dve.tensor_scalar(nmx[:, q, :, :], mx[:, q, :, :], MASKED_MAX, -SCALE, ALU.max, ALU.mult).then_inc(mx_done, 1)

            def probs(h, j):
                q = j % 2
                dve.wait_ge(exp_done, h * 6 + 6)
                step(dve.tensor_scalar(wts[:, q, :, :], sums[:, q, :, :], 1e-30, None, ALU.max))
                step(dve.reciprocal(wts[:, q, :, :], wts[:, q, :, :]))
                step(dve.tensor_tensor(wts[:, q, :, :], wts[:, q, :, :], g_n[:, :, 3 * j:3 * j + 3], ALU.mult))
                for t in range(NT):
                    for b in range(3):
                        n = (t + 1) * P
                        o = 2 * P * t + b * n
                        w = (b + 1) % 3
                        x = smc[:, q, t, :] if b == 2 else sm[:, q, o:o + n]
                        ins = dve.tensor_scalar(x, x, wts[:, q, t, w:w + 1], None, ALU.mult)
                ins.then_inc(p_done, 1)

            base = (A_BLOCKS + 4) * UPB
            with dve.Fori(0, NSA_G) as g:
                step.enter(g, 0, 2 + 4 * 4)
                for k in range(8):
                    if 0 <= k - 3 < NSA_HPG:
                        probs(g * NSA_HPG + (k - 3), k - 3)
                    lo(g * 8 + (base + k + AHEAD), k + AHEAD)
                    if k == 0:
                        step(dve.tensor_copy(g_n[:, :, :], gates[:, :, ds(g * 3 * NSA_HPG, 3 * NSA_HPG)]))
                        dve.wait_ge(nqk_in, g * 48 + 48)
                        rope(qk_n, rot_n, NSA_HPG + 2).then_inc(roped, 1)
                    if k == 1:
                        dve.wait_ge(qkt_done, g + 1)
                        dve.tensor_copy(qkT[:, 4:6, :].rearrange("p h t -> p (h t)"), psum[:, 6, :]).then_inc(qkt_v, 1)
                    if 0 <= k - 4 < NSA_HPG:
                        h = g * NSA_HPG + (k - 4)
                        up = ynT_hi[:, ds(h, 1), :].rearrange("p a t -> p (a t)")
                        dve.wait_ge(o_hi, h + 1)
                        dve.tensor_tensor(ynT_lo[:, ds(h, 1), :].rearrange("p a t -> p (a t)"), psum[:, 6, S:2 * S], up.bitcast(F32), ALU.subtract).then_inc(o_lo, 1)
                    if 0 <= k - 2 < NSA_HPG:
                        scores_max(g * NSA_HPG + (k - 2), k - 2)
                    if 0 <= k - 3 < NSA_HPG:
                        dve.wait_ge(pt_done, g * NSA_HPG + (k - 3) + 1)
                        dve.tensor_copy(pT[:, :, P:S], psum[:, 7, :].rearrange("p (a t) -> p a t", t=P)).then_inc(pt_v, 1)
                step.leave(NSA_G)

            def merged_lower(nb):
                dve.wait_ge(m_hi, nb + 1)
                dve.tensor_tensor(mT_lo[:, ds(nb * 4, 4), :].rearrange("p c t -> p (c t)"), psum[:, 4:6, :].rearrange("p b n -> p (b n)"),
                                  mT_hi[:, ds(nb * 4, 4), :].rearrange("p c t -> p (c t)").bitcast(F32), ALU.subtract).then_inc(m_lo, 1)

            def x_lower(b):
                dve.wait_ge(x_hi, b + 1)
                dve.tensor_tensor(h2T_lo[:, ds(b * 4, 4), :].rearrange("p c t -> p (c t)"), psum[:, 4:6, :].rearrange("p b n -> p (b n)"),
                                  h2T_hi[:, ds(b * 4, 4), :].rearrange("p c t -> p (c t)").bitcast(F32), ALU.subtract).then_inc(x_lo, 1)

            base = PROJ_BLOCKS * UPB
            dve.wait_ge(stored[0], 16 * PROJ_BLOCKS // 2)
            dve.wait_ge(stored[1], 16 * PROJ_BLOCKS // 2)
            with dve.Fori(0, 2) as i:
                step.enter(i, 0, 2)
                for nbp in range(2):
                    nb = i * 2 + nbp
                    for k in range(6):
                        n = i * 12 + (base + nbp * 6 + k + 1)
                        lo(i * 12 + (base + nbp * 6 + k + AHEAD), nbp * 6 + k + AHEAD)
                        if (nbp, k) == (1, 0):
                            merged_lower(nb - 1)
                        if k == UPG - 1:
                            dve.wait_ge(gab_sig, nb + 1)
                            dve.wait_ge(unit_done, n)
                            dve.tensor_tensor(mrg[:, 0, :, :], psum[:, 0:2, :], gab[:, 0, :, :], ALU.mult).then_inc(m_done, 1)
                    dve.wait_ge(unit_done, n)
                    step(dve.tensor_tensor(mrg[:, 1, :, :], psum[:, 2:4, :], gab[:, 1, :, :], ALU.mult))
                    dve.tensor_tensor(mrg[:, 1, :, :], mrg[:, 1, :, :], mrg[:, 0, :, :], ALU.add).then_inc(m_done, 1)
                merged_lower(nb)
                step.leave(2)

            base = PROJ_BLOCKS * UPB + 4 * (UPG + UPB)
            dve.wait_ge(xn_in, 32)
            dve.wait_ge(g2_in, 16)
            with dve.Fori(0, 2) as i:
                for par in range(2):
                    b = i * 2 + par
                    for k in range(UPB):
                        n = i * 8 + (base + par * 4 + k + 1)
                        lo(i * 8 + (base + par * 4 + k + AHEAD), k + AHEAD)
                        if (par, k) == (1, 0):
                            x_lower(b - 1)
                    dve.wait_ge(unit_done, n)
                    x = x_nat[:, :, ds(b * NB, NB)]
                    dve.tensor_tensor(x, x, psum[:, 2 * par:2 * par + 2, :], ALU.add).then_inc(x1_done, 1)
                    dve.wait_ge(x1_done, b + 1)
                    for t in range(NT):
                        ins = dve.tensor_tensor(mrg[:, 1, t, :], x_nat[:, t, ds(b * NB, NB)], g2[:, ds(b * NB, NB)], ALU.mult)
                    ins.then_inc(xg2_done, 1)
                x_lower(b)

            base = PROJ_BLOCKS * UPB + 4 * (UPG + UPB) + 4 * UPB
            dve.wait_ge(sq2, 8)
            step(dve.tensor_reduce(stat[:, 6:8], sq_x1[:, :, :], AX.X, ALU.add))
            dve.tensor_scalar(stat[:, 8:10], stat[:, 6:8], 1.0 / D, EPS, ALU.mult, ALU.add).then_inc(ms2_done, 1)
            dve.memset(zeros[:, :], 0.0).then_inc(zero_done, 1)
            dve.memset(ones[:, :], 1.0).then_inc(rsd_done, 1)
            lo(base + AHEAD, AHEAD)
            dve.wait_ge(sq2_done, 1)
            step(dve.reciprocal(rstd2[:, :], stat[:, 10:12]))
            refine(rstd2[:, :], stat[:, 8:10]).then_inc(rs2_done, 1)
            dve.wait_ge(rs2_done, 1)
            for t in range(NT):
                ins = dve.tensor_scalar(rs_diag[:, t, :], ident[:, :], rstd2[:, t:t + 1], None, ALU.mult)
            ins.then_inc(rsd_done, 1)
            for n in range(base + AHEAD + 1, U0 + AHEAD - 1):
                lo(n, n % 4)
            dve.wait_ge(rs_row_done, 1)
            dve.tensor_copy(rs_row[:, :], psum[:, 0, 0:S]).then_inc(rs_row_out, 1)
            lo(U0 + AHEAD - 1, AHEAD - 1)

            ROUTE = 20
            def top16(values, cut, top, index):
                step(dve.max(top[:, 0:8], values), alone=True)
                dve.max_index(index[:, 0:8], top[:, 0:8], values)
                step(dve.match_replace(cut, top[:, 0:8], values, -3e38), alone=True)
                step(dve.max(top[:, 8:16], cut), alone=True)
                step(dve.max_index(index[:, 8:16], top[:, 8:16], cut), alone=True)

            def route(u, part):
                if part in (0, 1):
                    if part == 0:
                        step(dve.tensor_copy(s_now[:, :, :].rearrange("p a n -> p (a n)"), sc[:, ds(u, 1), :].rearrange("p a n -> p (a n)")), alone=True)
                    top16(s_now[:, part, :], s_cut[:, part, :], v_top[:, part, :], i_top[:, part, :])
                if part == 2:
                    dve.tensor_copy(if_top[:, :, :], i_top[:, :, :])
                    step(dve.tensor_tensor(cand[:, :, :], v_top[:, 0, :, None].to_broadcast([P, TOPK, TOPK]),
                                           v_top[:, 1, None, :].to_broadcast([P, TOPK, TOPK]), ALU.add), alone=True)
                    top16(cand[:, :, :].rearrange("p a b -> p (a b)"), cand_cut[:, :, :].rearrange("p a b -> p (a b)"), vals[:, :], flat[:, :])
                    dve.tensor_scalar(rst[:, 0:1], vals[:, 0:1], -1.0, None, ALU.mult).then_inc(r_vals, 1)
                if part == 3:
                    dve.tensor_scalar(ab[:, 0, :], flat[:, :], 4, None, ALU.logical_shift_right)
                    step(dve.tensor_scalar(ab[:, 1, :], flat[:, :], TOPK - 1, None, ALU.bitwise_and))
                    step(dve.tensor_copy(abf[:, :, :], ab[:, :, :]))
                    for a in range(2):
                        ins = dve.tensor_tensor(hot[:, a, :, :], abf[:, a, :, None].to_broadcast([P, TOPK, TOPK]),
                                                iota[:, None, 0:TOPK].to_broadcast([P, TOPK, TOPK]), ALU.is_equal)
                    step(ins)
                    for a in range(2):
                        ins = dve.tensor_tensor(hot[:, a, :, :], hot[:, a, :, :], if_top[:, a, None, :].to_broadcast([P, TOPK, TOPK]), ALU.mult)
                    step(ins)
                    step(dve.tensor_reduce(e12[:, :, :], hot[:, :, :, :], AX.X, ALU.add))
                    dve.tensor_copy(rt[:, 0:2, ds(u, 1), :].rearrange("p w u k -> p w (u k)"), e12[:, :, :])
                    dve.wait_ge(r_exp, u + 1)
                    step(dve.reciprocal(rst[:, 2:3], rst[:, 1:2]))
                    dve.tensor_scalar(rt[:, 2, ds(u, 1), :].rearrange("p u k -> p (u k)"), rexp[:, :], rst[:, 2:3], None, ALU.mult).then_inc(routed, 1)

            def picks_hot(tb, half, prior):
                if prior is not None:
                    dve.wait_ge(tab_done, prior)
                if prior is not None:
                    dve.wait_ge(hot2_done, tb)
                hot1, hot2 = hots[half]
                dve.tensor_copy(rt16[:, :, :], rtT[:, :, ds(tb * TB, TB)]).then_inc(rt16_done, 1)
                dve.wait_ge(rt16_done, tb + 1)
                dve.tensor_tensor(hot1[:, :, :], iota[:, None, :].to_broadcast([P, TB, PEER_NK]),
                                  rt16[:, 0, :, None].to_broadcast([P, TB, PEER_NK]), ALU.is_equal).then_inc(hot1_done, 1)
                for j in range(TB):
                    ins = dve.tensor_scalar(hot2[:, j, :], iota[:, :], rt16[:, 1, j:j + 1], rt16[:, 2, j:j + 1], ALU.is_equal, ALU.mult)
                ins.then_inc(hot2_done, 1)

            def hidden(i, table):
                for k in range(8):
                    lo(i * 8 + (U0 + k + AHEAD), k + AHEAD)
                    if k % 2 == 0:
                        route(i, k // 2)
                    else:
                        m = i * 4 + k // 2
                        dve.wait_ge(unit_done, i * 8 + (U0 + k + 1))
                        if not (isinstance(i, int) and m < 2):
                            dve.wait_ge(hid_gelu, m - 1)
                        dve.tensor_tensor(hs[:, k // 2 % 2, :].rearrange("p (a t) -> p a t", a=2), psum[:, k // 2, :].rearrange("p (a t) -> p a t", a=2),
                                          rs_row[:, None, :].to_broadcast([P, 2, S]), ALU.mult).then_inc(hid_scaled, 1)
                    if k == 3 and table:
                        picks_hot(i - PEER_H, 0, None if isinstance(i, int) else i - PEER_H)

            dve.wait_ge(iota_in, 16)
            dve.wait_ge(rs_row_out, 1)
            dve.wait_ge(sc_out, 4)
            hidden(0, False)
            with dve.Fori(1, PEER_H) as i:
                step.enter(i, 1, ROUTE)
                hidden(i, False)
                step.leave(PEER_H - 1)
            dve.wait_ge(rt_out, 1)
            hidden(PEER_H, True)
            with dve.Fori(PEER_H + 1, 2 * PEER_H) as i:
                step.enter(i, PEER_H + 1, ROUTE)
                hidden(i, True)
                step.leave(PEER_H - 1)
            dve.wait_ge(rt_out, 2)
            for half in range(2):
                picks_hot(PEER_H + half, half, PEER_H)
            with dve.Fori(PEER_H // 2 + 1, PEER_H) as j:
                for half in range(2):
                    picks_hot(j * 2 + half, half, j * 2 + (half - 1))

            def weights(m, half):
                i = (m - half) // 2 if isinstance(m, int) else None
                x = h_in[:, half, :, :]
                dve.tensor_tensor(x.rearrange("p c (b t) -> p c b t", t=TB), x.rearrange("p c (b t) -> p c b t", t=TB),
                                  g_tab[:, :, half * VB:(half + 1) * VB, :].rearrange("p b c t -> p c b t"), ALU.mult).then_inc(prod_done, 1)
                dve.wait_ge(wup_done, m + 1)
                dve.tensor_tensor(w_low[:, half, :, :], x, w_up[:, half, :, :].bitcast(F32), ALU.subtract).then_inc(wlow_done, 1)

            def experts_out(i, last=False):
                for k in range(8):
                    if not (last and k + AHEAD >= 8):
                        lo(i * 8 + (V0 + k + AHEAD), k + AHEAD)
                    if k == 0:
                        dve.wait_ge(unit_done, i * 8 + V0)
                        weights(i * 2 + 1, 1)
                    if k == 4 and not last:
                        dve.wait_ge(unit_done, i * 8 + (V0 + 4))
                        dve.wait_ge(v_in, i * 32 + 64)
                        weights(i * 2 + 2, 0)

            dve.wait_ge(v_in, 32)
            weights(0, 0)
            experts_out(0)
            with dve.Fori(1, PEER_NK // 8 - 1) as i:
                experts_out(i)
            experts_out(PEER_NK // 8 - 1, True)

            dve.wait_ge(unit_done, UNITS)
            dve.wait_ge(gf_in, 16)
            for t in range(NT):
                dve.tensor_tensor(x_nat[:, t, :], x_nat[:, t, :], psum[:, 4 * t:4 * t + 4, :].rearrange("p b n -> p (b n)"), ALU.add).then_inc(x2_done, 1)
            for t in range(NT):
                dve.wait_ge(fsq, t + 1)
                dve.tensor_scalar(stat[:, 2 + t:3 + t], stat[:, t:t + 1], 1.0 / D, EPS, ALU.mult, ALU.add).then_inc(fms, 1)
                dve.wait_ge(frs, t + 1)
                step(dve.reciprocal(stat[:, 6 + t:7 + t], stat[:, 4 + t:5 + t]))
                step(refine(stat[:, 6 + t:7 + t], stat[:, 2 + t:3 + t], 1))
                dve.scalar_tensor_tensor(out_t[:, t, :], x_nat[:, t, :], stat[:, 6 + t:7 + t], gf[:, :], ALU.mult, ALU.mult).then_inc(out_done, 1)


ROUND = float(3 << 22)
TWO_PI = (6.28125, 0.0019350051879882812, float(2 * np.pi - 6.28125 - 0.0019350051879882812))


def _gla_masks():
    s, t = np.arange(P)[:, None], np.arange(P)[None, :]
    levels = [(s // (2 * m) == t // (2 * m)) & (s % (2 * m) < m) & (t % (2 * m) >= m) for m in LEVELS]
    return np.stack([*levels, s == t], axis=1).astype(np.float32)


def _shape_constants():
    t = np.arange(S)
    tri = np.zeros((P, S), np.float32)
    tri[:, P:] = np.where(np.arange(P)[None, :] <= np.arange(P)[:, None], 0.0, MASKED)
    end = np.arange(NCMP) * CMP_STRIDE + CMP_BLOCK - 1
    cmask = np.where(end[None, :] <= t[:, None], 0.0, MASKED).astype(np.float32)
    inv = np.power(np.float32(ROPE_THETA), -(np.arange(0, ROT, 2, dtype=np.float32) / np.float32(ROT)))
    return {
        "ident": np.eye(P, dtype=np.float32), "tri": tri, "cmask": cmask.reshape(NT, P, NCMP).transpose(1, 0, 2),
        "inv_f": inv.astype(np.float32)[None, :], "gla_masks": _gla_masks(),
        "iota": np.arange(PEER_NK, dtype=np.float32)[None, :],
    }


def _blocks(w):
    k, n = w.shape
    return w.reshape(k // (CU * P), CU, P, n // NB, NB).transpose(3, 0, 2, 1, 4).reshape(n // NB, k // (CU * P), P, UW)


def _layout(a):
    w = a["w_in"][0]
    gate, gqk, glr, gr, ga = 5120, 5168, 7216, 7232, 8256
    order = np.concatenate([w[:, 2048:3072], w[:, gqk:glr], w[:, gr:ga], w[:, 3072:5120], w[:, 0:2048], w[:, ga:]], axis=1)
    u = a["peer_u"][0].reshape(PEER_NK, PEER_NK, KC, P).transpose(1, 3, 2, 0)
    v = a["peer_v"][0].reshape(PEER_NK, PEER_NK, D).transpose(1, 0, 2)
    gla, nsa = _blocks(a["w_up_gla"][0]), _blocks(a["w_up_nsa"][0])
    merge = np.concatenate([gla, nsa], axis=1)
    units = np.concatenate([x.reshape(-1, P, UW) for x in (_blocks(order), merge, _blocks(a["w_out"][0]), _blocks(a["peer_w_q"][0]), u, v)])
    small = np.concatenate([w[:, glr:gr], w[:, gate:gqk]], axis=1).reshape(KC, P, 64).transpose(1, 0, 2)
    x = a["x"][0]
    keys = np.zeros((P, PEER_H, 2 * PEER_NK), np.float32)
    keys[:PEER_DK // 2, :, :PEER_NK] = a["peer_sub_k1"][0].transpose(2, 0, 1)
    keys[PEER_DK // 2:, :, PEER_NK:] = a["peer_sub_k2"][0].transpose(2, 0, 1)
    w1 = np.stack([a["nsa_cmp_k_w1"][0], a["nsa_cmp_v_w1"][0]]).reshape(2, 4, CMP_BLOCK // 4, DH, DH)
    return {
        "x": x.reshape(NT, P, D).transpose(1, 0, 2), "xT": x.T.reshape(KC, P, S).transpose(1, 0, 2),
        "positions": a["positions"].reshape(NT, P).T, "g1": a["norm1_g"][0].reshape(KC, P).T,
        "w_small": small, "w_units": units, "w_decay": a["gla_w_decay"][0], "b_decay": a["gla_b_decay"][0].reshape(GLA_H, P).T,
        "posT": np.stack([a["nsa_cmp_pos_k"][0], a["nsa_cmp_pos_v"][0]]).transpose(2, 0, 1),
        "w1": w1.transpose(0, 1, 3, 2, 4).reshape(8, DH, CMP_BLOCK // 4, DH),
        "w2": np.stack([a["nsa_cmp_k_w2"][0], a["nsa_cmp_v_w2"][0]], axis=1),
        "gla_g": a["gla_norm_g"], "g2": a["norm2_g"], "gf": a["final_g"][None, :], "keys": keys,
    }


def kernel(**inputs):
    import concourse.bacc as bacc
    from concourse.bass_utils import run_bass_kernel_spmd as run

    nc = bacc.Bacc("TRN2", target_bir_lowering=False, num_devices=1)
    laid = {**_layout({k: np.asarray(v) for k, v in inputs.items()}), **_shape_constants()}
    arrays = {f"in_{name}": np.ascontiguousarray(a) for name, a in laid.items()}
    io = {name: nc.dram_tensor(f"in_{name}", arrays[f"in_{name}"].shape, mybir.dt.from_np(arrays[f"in_{name}"].dtype), kind="ExternalInput").ap()
          for name in laid}
    io["out"] = nc.dram_tensor("out_0", (S, D), F32, kind="ExternalOutput").ap()
    hybrid_block(nc, io)
    r = run(nc, [arrays], core_ids=[0])
    return r.results[0]["out_0"].reshape(1, S, D)
```

```python
from contextlib import ExitStack

import concourse.bass as bass
import numpy as np
from concourse import mybir

F32 = mybir.dt.float32
F32R = mybir.dt.float32r
BF16 = mybir.dt.bfloat16
I32 = mybir.dt.int32
U32 = mybir.dt.uint32
ALU = mybir.AluOpType
ACT = mybir.ActivationFunctionType
AX = mybir.AxisListType
ds = bass.ds

P = 128
D = 2048
S = 256
NT = S // P
KC = D // P
NB = 512
CU = 4
UW = CU * NB
EPS = 1e-6

GLA_H, GLA_DK, GLA_DV, GLA_LR, GLA_TAU = 4, 128, 256, 16, 16.0
NSA_G, NSA_HPG, DH = 4, 4, 128
NSA_H = NSA_G * NSA_HPG
W1_SLOTS = 6
ROT = DH // 4
HALF = ROT // 2
ROPE_THETA = 500000.0
CMP_BLOCK, CMP_STRIDE = 32, 16
NCMP = (S - CMP_BLOCK) // CMP_STRIDE + 1
PEER_H, PEER_NK, PEER_DK, TOPK = 8, 128, 128, 16
SCALE = float(DH) ** -0.5
MASKED = -1e30
MASKED_MAX = -1e29

B_KCM, B_VCM, B_GQ, B_GK, B_GV, B_GR, B_KSL, B_VSL, B_KWN, B_VWN, B_NQ, B_GA, B_GB = 0, 1, 2, 3, 4, 6, 8, 9, 10, 11, 12, 16, 20
PROJ_BLOCKS = 24
A_BLOCKS = 12
UPB = KC // CU
UPG = GLA_H * GLA_DV // P // CU
U0 = PROJ_BLOCKS * UPB + 4 * (UPG + UPB) + 4 * UPB + 2 * UPB
V0 = U0 + PEER_NK
UNITS = V0 + PEER_NK
RAW = 2
SPLIT = 4
AHEAD = SPLIT - 1

LEVELS = [64, 32, 16, 8, 4, 2, 1]
NL = len(LEVELS) + 2
FIRST = 1
KL_POOL = 5
L128, LDIAG = len(LEVELS), len(LEVELS) + 1

ROUTES = NT * PEER_H
PICKS = PEER_H * TOPK
TB = 16
U_IT = PEER_NK // 8
I_T1, I_T2, I_T3 = 4, 8, 14
VB = 4


def hybrid_block(nc, io):
    ctx = ExitStack()
    with ctx:
        def sem(name):
            return ctx.enter_context(nc.semaphore(name))

        def place(stack, name, shape, dt=F32):
            return stack.enter_context(nc.sbuf_tensor(name, shape, dt))

        KB = 1024
        buf = {}

        def region(offset, limit, *specs):
            with ExitStack() as stack:
                if offset:
                    stack.enter_context(nc.sbuf_tensor(f"below_{specs[0][0]}", [P, offset], mybir.dt.uint8))
                size = 0
                for name, shape, *dt in specs:
                    dt = dt[0] if dt else F32
                    buf[name] = stack.enter_context(nc.sbuf_tensor(name, shape, dt))
                    size += -(-int(np.prod(shape[1:])) * (2 if dt == BF16 else 4) // 32) * 32
                assert offset + size <= limit, (specs[0][0], offset + size, limit)

        AT_W, AT_EVAC, AT_MIX, AT_YN, AT_NSA, AT_X, END = (n * KB - 192 for n in (1, 81, 89, 130, 162, 192, 208))
        nlev = len(LEVELS) + 1
        region(0, AT_W, ("ident", [P, P]), ("rstd1", [P, NT]), ("rstd2", [P, NT]), ("stat", [P, 16]), ("newton", [P, NT]), ("sq_x1", [P, NT, 4]), ("glr", [P, NT, GLA_LR]))
        region(AT_W, AT_EVAC, ("w_raw", [P, RAW, UW]), ("w_hi", [P, SPLIT, UW], F32R), ("w_lo", [P, SPLIT, UW], F32R))
        region(AT_EVAC, AT_MIX, ("evac", [P, 2, NT, NB]))
        region(AT_X, END, ("ygT_hi", [P, 2 * GLA_H, S], F32R), ("ygT_lo", [P, 2 * GLA_H, S], F32R))
        region(AT_YN, AT_NSA, ("ynT_hi", [P, NSA_H, S], F32R), ("ynT_lo", [P, NSA_H, S], F32R))
        region(AT_X, END, ("x_nat", [P, NT, D]))
        region(AT_MIX, AT_YN, ("hT_hi", [P, KC, S], F32R), ("hT_lo", [P, KC, S], F32R), ("gates", [P, NT, 3 * NSA_H]),
               ("cos_t", [P, NT, HALF]), ("sin_t", [P, NT, HALF]), ("kcT", [P, NSA_G * NCMP]), ("vc", [NCMP, NSA_G, DH]),
               ("tri", [P, S]), ("cmask", [P, NT, NCMP]), ("bT", [P, GLA_H + 1, S]))
        region(AT_YN, AT_X, ("xgT", [P, KC, S]), ("g1", [P, KC]), ("w_small", [P, KC, 64]), ("pos_i", [P, NT], I32),
               ("pos_f", [P, NT]), ("inv_f", [P, HALF]), ("ang", [P, NT, HALF]), ("turns", [P, NT, HALF]), ("sq_junk", [P, D]))
        region(AT_YN, AT_X, ("glrT", [GLA_LR, S]), ("w_decay", [GLA_LR, GLA_H * GLA_DK]), ("b_decay", [P, GLA_H]),
               ("kv_c", [P, 2, NT, NSA_G * DH]), ("rot_c", [P, 4, NT, NSA_G, HALF]), ("kvT_c", [P, 2, NSA_G, S]),
               ("blk_c", [P, 2, CMP_BLOCK, NSA_G, NCMP]), ("posT", [P, 2, CMP_BLOCK]), ("w1", [P, W1_SLOTS, CMP_BLOCK // 4, DH]),
               ("w2", [P, 2, DH]), ("hid_c", [P, 2, NSA_G * NCMP]))
        region(AT_YN, AT_X, ("masks", [P, nlev, P]), ("gnorm", [P, GLA_DV]), ("qk_g", [P, 2, NT, GLA_DK]), ("v_g", [P, NT, GLA_DV]),
               ("r_g", [P, NT, GLA_DV]), ("sig_g", [P, NT, GLA_DV]), ("qT_g", [P, S]), ("kT_g", [P, S]), ("dec", [P, NL, S]),
               ("qL", [P, NL, S]), ("kL", [P, NL, S]), ("att_m", [P, nlev, P]), ("att_T", [P, 3, P]), ("y_g", [P, NT, GLA_DV]), ("gst", [P, 8]))
        region(AT_NSA, AT_X, ("qk_n", [P, NT, NSA_HPG + 2, DH]), ("rot_n", [P, 4, NT, NSA_HPG + 2, HALF]), ("v_n", [P, 2, NT, DH]),
               ("qkT", [P, NSA_HPG + 2, S]), ("g_n", [P, NT, 3 * NSA_HPG]), ("vc_n", [NCMP, DH]), ("sm", [P, 2, 3 * S]),
               ("smc", [P, 2, NT, NCMP]), ("mx", [P, 2, NT, 3]), ("nmx", [P, 2, NT, 3]), ("sums", [P, 2, NT, 3]), ("wts", [P, 2, NT, 3]),
               ("pT", [P, 4, S]), ("pcT", [NCMP, S]))
        region(AT_MIX, AT_YN, ("mT_hi", [P, KC, S], F32R), ("mT_lo", [P, KC, S], F32R), ("g2", [P, D]))
        region(AT_NSA, AT_X, ("gab", [P, 2, NT, NB]))
        region(AT_EVAC, AT_MIX, ("keys", [P, PEER_H, 2 * PEER_NK]))
        region(AT_MIX, AT_MIX + 16 * KB, ("sc", [P, ROUTES, 2 * PEER_NK]))
        region(AT_NSA, AT_NSA + 8 * KB, ("qpT", [P, PEER_H, S]))
        region(AT_MIX + 16 * KB, AT_YN, ("hst", [P, 2, 4 * S]), ("hs", [P, 2, 2 * S]), ("rs_row", [P, S]), ("rt", [P, 3, ROUTES, TOPK]),
               ("gate_b", [P, TB, PEER_NK]))
        region(AT_NSA + 16 * KB, AT_X, ("rtT", [P, 3, S]), ("rt16", [P, 3, TB]),
               ("iota", [P, PEER_NK]), ("s_now", [P, 2, PEER_NK]), ("s_cut", [P, 2, PEER_NK]), ("v_top", [P, 2, TOPK]),
               ("i_top", [P, 2, TOPK], U32), ("if_top", [P, 2, TOPK]), ("cand", [P, TOPK, TOPK]), ("cand_cut", [P, TOPK, TOPK]),
               ("vals", [P, TOPK]), ("flat", [P, TOPK], U32), ("ab", [P, 2, TOPK], U32), ("abf", [P, 2, TOPK]),
               ("ones", [P, P]), ("rs_diag", [P, NT, P]), ("hot", [P, 2, TOPK, TOPK]), ("e12", [P, 2, TOPK]), ("rexp", [P, TOPK]), ("rst", [P, 4]))
        region(AT_NSA, AT_NSA + 16 * KB, ("hot1a", [P, TB, PEER_NK]), ("hot2a", [P, TB, PEER_NK]))
        region(AT_MIX, AT_MIX + 16 * KB, ("hot1b", [P, TB, PEER_NK]), ("hot2b", [P, TB, PEER_NK]))
        region(AT_EVAC, AT_MIX, ("gate_a", [P, TB, PEER_NK]))
        region(AT_MIX, AT_MIX + 16 * KB, ("h_in", [P, 2, VB, S]), ("g_tab", [P, S // TB, 2 * VB, TB]))
        region(AT_NSA, AT_NSA + 16 * KB, ("w_up", [P, 2, VB, S], F32R), ("w_low", [P, 2, VB, S], F32R))
        region(AT_YN, AT_NSA, ("out_t", [P, NT, D]))
        region(AT_MIX + 16 * KB, AT_YN, ("gf", [P, D]), ("sq_last", [P, D]))
        ident, rstd1, rstd2, stat, sq_x1, w_raw, w_hi, w_lo, evac = (buf["ident"], buf["rstd1"], buf["rstd2"], buf["stat"], buf["sq_x1"], buf["w_raw"], buf["w_hi"], buf["w_lo"], buf["evac"])
        ygT_hi, ygT_lo, ynT_hi, ynT_lo, x_nat, hT_hi, hT_lo, gates, cos_t = (buf["ygT_hi"], buf["ygT_lo"], buf["ynT_hi"], buf["ynT_lo"], buf["x_nat"], buf["hT_hi"], buf["hT_lo"], buf["gates"], buf["cos_t"])
        sin_t, kcT, vc, tri, cmask, bT, xgT, g1, w_small = (buf["sin_t"], buf["kcT"], buf["vc"], buf["tri"], buf["cmask"], buf["bT"], buf["xgT"], buf["g1"], buf["w_small"])
        pos_i, pos_f, inv_f, ang, turns, sq_junk, glrT, w_decay, b_decay = (buf["pos_i"], buf["pos_f"], buf["inv_f"], buf["ang"], buf["turns"], buf["sq_junk"], buf["glrT"], buf["w_decay"], buf["b_decay"])
        kv_c, rot_c, kvT_c, blk_c, posT, w1, w2, hid_c, masks = (buf["kv_c"], buf["rot_c"], buf["kvT_c"], buf["blk_c"], buf["posT"], buf["w1"], buf["w2"], buf["hid_c"], buf["masks"])
        gnorm, qk_g, v_g, r_g, sig_g, qT_g, kT_g, dec, qL = (buf["gnorm"], buf["qk_g"], buf["v_g"], buf["r_g"], buf["sig_g"], buf["qT_g"], buf["kT_g"], buf["dec"], buf["qL"])
        kL, att_m, att_T, y_g, gst, qk_n, rot_n, v_n, qkT = (buf["kL"], buf["att_m"], buf["att_T"], buf["y_g"], buf["gst"], buf["qk_n"], buf["rot_n"], buf["v_n"], buf["qkT"])
        g_n, vc_n, sm, smc, mx, nmx, sums, wts, pT = (buf["g_n"], buf["vc_n"], buf["sm"], buf["smc"], buf["mx"], buf["nmx"], buf["sums"], buf["wts"], buf["pT"])
        pcT, mT_hi, mT_lo, g2, gab, qpT, keys, sc, hst = (buf["pcT"], buf["mT_hi"], buf["mT_lo"], buf["g2"], buf["gab"], buf["qpT"], buf["keys"], buf["sc"], buf["hst"])
        hs, rs_row, rt, gate_a, gate_b, rtT, rt16, iota, s_now = (buf["hs"], buf["rs_row"], buf["rt"], buf["gate_a"], buf["gate_b"], buf["rtT"], buf["rt16"], buf["iota"], buf["s_now"])
        s_cut, v_top, i_top, if_top, cand, cand_cut, vals, flat, ab = (buf["s_cut"], buf["v_top"], buf["i_top"], buf["if_top"], buf["cand"], buf["cand_cut"], buf["vals"], buf["flat"], buf["ab"])
        abf, hot, e12, rexp, rst, hot1a, hot2a, hot1b, hot2b, h_in = (buf["abf"], buf["hot"], buf["e12"], buf["rexp"], buf["rst"], buf["hot1a"], buf["hot2a"], buf["hot1b"], buf["hot2b"], buf["h_in"])
        g_tab, w_up, w_low, out_t, gf, sq_last = (buf["g_tab"], buf["w_up"], buf["w_low"], buf["out_t"], buf["gf"], buf["sq_last"])
        hots = ((hot1a, hot2a), (hot1b, hot2b))
        glr, newton, ones, rs_diag = buf["glr"], buf["newton"], buf["ones"], buf["rs_diag"]
        mrg = evac
        h2T_hi, h2T_lo = ynT_hi, ynT_lo
        zT = kvT_c[:, 0, :, :].rearrange("p g t -> p (g t)")
        zA = kvT_c[:, 1, :, :].rearrange("p g t -> p (g t)")

        psum = ctx.enter_context(nc.psum_tensor("psum", [P, 8, NB], F32))
        hid = nc.dram_tensor("hid_scratch", [PEER_NK // 4, P, 4 * S], F32, kind="Internal").ap()
        tab = nc.dram_tensor("tab_scratch", [S // TB, P, PEER_NK, TB], F32, kind="Internal").ap()
        proj = nc.dram_tensor("proj_scratch", [PROJ_BLOCKS, P, NT, NB], F32, kind="Internal").ap()

        def sems(*names):
            return [sem(n) for n in names]

        xT_in = sems(*(f"xT_landed{q}" for q in range(4)))
        xn_in, g1_in, const_in, small_in, ssq1, ms1_done, sq1_done, rs1_done = sems(
            "xn_in", "g1_in", "const_in", "small_in", "ssq1", "ms1_done", "sq1_done", "rs1_done")
        xg_done, h_hi, h_lo, ang_ready, trig_done, small_done, small_out = sems(
            "xg_done", "h_hi", "h_lo", "ang_ready", "trig_done", "small_done", "small_out")
        v_step, a_step = sems("v_step", "a_step")
        w_in_s = sems(*(f"w_landed{k}" for k in range(RAW)))
        hi_done, lo_done, unit_done, evac_done = sems("hi_done", "lo_done", "unit_done", "evac_done")
        stored = sems("stored0", "stored1")
        prep_in, kvc_in, w1_used, pe_prep, act_prep, dve_prep = sems("prep_in", "kvc_in", "w1_used", "pe_prep", "act_prep", "dve_prep")
        w1_in = sems(*(f"w1_landed{k}" for k in range(W1_SLOTS)))
        g_msk, g_one, g_in, g_vr_in, g_silu, g_qkt, g_qe, g_ke, g_dec, g_exp, g_ql, g_kl = sems(
            "g_consts_in", "g_ones", "g_qk_in", "g_vr_in", "g_silu", "g_turned", "g_q_out", "g_k_out", "g_decay", "g_exp", "g_q_scaled", "g_k_scaled")
        g_lev, g_att, g_a01, g_o, g_rn, g_sig, g_y, g_yt, g_yhi, g_ylo = sems(
            "g_levels", "g_att", "g_att01", "g_out", "g_rnorm", "g_sig", "g_y", "g_y_turned", "g_y_hi", "g_y_lo")
        nqk_in, nv_in, roped, qkt_done, qkt_a, qkt_v, vcn_done = sems(
            "n_qk_in", "n_v_in", "n_roped", "n_qk_turned", "n_qk_out_act", "n_qk_out_dve", "n_vc_ready")
        s_done, mx_done, exp_done, p_done, pt_done, pt_a, pt_v, pv_done, o_hi, o_lo = sems(
            "scores_done", "max_done", "exp_done", "probs_done", "probs_turned", "pT_out_act", "pT_out_dve", "pv_done", "o_hi", "o_lo")
        gab_in, gab_sig, m_done, mt_done, m_hi, m_lo, g2_in = sems(
            "gates_in", "gates_sig", "merge_read", "merged_turned", "m_hi", "m_lo", "g2_in")
        x1_done, sq2, xg2_done, xt_done, x_hi, x_lo, ms2_done, sq2_done, rs2_done, h2_done = sems(
            "x1_done", "sq2", "xg2_done", "xg2_turned", "x_hi", "x_lo", "ms2_done", "sq2_done", "rs2_done", "h2_done")
        qpt_out, sc_done, sc_out, keys_in, iota_in, gf_in = sems("queryT_out", "sc_done", "sc_out", "keys_in", "iota_in", "gf_in")
        rsd_done, rs_row_done, rs_row_out, r_vals, r_exp, routed = sems(
            "rs_diag_done", "rs_row_done", "rs_row_out", "r_vals", "r_exp", "routed")
        hid_scaled, hid_gelu = sems("hid_scaled", "hid_gelu")
        hid_st = sems("hid_stored0", "hid_stored1")
        rt_turned, rt_out, rt16_done, hot1_done, hot2_done, tab_done, tab_out = sems(
            "rt_turned", "rt_out", "rt16_done", "hot1_done", "hot2_done", "tab_done", "tab_out")
        tab_st = sems("tab_stored0", "tab_stored1")
        v_in, prod_done, wup_done, wlow_done, acc_done = sems("v_operands_in", "prod_done", "w_up_done", "w_low_done", "acc_done")
        x2_done, fsq, fms, frs, out_done, out_st = sems("x2_done", "fsq", "fms", "frs", "out_done", "out_stored")

        block = ctx.enter_context(nc.Block())

        def wait_alone(eng, s, value):
            eng.wait_ge(s, value)
            eng.nop(nofuse=True)

        class Steps:

            def __init__(self, eng, s):
                self.eng, self.s, self.n, self.base = eng, s, 0, 0

            def __call__(self, ins, alone=False):
                self.n += 1
                ins.then_inc(self.s, 1)
                self.eng.wait_ge(self.s, self.base + self.n)
                if alone:
                    self.eng.nop(nofuse=True)

            def enter(self, i, first, per):
                self.start, self.per = self.n, per
                self.base, self.first = (i - first) * per, first

            def leave(self, count):
                assert self.n - self.start == self.per, (self.n - self.start, self.per)
                self.n = self.start + self.per * count
                self.base = 0

        @block.sync
        def _(sp):
            for q in range(4):
                sp.dma_start(xgT[:, 4 * q:4 * q + 4, :], io["xT"][:, 4 * q:4 * q + 4, :]).then_inc(xT_in[q], 16)
                if q < RAW:
                    sp.dma_start(w_raw[:, q, :], io["w_units"][q]).then_inc(w_in_s[q], 16)
            with sp.Fori(1, UNITS // RAW) as i:
                for s in range(RAW):
                    sp.wait_ge(hi_done, i * RAW + (s - RAW + 1))
                    sp.wait_ge(lo_done, i * RAW + (s - RAW + 1))
                    sp.dma_start(w_raw[:, s, :], io["w_units"][ds(i * RAW + s, 1), :, :].rearrange("a p n -> p (a n)")).then_inc(w_in_s[s], 16)
            for t in range(NT):
                sp.wait_ge(out_done, t + 1)
                sp.dma_start(io["out"][t * P:(t + 1) * P, :], out_t[:, t, :]).then_inc(out_st, 16)
            sp.wait_ge(out_st, 16 * NT)

        @block.gpsimd
        def _(pool):
            pool.wait_ge(xT_in[3], 16)
            pool.dma_start(x_nat[:, :, :], io["x"]).then_inc(xn_in, 16)
            pool.dma_start(w_small[:, :, :], io["w_small"]).then_inc(small_in, 16)
            pool.wait_ge(small_done, 1)
            pool.wait_ge(h_lo, 4)
            pool.wait_ge(trig_done, 2)
            for dst, name in ((w_decay[:, :], "w_decay"), (b_decay[:, :], "b_decay"), (posT[:, :, :], "posT"), (w2[:, :, :], "w2")):
                pool.dma_start(dst, io[name]).then_inc(prep_in, 16)
            pool.wait_ge(stored[0], 16)
            pool.wait_ge(stored[1], 16)
            for a, b in ((0, B_KCM), (1, B_VCM)):
                pool.dma_start(kv_c[:, a, :, :], proj[b]).then_inc(kvc_in, 16)
            for n in range(8):
                if n >= W1_SLOTS:
                    pool.wait_ge(w1_used, n - W1_SLOTS + 1)
                pool.dma_start(w1[:, n % W1_SLOTS, :, :], io["w1"][n]).then_inc(w1_in[n % W1_SLOTS], 16)

            pool.wait_ge(pe_prep, 5)
            pool.wait_ge(act_prep, 8)
            pool.wait_ge(dve_prep, 11)
            pool.dma_start(masks[:, :, :], io["gla_masks"]).then_inc(g_msk, 16)
            pool.dma_start(gnorm[:, :], io["gla_g"].partition_broadcast(P)).then_inc(g_msk, 16)
            for k in range(2):
                pool.wait_ge(stored[k], 16 * B_KSL // 2)
            def distances(h):
                for n, m in enumerate([*LEVELS, P]):
                    b = bT[:, ds(h, 1), :].rearrange("p a (n m) -> p (a n) m", m=2 * m)
                    ins = pool.tensor_tensor(dec[:, n, :].rearrange("p (n m) -> p n m", m=2 * m), b,
                                             b[:, :, m - 1:m].to_broadcast([P, S // (2 * m), 2 * m]), ALU.subtract)
                ins.then_inc(g_dec, 1)

            distances(0)
            pool.wait_ge(g_one, 1)
            with pool.Fori(0, GLA_H // 2) as i:
                for hp in range(2):
                    h = i * 2 + hp
                    wait_alone(pool, g_qkt, h + FIRST)
                    for a, b in ((0, B_GQ), (1, B_GK)):
                        pool.dma_start(qk_g[:, a, :, :], proj[b][:, :, ds(h * GLA_DK, GLA_DK)]).then_inc(g_in, 16)
                    wait_alone(pool, g_o, h + FIRST)
                    wait_alone(pool, g_y, h + FIRST)
                    wait_alone(pool, g_sig, h + FIRST)
                    for dst, b in ((v_g, B_GV), (r_g, B_GR)):
                        pool.dma_start(dst[:, :, :], proj[ds(i + b, 1), :, :, hp * GLA_DV:(hp + 1) * GLA_DV].rearrange("a p t n -> p (a t) n")).then_inc(g_vr_in, 16)
                    wait_alone(pool, g_exp, h + 1)
                    wait_alone(pool, g_ke, h + 1)
                    pool.tensor_tensor(kL[:, 0:KL_POOL, :], dec[:, 0:KL_POOL, :], kT_g[:, None, :].to_broadcast([P, KL_POOL, S]), ALU.mult).then_inc(g_kl, 1)
                    wait_alone(pool, g_sig, h + 1 + FIRST)
                    pool.tensor_tensor(sig_g[:, :, :], sig_g[:, :, :], r_g[:, :, :], ALU.mult).then_inc(g_silu, 1)
                    wait_alone(pool, g_kl, h + 1)
                    wait_alone(pool, g_ql, h + 1)
                    distances(h + 1)

            pool.wait_ge(g_ylo, GLA_H + FIRST)
            pool.wait_ge(g_yhi, GLA_H + FIRST)
            with pool.Fori(0, NSA_G) as g:
                wait_alone(pool, stored[0], g * 16 + 16 * (B_NQ // 2 + 1))
                wait_alone(pool, stored[1], g * 16 + 16 * (B_NQ // 2))
                wait_alone(pool, qkt_done, g + FIRST)
                pool.dma_start(qk_n[:, :, 0:NSA_HPG, :], proj[ds(g + B_NQ, 1), :, :, :].rearrange("a p t (h d) -> p (a t) h d", d=DH)).then_inc(nqk_in, 16)
                for a, b in ((NSA_HPG, B_KSL), (NSA_HPG + 1, B_KWN)):
                    pool.dma_start(qk_n[:, :, a, :], proj[b][:, :, ds(g * DH, DH)]).then_inc(nqk_in, 16)
                wait_alone(pool, pv_done, g * NSA_HPG + FIRST)
                for a, b in ((0, B_VSL), (1, B_VWN)):
                    pool.dma_start(v_n[:, a, :, :], proj[b][:, :, ds(g * DH, DH)]).then_inc(nv_in, 16)

            pool.wait_ge(pv_done, NSA_H + FIRST)
            pool.wait_ge(o_lo, NSA_H + FIRST)
            pool.wait_ge(unit_done, PROJ_BLOCKS * UPB)
            pool.wait_ge(stored[0], 16 * PROJ_BLOCKS // 2)
            pool.wait_ge(stored[1], 16 * PROJ_BLOCKS // 2)
            pool.dma_start(g2[:, :], io["g2"].partition_broadcast(P)).then_inc(g2_in, 16)
            with pool.Fori(0, 4) as nb:
                wait_alone(pool, m_done, nb * 2 + FIRST)
                for a, b in ((0, B_GA), (1, B_GB)):
                    pool.dma_start(gab[:, a, :, :], proj[ds(nb + b, 1), :, :, :].rearrange("a p t n -> p (a t) n")).then_inc(gab_in, 16)

            pool.wait_ge(unit_done, PROJ_BLOCKS * UPB + 3 * (UPG + UPB) + UPG)
            pool.dma_start(x_nat[:, :, :], io["x"]).then_inc(xn_in, 16)

            pool.wait_ge(xt_done, 4)
            pool.dma_start(keys[:, :, :], io["keys"]).then_inc(keys_in, 16)
            pool.dma_start(iota[:, :], io["iota"].partition_broadcast(P)).then_inc(iota_in, 16)

            def v_load(i):
                pool.dma_start(h_in[:, :, :, :].rearrange("p a c t -> p a (c t)"),
                               hid[ds(i * 2, 2), :, :].rearrange("a p n -> p a n")).then_inc(v_in, 16)
                pool.dma_start(g_tab[:, :, :, :], tab[:, :, ds(i * 2 * VB, 2 * VB), :].rearrange("b p c t -> p b c t")).then_inc(v_in, 16)

            pool.wait_ge(tab_done, S // TB)
            pool.wait_ge(hid_st[0], 16 * (I_T3 - 1))
            pool.wait_ge(hid_st[1], 16 * (I_T3 - 1))
            pool.wait_ge(tab_st[0], 16 * 10)
            pool.wait_ge(tab_st[1], 16 * 6)
            v_load(0)
            pool.wait_ge(hid_st[0], 16 * U_IT)
            pool.wait_ge(hid_st[1], 16 * U_IT)
            pool.dma_start(gf[:, :], io["gf"].partition_broadcast(P)).then_inc(gf_in, 16)
            with pool.Fori(1, PEER_NK // (2 * VB)) as i:
                wait_alone(pool, wlow_done, i * 2)
                v_load(i)

        @block.scalar
        def _(act):
            for s in (g_sig, g_yhi, o_hi, pt_a, m_hi, x_hi):
                act.sem_inc(s, FIRST)
            step = Steps(act, a_step)

            def hi(n, s):
                act.wait_ge(w_in_s[s % RAW], (n - s % RAW) * (16 // RAW) + 16)
                wait = n - (SPLIT - 1)
                if not (isinstance(wait, int) and wait <= 0):
                    act.wait_ge(unit_done, wait)
                act.activation(w_hi[:, s % SPLIT, :], w_raw[:, s % RAW, :], ACT.Copy).then_inc(hi_done, 1)

            def evacuate(b, par, first=False):
                act.wait_ge(unit_done, b * UPB + UPB)
                if not first:
                    act.wait_ge(stored[par], (b - par) * 8)
                for t in range(NT):
                    act.activation(evac[:, par, t, :], psum[:, 2 * par + t, :], ACT.Copy, scale=rstd1[:, t:t + 1]).then_inc(evac_done, 1)
                act.wait_ge(evac_done, b * 2 + 2)
                dst = proj[b] if isinstance(b, int) else proj[ds(b, 1), :, :, :].rearrange("a p t n -> p (a t) n")
                act.dma_start(dst, evac[:, par, :, :]).then_inc(stored[par], 16)

            act.dma_start(g1[:, :], io["g1"]).then_inc(g1_in, 16)
            for dst, name in ((ident[:, :], "ident"), (pos_i[:, :], "positions"),
                              (tri[:, :], "tri"), (cmask[:, :, :], "cmask")):
                act.dma_start(dst, io[name]).then_inc(const_in, 16)
            act.dma_start(inv_f[:, :], io["inv_f"].partition_broadcast(P)).then_inc(const_in, 16)
            for q in range(4):
                act.wait_ge(xg_done, q + 1)
                act.activation(hT_hi[:, 4 * q:4 * q + 4, :], xgT[:, 4 * q:4 * q + 4, :], ACT.Copy).then_inc(h_hi, 1)
                if q < AHEAD:
                    hi(q, q)

            for k in range(UPB):
                hi(k + AHEAD, k + AHEAD)
                if k == 1:
                    act.wait_ge(xn_in, 16)
                    for t in range(NT):
                        act.activation(sq_junk[:, :], x_nat[:, t, :], ACT.Square, accum_out=stat[:, t:t + 1]).then_inc(ssq1, 1)
                        act.wait_ge(ssq1, t + 1)
                if k == 2:
                    act.wait_ge(ms1_done, 1)
                    act.activation(stat[:, 4:6], stat[:, 2:4], ACT.Sqrt).then_inc(sq1_done, 1)
                    act.wait_ge(ang_ready, 1)
                    act.activation(sin_t[:, :, :], ang[:, :, :], ACT.Sin).then_inc(trig_done, 1)
                    act.activation(turns[:, :, :], ang[:, :, :], ACT.Sin, scale=0.5).then_inc(trig_done, 1)
            act.wait_ge(small_done, 1)
            act.wait_ge(rs1_done, 1)
            for t in range(NT):
                act.activation(glr[:, t, :], psum[:, 4, t * 64:t * 64 + GLA_LR], ACT.Copy, scale=rstd1[:, t:t + 1]).then_inc(small_out, 1)
                act.activation(gates[:, t, :], psum[:, 4, t * 64 + GLA_LR:(t + 1) * 64], ACT.Sigmoid, scale=rstd1[:, t:t + 1]).then_inc(small_out, 1)
            evacuate(0, 0, True)
            for k in range(UPB):
                hi(UPB + k + AHEAD, k + AHEAD)
            evacuate(1, 1, True)
            for k in range(2 * UPB):
                hi(2 * UPB + k + AHEAD, k + AHEAD)
                if k == 0:
                    act.wait_ge(pe_prep, 1)
                    act.activation(glrT[:, :], psum[0:GLA_LR, 4, 0:S], ACT.Copy).then_inc(act_prep, 1)
                if k == 1:
                    act.wait_ge(dve_prep, 4)
                    step(act.activation(zA, zT, ACT.Abs))
                    step(act.activation(zA, zA, ACT.Exp, scale=-1.0))
                    act.activation(zA, zA, ACT.Ln, bias=1.0).then_inc(act_prep, 1)
                if k in (3, 4):
                    a = k - 3
                    act.wait_ge(pe_prep, 3 + a)
                    act.activation(kvT_c[:, a, :, :].rearrange("p g t -> p (g t)"), psum[:, 4 + 2 * a:6 + 2 * a, :].rearrange("p b n -> p (b n)"), ACT.Copy).then_inc(act_prep, 1)
                if k in (5, 6):
                    a = k - 5
                    act.wait_ge(w1_used, 4 * a + 4)
                    act.activation(hid_c[:, a, :], psum[:, 4 + a, 0:NSA_G * NCMP], ACT.Gelu_apprx_tanh).then_inc(act_prep, 1)
                if k == 7:
                    act.wait_ge(pe_prep, 5)
                    act.activation(kcT[:, :], psum[:, 6, 0:NSA_G * NCMP], ACT.Copy).then_inc(act_prep, 1)
                    act.activation(vc[:, :, :].rearrange("n g d -> n (g d)"), psum[0:NCMP, 7, :], ACT.Copy).then_inc(act_prep, 1)
                if k % UPB == UPB - 1:
                    evacuate(2 + k // UPB, k // UPB)
            with act.Fori(2, A_BLOCKS // 2) as i:
                for par in range(2):
                    for k in range(UPB):
                        hi(i * 8 + (par * 4 + k + AHEAD), k + AHEAD)
                    evacuate(i * 2 + par, par)

            def decays(h):
                act.wait_ge(g_dec, h + 1)
                step(act.activation(dec[:, 0:LDIAG, :], dec[:, 0:LDIAG, :], ACT.Abs))
                act.activation(dec[:, 0:LDIAG, :], dec[:, 0:LDIAG, :], ACT.Exp, scale=-1.0 / GLA_TAU).then_inc(g_exp, 1)

            def gla_slot(h, k):
                if k == 0:
                    act.wait_ge(g_qkt, h + 1 + FIRST)
                    act.activation(qT_g[:, :], psum[:, 4, 0:S], ACT.Copy, scale=GLA_DK ** -0.5).then_inc(g_qe, 1)
                    act.wait_ge(g_vr_in, h * 32 + 32)
                    act.activation(sig_g[:, :, :], r_g[:, :, :], ACT.Sigmoid).then_inc(g_sig, 1)
                if k == 2:
                    act.wait_ge(g_o, h + 1 + FIRST)
                    for t in range(NT):
                        step(act.activation(y_g[:, t, :], psum[:, 7, t * GLA_DV:(t + 1) * GLA_DV], ACT.Square, accum_out=gst[:, t:t + 1]))
                    act.activation(gst[:, 2:4], gst[:, 0:2], ACT.Sqrt, scale=1.0 / GLA_DV, bias=eps_ap).then_inc(g_rn, 1)
                if k == 3:
                    decays(h + 1)
                    act.wait_ge(g_yt, h + 1)
                    act.activation(ygT_hi[:, ds(h * 2, 2), :].rearrange("p c t -> p (c t)"), psum[:, 4, :], ACT.Copy).then_inc(g_yhi, 1)

            eps_ap = stat[:, 12:13]
            act.wait_ge(g_msk, 32)
            decays(0)
            base = A_BLOCKS * UPB
            with act.Fori(0, GLA_H // 2) as i:
                step.enter(i, 0, 2 * 3)
                for hp in range(2):
                    for k in range(UPB):
                        hi(i * 8 + (base + hp * 4 + k + AHEAD), k + AHEAD)
                        gla_slot(i * 2 + hp, k)
                    evacuate(i * 2 + (A_BLOCKS + hp), hp)
                step.leave(GLA_H // 2)

            base = (A_BLOCKS + 4) * UPB
            with act.Fori(0, NSA_G) as g:
                for k in range(8):
                    hi(g * 8 + (base + k + AHEAD), k + AHEAD)
                    if k == 0:
                        act.wait_ge(pv_done, g * NSA_HPG + FIRST)
                        act.activation(vc_n[:, :], vc[:, ds(g, 1), :].rearrange("n a d -> n (a d)"), ACT.Copy).then_inc(vcn_done, 1)
                    if k == 1:
                        act.wait_ge(qkt_done, g + 1 + FIRST)
                        for b in range(2):
                            act.activation(qkT[:, 2 * b:2 * b + 2, :].rearrange("p h t -> p (h t)"), psum[:, 4 + b, :], ACT.Copy).then_inc(qkt_a, 1)
                    j = k - 4
                    if 0 <= j < NSA_HPG:
                        act.wait_ge(pv_done, g * NSA_HPG + j + 1 + FIRST)
                        act.activation(ynT_hi[:, ds(g * NSA_HPG + j, 1), :].rearrange("p a t -> p (a t)"), psum[:, 6, S:2 * S], ACT.Copy).then_inc(o_hi, 1)
                    j = k - 3
                    if 0 <= j < NSA_HPG:
                        act.wait_ge(pt_done, g * NSA_HPG + j + 1)
                        act.activation(pT[:, 0:2, 0:P], psum[:, 6, 0:S].rearrange("p (a t) -> p a t", a=2), ACT.Copy).then_inc(pt_a, 1)
                        act.activation(pcT[:, :], psum[0:NCMP, 6, S:2 * S], ACT.Copy).then_inc(pt_a, 1)
                    j = k - 2
                    if 0 <= j < NSA_HPG:
                        q = j % 2
                        act.wait_ge(mx_done, g * NSA_HPG + j + 1 + FIRST)
                        for t in range(NT):
                            for b in (2, 0, 1):
                                w = (b + 1) % 3
                                src = smc[:, q, t, :] if b == 2 else sm[:, q, 2 * P * t + b * (t + 1) * P:2 * P * t + (b + 1) * (t + 1) * P]
                                act.activation(src, src, ACT.Exp, scale=SCALE, bias=nmx[:, q, t, w:w + 1],
                                               accum_out=sums[:, q, t, w:w + 1]).then_inc(exp_done, 1)
                    if k % 4 == 3:
                        evacuate(g * 2 + (A_BLOCKS + 4 + k // 4), k // 4)

            base = PROJ_BLOCKS * UPB
            act.wait_ge(stored[0], 16 * PROJ_BLOCKS // 2)
            act.wait_ge(stored[1], 16 * PROJ_BLOCKS // 2)
            with act.Fori(0, 2) as i:
                for nbp in range(2):
                    nb = i * 2 + nbp
                    for k in range(6):
                        hi(i * 12 + (base + nbp * 6 + k + AHEAD), nbp * 6 + k + AHEAD)
                        if k == 0:
                            act.wait_ge(gab_in, nb * 32 + 32)
                            act.activation(gab[:, :, :, :], gab[:, :, :, :], ACT.Sigmoid).then_inc(gab_sig, 1)
                        if (nbp, k) in ((1, 0), (1, 5)):
                            m = nb - 1 if k == 0 else nb
                            act.wait_ge(mt_done, m + 1)
                            act.activation(mT_hi[:, ds(m * 4, 4), :].rearrange("p c t -> p (c t)"), psum[:, 4:6, :].rearrange("p b n -> p (b n)"), ACT.Copy).then_inc(m_hi, 1)

            def x_upper(b):
                act.wait_ge(xt_done, b + 1)
                act.activation(h2T_hi[:, ds(b * 4, 4), :].rearrange("p c t -> p (c t)"), psum[:, 4:6, :].rearrange("p b n -> p (b n)"), ACT.Copy).then_inc(x_hi, 1)

            base = PROJ_BLOCKS * UPB + 4 * (UPG + UPB)
            with act.Fori(0, 2) as i:
                for par in range(2):
                    b = i * 2 + par
                    for k in range(UPB):
                        hi(i * 8 + (base + par * 4 + k + AHEAD), k + AHEAD)
                        if (par, k) == (1, 0):
                            x_upper(b - 1)
                    act.wait_ge(x1_done, b + 1 + FIRST)
                    for t in range(NT):
                        act.activation(gab[:, t, 0, :], x_nat[:, t, ds(b * NB, NB)], ACT.Square, accum_out=sq_x1[:, t, ds(b, 1)]).then_inc(sq2, 1)
                        act.wait_ge(sq2, b * 2 + t + 1)
                x_upper(b)

            base = PROJ_BLOCKS * UPB + 4 * (UPG + UPB) + 4 * UPB
            def scores_out(par):
                act.wait_ge(rs2_done, 1)
                act.wait_ge(sc_done, par + 1)
                for t in range(NT):
                    act.activation(sc[:, t * PEER_H + 4 * par:t * PEER_H + 4 * par + 4, :].rearrange("p h n -> p (h n)"),
                                   psum[:, 4 + 2 * t:6 + 2 * t, :].rearrange("p b n -> p (b n)"), ACT.Copy, scale=rstd2[:, t:t + 1]).then_inc(sc_out, 1)

            act.wait_ge(ms2_done, 1)
            act.activation(stat[:, 10:12], stat[:, 8:10], ACT.Sqrt).then_inc(sq2_done, 1)
            for par in range(2):
                for k in range(UPB):
                    n = base + par * 4 + k + AHEAD
                    hi(n, n % 4)
                    if (par, k) == (1, 0):
                        scores_out(0)
                act.wait_ge(unit_done, base + par * UPB + UPB)
                act.activation(qpT[:, 4 * par:4 * par + 4, :].rearrange("p h t -> p (h t)"), psum[:, 2 * par:2 * par + 2, :].rearrange("p b n -> p (b n)"), ACT.Copy).then_inc(qpt_out, 1)
            scores_out(1)

            def route_exp(u):
                act.wait_ge(r_vals, u + 1)
                act.activation(rexp[:, :], vals[:, :], ACT.Exp, bias=rst[:, 0:1], accum_out=rst[:, 1:2]).then_inc(r_exp, 1)

            def table_out(tb, half, prior):
                act.wait_ge(tab_done, tb + 1)
                if prior is not None:
                    act.wait_ge(tab_st[half], 16 * prior)
                dst = (gate_a, gate_b)[half]
                act.activation(dst[:, :, :].rearrange("p a b -> p (a b)").rearrange("p (c t) -> p t c", t=TB),
                               psum[:, 4:8, :].rearrange("p b (t c) -> p (b t) c", c=PEER_NK), ACT.Copy).then_inc(tab_out, 1)
                act.wait_ge(tab_out, tb + 1)
                dram = tab[tb] if isinstance(tb, int) else tab[ds(tb, 1), :, :, :].rearrange("a p c t -> p (a c) t")
                act.dma_start(dram, dst[:, :, :].rearrange("p a b -> p (a b)").rearrange("p (c t) -> p c t", t=TB)).then_inc(tab_st[half], 16)

            def picks_out(t):
                act.wait_ge(rt_turned, t + 1)
                act.activation(rtT[:, :, t * P:(t + 1) * P], psum[:, 4, 0:3 * P].rearrange("p (w n) -> p w n", w=3), ACT.Copy).then_inc(rt_out, 1)

            def hidden(i, routes=False, tile=None, one=False, two=False):
                for k in range(8):
                    if k % 4 == 3 and routes:
                        route_exp(i * 2 + k // 4)
                    hi(i * 8 + (U0 + k + AHEAD), k + AHEAD)
                    if k == 0 and tile is not None:
                        picks_out(tile)
                    if k % 2 == 1:
                        m, half = i * 4 + k // 2, k // 4
                        act.wait_ge(hid_scaled, m + 1)
                        if k % 4 == 1 and not (isinstance(i, int) and i == 0):
                            act.wait_ge(hid_st[half], i * 16)
                        o = (k // 2 % 2) * 2 * S
                        act.activation(hst[:, half, o:o + 2 * S], hs[:, k // 2 % 2, :], ACT.Gelu_apprx_tanh).then_inc(hid_gelu, 1)
                        if k % 4 == 3:
                            act.wait_ge(hid_gelu, m + 1)
                            dst = hid[2 * i + half] if isinstance(i, int) else hid[ds(i * 2 + half, 1), :, :].rearrange("a p n -> p (a n)")
                            act.dma_start(dst, hst[:, half, :]).then_inc(hid_st[half], 16)
                    if k == 6 and one:
                        first = isinstance(i, int) and i == I_T1
                        table_out(i - I_T1, 0, None if first else i - I_T1)
                    if k % 4 == 3 and two:
                        j, half = i - I_T2, k // 4
                        first = isinstance(i, int) and i == I_T2
                        prior = j + (I_T2 - I_T1) if half == 0 else None if first else j
                        table_out(j * 2 + (I_T2 - I_T1 + half), half, prior)
                    if k == 4 and isinstance(i, int) and i == U_IT - 1:
                        weights_upper(0, 0)

            def weights_upper(m, half):
                act.wait_ge(prod_done, m + 1)
                act.activation(w_up[:, half, :, :], h_in[:, half, :, :], ACT.Copy).then_inc(wup_done, 1)

            hidden(0, routes=True)
            with act.Fori(1, I_T1) as i:
                hidden(i, routes=True)
            hidden(I_T1, routes=True, tile=0, one=True)
            with act.Fori(I_T1 + 1, I_T2) as i:
                hidden(i, routes=True, one=True)
            hidden(I_T2, tile=1, two=True)
            with act.Fori(I_T2 + 1, I_T3) as i:
                hidden(i, two=True)
            for i in range(I_T3, U_IT):
                hidden(i)

            def experts_out(i, last=False):
                for k in range(8):
                    if not (last and k + AHEAD >= 8):
                        hi(i * 8 + (V0 + k + AHEAD), k + AHEAD)
                    if k == 0:
                        weights_upper(i * 2 + 1, 1)
                    if k == 4 and not last:
                        weights_upper(i * 2 + 2, 0)

            experts_out(0)
            with act.Fori(1, PEER_NK // 8 - 1) as i:
                experts_out(i)
            experts_out(PEER_NK // 8 - 1, True)
            for t in range(NT):
                act.wait_ge(x2_done, t + 1)
                act.activation(sq_last[:, :], x_nat[:, t, :], ACT.Square, accum_out=stat[:, t:t + 1]).then_inc(fsq, 1)
                act.wait_ge(fms, t + 1)
                act.activation(stat[:, 4 + t:5 + t], stat[:, 2 + t:3 + t], ACT.Sqrt).then_inc(frs, 1)

        @block.tensor
        def _(pe):
            for s in (g_qkt, g_o, qkt_done, pv_done):
                pe.sem_inc(s, FIRST)
            def unit(n, k4, par, xh, xl, kc0, first, last, free, half=None):
                s = k4 % SPLIT
                if half in (None, 0):
                    pe.wait_ge(hi_done, n + 1)
                    pe.wait_ge(lo_done, n + 1)
                    if first and free is not None:
                        pe.wait_ge(*free)
                cs = range(CU) if half is None else range(half * 2, half * 2 + 2)
                for c in cs:
                    rh, rl = w_hi[:, s, c * NB:(c + 1) * NB], w_lo[:, s, c * NB:(c + 1) * NB]
                    for t in range(NT):
                        ts = slice(t * P, (t + 1) * P)
                        out = psum[:, 2 * par + t, :]
                        st, en = first and c == 0, last and c == CU - 1
                        pe.matmul(out, xh[:, kc0 + c, ts], rh, start=st, stop=False, skip_group_check=True)
                        pe.matmul(out, xh[:, kc0 + c, ts], rl, start=False, stop=False, skip_group_check=True)
                        ins = pe.matmul(out, xl[:, kc0 + c, ts], rh, start=False, stop=en, skip_group_check=True)
                if half in (None, 1):
                    ins.then_inc(unit_done, 1)

            def proj_unit(n, k, par, b, half=None):
                free = None if isinstance(b, int) and b < 2 else (evac_done, b * 2 - 2)
                unit(n, k, par, hT_hi, hT_lo, 4 * k, k == 0, k == UPB - 1, free, half)

            for k in range(UPB):
                pe.wait_ge(h_hi, k + 1)
                pe.wait_ge(h_lo, k + 1)
                proj_unit(k, k, 0, 0)
            pe.wait_ge(small_in, 16)
            for t in range(NT):
                for c in range(KC):
                    ins = pe.matmul(psum[:, 4, t * 64:(t + 1) * 64], xgT[:, c, t * P:(t + 1) * P], w_small[:, c, :],
                                    start=c == 0, stop=c == KC - 1, skip_group_check=True)
            ins.then_inc(small_done, 1)
            for k in range(UPB):
                proj_unit(UPB + k, k, 1, 1)

            def prep_part(k):
                if k == 0:
                    pe.wait_ge(small_out, 4)
                    pe.wait_ge(const_in, 80)
                    for t in range(NT):
                        ins = pe.transpose(psum[0:GLA_LR, 4, t * P:(t + 1) * P], glr[:, t, :], ident[:, :])
                    ins.then_inc(pe_prep, 1)
                if k == 1:
                    pe.wait_ge(act_prep, 1)
                    pe.wait_ge(prep_in, 64)
                    for h in range(GLA_H):
                        ins = pe.matmul(psum[:, 4 + h // 2, (h % 2) * S:(h % 2 + 1) * S], w_decay[:, h * GLA_DK:(h + 1) * GLA_DK], glrT[:, :],
                                        start=True, stop=True, skip_group_check=True)
                    ins.then_inc(pe_prep, 1)
                if k in (3, 4):
                    a = k - 3
                    pe.wait_ge(dve_prep, 10)
                    for g in range(NSA_G):
                        for t in range(NT):
                            ins = pe.transpose(psum[:, 4 + 2 * a + g // 2, (g % 2) * S + t * P:(g % 2) * S + (t + 1) * P],
                                               kv_c[:, a, t, g * DH:(g + 1) * DH], ident[:, :])
                    ins.then_inc(pe_prep, 1)
                if k in (5, 6):
                    a = k - 5
                    pe.wait_ge(dve_prep, 11)
                    for q in range(4):
                        n = a * 4 + q
                        pe.wait_ge(w1_in[n % W1_SLOTS], 16 * (n // W1_SLOTS + 1))
                        for i in range(CMP_BLOCK // 4):
                            c = q * (CMP_BLOCK // 4) + i
                            ins = pe.matmul(psum[:, 4 + a, 0:NSA_G * NCMP], w1[:, n % W1_SLOTS, i, :], blk_c[:, a, c, :, :].rearrange("p g n -> p (g n)"),
                                            start=c == 0, stop=c == CMP_BLOCK - 1, skip_group_check=True)
                        ins.then_inc(w1_used, 1)
                if k == 7:
                    pe.wait_ge(act_prep, 6)
                    pe.matmul(psum[:, 6, 0:NSA_G * NCMP], w2[:, 0, :], hid_c[:, 0, :], start=True, stop=True, skip_group_check=True)
                    for g in range(NSA_G):
                        ins = pe.matmul(psum[0:NCMP, 7, g * DH:(g + 1) * DH], hid_c[:, 1, g * NCMP:(g + 1) * NCMP], w2[:, 1, :],
                                        start=True, stop=True, skip_group_check=True)
                    ins.then_inc(pe_prep, 1)

            for k in range(2 * UPB):
                proj_unit((2 * UPB + k), k % UPB, k // UPB, 2 + k // UPB)
                prep_part(k)
            with pe.Fori(2, A_BLOCKS // 2) as i:
                for par in range(2):
                    for k in range(UPB):
                        proj_unit(i * 8 + (par * 4 + k), k, par, i * 2 + par)

            def gla_part(h, k, half):
                if (k, half) == (0, 1):
                    pe.wait_ge(g_in, h * 32 + 32)
                    pe.wait_ge(g_yhi, h + FIRST)
                    pe.wait_ge(g_ylo, h + FIRST)
                    for a in range(2):
                        for t in range(NT):
                            ins = pe.transpose(psum[:, 4, a * S + t * P:a * S + (t + 1) * P], qk_g[:, a, t, :], ident[:, :])
                    ins.then_inc(g_qkt, 1)
                if (k, half) in ((1, 1), (2, 0)):
                    t = k - 1
                    if t == 0:
                        pe.wait_ge(g_ql, h + 1)
                        pe.wait_ge(g_kl, h + 1)
                        pe.wait_ge(g_att, h * 2 + FIRST)
                    else:
                        pe.wait_ge(g_att, h * 2 + 1 + FIRST)
                    ts = slice(t * P, (t + 1) * P)
                    for n, lev in enumerate([*range(len(LEVELS)), LDIAG]):
                        ins = pe.matmul(psum[:, 5 + n // 4, (n % 4) * P:(n % 4 + 1) * P], kL[:, lev, ts], qL[:, lev, ts],
                                        start=True, stop=True, skip_group_check=True)
                    if t == 0:
                        ins = pe.matmul(psum[:, 4, 0:P], kL[:, L128, 0:P], qL[:, L128, P:S], start=True, stop=True, skip_group_check=True)
                    ins.then_inc(g_lev, 1)
                if (k, half) == (2, 1):
                    pe.wait_ge(g_vr_in, h * 32 + 32)
                    pe.wait_ge(g_att, h * 2 + 2 + FIRST)
                    pe.wait_ge(g_a01, h + 1)
                    pe.matmul(psum[:, 7, 0:GLA_DV], att_T[:, 0, :], v_g[:, 0, :], start=True, stop=True, skip_group_check=True)
                    pe.matmul(psum[:, 7, GLA_DV:2 * GLA_DV], att_T[:, 2, :], v_g[:, 0, :], start=True, stop=False, skip_group_check=True)
                    pe.matmul(psum[:, 7, GLA_DV:2 * GLA_DV], att_T[:, 1, :], v_g[:, 1, :], start=False, stop=True,
                              skip_group_check=True).then_inc(g_o, 1)
                if (k, half) == (3, 1):
                    pe.wait_ge(g_y, h + 1 + FIRST)
                    for c in range(2):
                        for t in range(NT):
                            ins = pe.transpose(psum[:, 4, c * S + t * P:c * S + (t + 1) * P], y_g[:, t, c * P:(c + 1) * P], ident[:, :])
                    ins.then_inc(g_yt, 1)

            pe.wait_ge(act_prep, 8)
            base = A_BLOCKS * UPB
            with pe.Fori(0, GLA_H // 2) as i:
                for hp in range(2):
                    for k in range(UPB):
                        for half in range(2):
                            proj_unit(i * 8 + (base + hp * 4 + k), k, hp, i * 2 + (A_BLOCKS + hp), half)
                            gla_part(i * 2 + hp, k, half)

            def scores(g, j):
                h = g * NSA_HPG + j
                pe.wait_ge(mx_done, h + FIRST)
                if j == 0:
                    pe.wait_ge(qkt_a, g * 2 + 2)
                    pe.wait_ge(qkt_v, g + 1)
                for t in range(NT):
                    q = qkT[:, j, t * P:(t + 1) * P]
                    n = (t + 1) * P
                    for b in range(2):
                        pe.matmul(psum[:, 4 + t, b * n:(b + 1) * n], q, qkT[:, NSA_HPG + b, 0:n], start=True, stop=True, skip_group_check=True)
                    ins = pe.matmul(psum[:, 4, S + t * 16:S + t * 16 + NCMP], q, kcT[:, ds(g * NCMP, NCMP)], start=True, stop=True, skip_group_check=True)
                ins.then_inc(s_done, 1)

            def turn(g, j):
                h = g * NSA_HPG + j
                q = j % 2
                pe.wait_ge(p_done, h + 1)
                pe.wait_ge(o_hi, h + FIRST)
                pe.wait_ge(o_lo, h + FIRST)
                pe.wait_ge(pt_a, h * 2 + FIRST)
                pe.wait_ge(pt_v, h + FIRST)
                for b in range(2):
                    pe.transpose(psum[:, 6, b * P:(b + 1) * P], sm[:, q, b * P:(b + 1) * P], ident[:, :])
                for t in range(NT):
                    pe.transpose(psum[0:NCMP, 6, S + t * P:S + (t + 1) * P], smc[:, q, t, :], ident[:, :])
                for b in range(2):
                    for kt in range(2):
                        o = (kt * 2 + b) * P
                        ins = pe.transpose(psum[:, 7, o:o + P], sm[:, q, 2 * P + b * S + kt * P:2 * P + b * S + (kt + 1) * P], ident[:, :])
                ins.then_inc(pt_done, 1)

            def values(g, j):
                h = g * NSA_HPG + j
                pe.wait_ge(pt_a, h * 2 + 2 + FIRST)
                pe.wait_ge(pt_v, h + 1 + FIRST)
                if j == 0:
                    pe.wait_ge(nv_in, g * 32 + 32)
                    pe.wait_ge(vcn_done, g + 1)
                out = psum[:, 6, S:2 * S]
                pe.matmul(out, v_n[:, 0, 0, :], pT[:, 0, :], start=True, stop=False, skip_group_check=True)
                pe.matmul(out, v_n[:, 1, 0, :], pT[:, 1, :], start=False, stop=False, skip_group_check=True)
                pe.matmul(out, vc_n[:, :], pcT[:, :], start=False, stop=False, skip_group_check=True)
                out = psum[:, 6, S + P:2 * S]
                pe.matmul(out, v_n[:, 0, 1, :], pT[:, 2, P:S], start=False, stop=False, skip_group_check=True)
                pe.matmul(out, v_n[:, 1, 1, :], pT[:, 3, P:S], start=False, stop=True, skip_group_check=True).then_inc(pv_done, 1)

            base = (A_BLOCKS + 4) * UPB
            with pe.Fori(0, NSA_G) as g:
                for k in range(8):
                    proj_unit(g * 8 + (base + k), k % 4, k // 4, g * 2 + (A_BLOCKS + 4 + k // 4))
                    if k == 1:
                        pe.wait_ge(g_yhi, GLA_H + FIRST)
                        pe.wait_ge(g_ylo, GLA_H + FIRST)
                        pe.wait_ge(roped, g + 1)
                        pe.wait_ge(mx_done, g * NSA_HPG + FIRST)
                        pe.wait_ge(o_hi, g * NSA_HPG + FIRST)
                        pe.wait_ge(o_lo, g * NSA_HPG + FIRST)
                        for a in range(NSA_HPG + 2):
                            for t in range(NT):
                                ins = pe.transpose(psum[:, 4 + a // 2, (a % 2) * S + t * P:(a % 2) * S + (t + 1) * P], qk_n[:, t, a, :], ident[:, :])
                        ins.then_inc(qkt_done, 1)
                    if 0 <= k - 4 < NSA_HPG:
                        values(g, k - 4)
                    if 0 <= k - 2 < NSA_HPG:
                        scores(g, k - 2)
                    if 0 <= k - 3 < NSA_HPG:
                        turn(g, k - 3)

            def turn_block(src, ins_done, done):
                pe.wait_ge(*ins_done)
                for c in range(4):
                    for t in range(NT):
                        ins = pe.transpose(psum[:, 4 + c // 2, (c % 2) * S + t * P:(c % 2) * S + (t + 1) * P], src[:, t, c * P:(c + 1) * P], ident[:, :])
                ins.then_inc(done, 1)

            def turn_merged(nb):
                pe.wait_ge(m_hi, nb + FIRST)
                pe.wait_ge(m_lo, nb + FIRST)
                turn_block(mrg[:, 1, :, :], (m_done, nb * 2 + 2 + FIRST), mt_done)

            def turn_x(b):
                pe.wait_ge(x_hi, b + FIRST)
                pe.wait_ge(x_lo, b + FIRST)
                turn_block(mrg[:, 1, :, :], (xg2_done, b + 1), xt_done)

            base = PROJ_BLOCKS * UPB
            pe.wait_ge(evac_done, 2 * PROJ_BLOCKS - 2)
            with pe.Fori(0, 2) as i:
                for nbp in range(2):
                    nb = i * 2 + nbp
                    for k in range(UPG):
                        if nbp == 1 and k == 1:
                            turn_merged(nb - 1)
                        unit(i * 12 + (base + nbp * 6 + k), nbp * 6 + k, 0, ygT_hi, ygT_lo, 4 * k, k == 0, k == UPG - 1, (m_done, nb * 2 + FIRST))
                    pe.wait_ge(o_hi, NSA_H + FIRST)
                    pe.wait_ge(o_lo, NSA_H + FIRST)
                    pe.wait_ge(evac_done, 2 * PROJ_BLOCKS)
                    for k in range(UPB):
                        unit(i * 12 + (base + nbp * 6 + UPG + k), nbp * 6 + UPG + k, 1, ynT_hi, ynT_lo, 4 * k, k == 0, k == UPB - 1, (m_done, nb * 2 + FIRST))
                turn_merged(nb)

            base = PROJ_BLOCKS * UPB + 4 * (UPG + UPB)
            pe.wait_ge(m_hi, 4 + FIRST)
            pe.wait_ge(m_lo, 4 + FIRST)
            with pe.Fori(0, 2) as i:
                for par in range(2):
                    b = i * 2 + par
                    for k in range(UPB):
                        if par == 1 and k == 1:
                            turn_x(b - 1)
                        unit(i * 8 + (base + par * 4 + k), k, par, mT_hi, mT_lo, 4 * k, k == 0, k == UPB - 1, (x1_done, b + FIRST))
                turn_x(b)

            base = PROJ_BLOCKS * UPB + 4 * (UPG + UPB) + 4 * UPB

            def query_unit(par, k):
                n = base + par * UPB + k
                pe.wait_ge(hi_done, n + 1)
                pe.wait_ge(lo_done, n + 1)
                for c in range(CU):
                    kc = CU * k + c
                    for h in range(4):
                        wh, wl = w_hi[:, n % SPLIT, c * NB + h * P:c * NB + (h + 1) * P], w_lo[:, n % SPLIT, c * NB + h * P:c * NB + (h + 1) * P]
                        out = psum[:, 2 * par + h // 2, (h % 2) * S:(h % 2 + 1) * S]
                        pe.matmul(out, wh, h2T_hi[:, kc, :], start=kc == 0 and h % 2 == 0, stop=False, skip_group_check=True)
                        pe.matmul(out, wl, h2T_hi[:, kc, :], start=False, stop=False, skip_group_check=True)
                        ins = pe.matmul(out, wh, h2T_lo[:, kc, :], start=False, stop=kc == KC - 1, skip_group_check=True)
                ins.then_inc(unit_done, 1)

            def query_scores(par):
                pe.wait_ge(qpt_out, par + 1)
                pe.wait_ge(keys_in, 16)
                if par:
                    pe.wait_ge(sc_out, 2)
                for t in range(NT):
                    for h in range(4):
                        ins = pe.matmul(psum[:, 4 + 2 * t + h // 2, (h % 2) * S:(h % 2 + 1) * S], qpT[:, 4 * par + h, t * P:(t + 1) * P],
                                        keys[:, 4 * par + h, :], start=True, stop=True, skip_group_check=True)
                ins.then_inc(sc_done, 1)

            pe.wait_ge(x_hi, 4 + FIRST)
            pe.wait_ge(x_lo, 4 + FIRST)
            pe.wait_ge(x1_done, 4 + FIRST)
            for par in range(2):
                for k in range(UPB):
                    query_unit(par, k)
                    if (par, k) == (1, 0):
                        query_scores(0)
                    if (par, k) == (1, 1):
                        pe.wait_ge(rsd_done, 2)
                        for t in range(NT):
                            ins = pe.matmul(psum[:, 0, t * P:(t + 1) * P], ones[:, :], rs_diag[:, t, :], start=True, stop=True, skip_group_check=True)
                        ins.then_inc(rs_row_done, 1)
            query_scores(1)

            def hidden(i, tile=None, one=False, two=False):
                for k in range(8):
                    n = i * 8 + (U0 + k)
                    m = i * 4 + k // 2
                    pe.wait_ge(hi_done, n + 1)
                    pe.wait_ge(lo_done, n + 1)
                    if k % 2 == 0 and not (isinstance(i, int) and i == 0):
                        pe.wait_ge(hid_scaled, m - 3)
                    s, out = k % SPLIT, psum[:, k // 2, (k % 2) * S:(k % 2 + 1) * S]
                    for c in range(KC):
                        uh, ul = w_hi[:, s, c * P:(c + 1) * P], w_lo[:, s, c * P:(c + 1) * P]
                        pe.matmul(out, uh, h2T_hi[:, c, :], start=c == 0, stop=False, skip_group_check=True)
                        pe.matmul(out, ul, h2T_hi[:, c, :], start=False, stop=False, skip_group_check=True)
                        ins = pe.matmul(out, uh, h2T_lo[:, c, :], start=False, stop=c == KC - 1, skip_group_check=True)
                    ins.then_inc(unit_done, 1)
                    if k == 0 and tile is not None:
                        turn_picks(tile)
                    if k == 5 and one:
                        table(i - I_T1, 0, 0 if isinstance(i, int) and i == I_T1 else i - I_T1)
                    if k % 4 == 2 and two:
                        tb = i * 2 + (k // 4 - I_T2 - I_T1)
                        table(tb, k // 4, tb)

            def turn_picks(t):
                pe.wait_ge(routed, PEER_H * (t + 1))
                if t:
                    pe.wait_ge(tab_out, I_T2 - I_T1)
                for w in range(3):
                    ins = pe.transpose(psum[:, 4, w * P:(w + 1) * P], rt[:, w, t * PEER_H:(t + 1) * PEER_H, :].rearrange("p u k -> p (u k)"), ident[:, :])
                ins.then_inc(rt_turned, 1)

            def table(tb, half, prior):
                pe.wait_ge(hot1_done, tb + 1)
                pe.wait_ge(hot2_done, tb + 1)
                if not (isinstance(prior, int) and prior == 0):
                    pe.wait_ge(tab_out, prior)
                for j in range(TB):
                    ins = pe.matmul(psum[:, 4 + j // 4, (j % 4) * P:(j % 4 + 1) * P], hots[half][0][:, j, :], hots[half][1][:, j, :], start=True, stop=True, skip_group_check=True)
                ins.then_inc(tab_done, 1)

            pe.wait_ge(rs_row_out, 1)
            hidden(0)
            with pe.Fori(1, I_T1) as i:
                hidden(i)
            hidden(I_T1, tile=0, one=True)
            with pe.Fori(I_T1 + 1, I_T2) as i:
                hidden(i, one=True)
            hidden(I_T2, tile=1, two=True)
            with pe.Fori(I_T2 + 1, I_T3) as i:
                hidden(i, two=True)
            for i in range(I_T3, U_IT):
                hidden(i)

            def products(k, t, first=False, last=False):
                s = k % SPLIT
                wh, wl = w_up[:, k // VB, k % VB, t * P:(t + 1) * P], w_low[:, k // VB, k % VB, t * P:(t + 1) * P]
                for q in range(4):
                    vh, vl = w_hi[:, s, q * NB:(q + 1) * NB], w_lo[:, s, q * NB:(q + 1) * NB]
                    out = psum[:, 4 * t + q, :]
                    pe.matmul(out, wh, vh, start=first, stop=False, skip_group_check=True)
                    pe.matmul(out, wh, vl, start=False, stop=False, skip_group_check=True)
                    ins = pe.matmul(out, wl, vh, start=False, stop=last, skip_group_check=True)
                return ins

            def experts(i, ks=range(8)):
                for k in ks:
                    n = i * 8 + (V0 + k)
                    pe.wait_ge(hi_done, n + 1)
                    pe.wait_ge(lo_done, n + 1)
                    if k % VB == 0:
                        pe.wait_ge(wlow_done, i * 2 + (k // VB + 1))
                    first = isinstance(i, int) and i == 0 and k == 0
                    if first:
                        pe.wait_ge(tab_out, S // TB)
                    products(k, 1, first)
                    if first:
                        pe.wait_ge(hid_scaled, PEER_NK // 2)
                    products(k, 0, first).then_inc(unit_done, 1)

            experts(0)
            with pe.Fori(1, U_IT - 1) as i:
                experts(i)
            experts(U_IT - 1, range(VB))
            pe.wait_ge(hi_done, UNITS)
            pe.wait_ge(lo_done, UNITS)
            pe.wait_ge(wlow_done, 2 * U_IT)
            for t in range(NT):
                for k in range(VB, 8):
                    ins = products(k, t, last=k == 7)
                ins.then_inc(acc_done, 1)

        @block.vector
        def _(dve):
            for s in (g_y, g_ylo, g_att, mx_done, o_lo, pt_v, m_done, m_lo, x1_done, x_lo):
                dve.sem_inc(s, FIRST)
            step = Steps(dve, v_step)

            def lo(n, s):
                dve.wait_ge(hi_done, n + 1)
                wait = n - (SPLIT - 1)
                if not (isinstance(wait, int) and wait <= 0):
                    dve.wait_ge(unit_done, wait)
                dve.tensor_tensor(w_lo[:, s % SPLIT, :], w_raw[:, s % RAW, :], w_hi[:, s % SPLIT, :].bitcast(F32), ALU.subtract).then_inc(lo_done, 1)

            def lower(dst, src, up, n, s, value):
                dve.wait_ge(s, value)
                return dve.tensor_tensor(dst, src, up.bitcast(F32), ALU.subtract)

            def rope(x, rot, n):
                cs = cos_t[:, :, None, :].to_broadcast([P, NT, n, HALF])
                sn = sin_t[:, :, None, :].to_broadcast([P, NT, n, HALF])
                x1, x2 = x[:, :, 0:n, 0:HALF], x[:, :, 0:n, HALF:ROT]
                dve.tensor_tensor(rot[:, 0], x1, cs, ALU.mult)
                dve.tensor_tensor(rot[:, 1], x2, sn, ALU.mult)
                dve.tensor_tensor(rot[:, 2], x2, cs, ALU.mult)
                step(dve.tensor_tensor(rot[:, 3], x1, sn, ALU.mult))
                dve.tensor_tensor(x1, rot[:, 0], rot[:, 1], ALU.subtract)
                return dve.tensor_tensor(x2, rot[:, 2], rot[:, 3], ALU.add)

            def refine(r, v, n=NT):
                t = newton[:, 0:n]
                step(dve.tensor_tensor(t, r, r, ALU.mult))
                step(dve.tensor_tensor(t, t, v, ALU.mult))
                step(dve.tensor_scalar(t, t, -0.5, 1.5, ALU.mult, ALU.add))
                return dve.tensor_tensor(r, r, t, ALU.mult)

            dve.memset(stat[:, 12:13], EPS)
            dve.wait_ge(g1_in, 16)
            for q in range(4):
                c = slice(4 * q, 4 * q + 4)
                dve.wait_ge(xT_in[q], 16)
                dve.tensor_tensor(xgT[:, c, :], xgT[:, c, :], g1[:, c, None].to_broadcast([P, 4, S]), ALU.mult).then_inc(xg_done, 1)
                dve.wait_ge(h_hi, q + 1)
                dve.tensor_tensor(hT_lo[:, c, :], xgT[:, c, :], hT_hi[:, c, :].bitcast(F32), ALU.subtract).then_inc(h_lo, 1)
                if q < AHEAD:
                    lo(q, q)
            lo(AHEAD, AHEAD)
            lo(AHEAD + 1, AHEAD + 1)
            dve.wait_ge(ssq1, 2)
            dve.tensor_scalar(stat[:, 2:4], stat[:, 0:2], 1.0 / D, EPS, ALU.mult, ALU.add).then_inc(ms1_done, 1)
            dve.wait_ge(const_in, 80)
            step(dve.tensor_copy(pos_f[:, :], pos_i[:, :]))
            for t in range(NT):
                ins = dve.tensor_scalar(ang[:, t, :], inv_f[:, :], pos_f[:, t:t + 1], None, ALU.mult)
            step(ins)
            step(dve.tensor_scalar(turns[:, :, :], ang[:, :, :], float(1 / (2 * np.pi)), None, ALU.mult))
            step(dve.tensor_scalar(turns[:, :, :], turns[:, :, :], ROUND, None, ALU.add))
            step(dve.tensor_scalar(turns[:, :, :], turns[:, :, :], ROUND, None, ALU.subtract))
            for part in TWO_PI:
                step(dve.scalar_tensor_tensor(ang[:, :, :], turns[:, :, :], -part, ang[:, :, :], ALU.mult, ALU.add))
            dve.tensor_scalar(ang[:, :, :], ang[:, :, :], 3.1415925, -3.1415925, ALU.min, ALU.max).then_inc(ang_ready, 1)
            lo(AHEAD + 2, AHEAD + 2)
            dve.wait_ge(sq1_done, 1)
            step(dve.reciprocal(rstd1[:, :], stat[:, 4:6]))
            refine(rstd1[:, :], stat[:, 2:4]).then_inc(rs1_done, 1)
            lo(AHEAD + 3, AHEAD + 3)
            dve.wait_ge(trig_done, 2)
            step(dve.tensor_tensor(cos_t[:, :, :], turns[:, :, :], turns[:, :, :], ALU.mult))
            step(dve.tensor_scalar(cos_t[:, :, :], cos_t[:, :, :], -2.0, 1.0, ALU.mult, ALU.add))
            for k in range(UPB):
                lo(UPB + k + AHEAD, k + AHEAD)
            for k in range(2 * UPB):
                lo(2 * UPB + k + AHEAD, k + AHEAD)
                if k == 1:
                    dve.memset(bT[:, GLA_H, :], 0.0)
                    dve.wait_ge(pe_prep, 2)
                    dve.wait_ge(prep_in, 64)
                    for h in range(GLA_H):
                        dve.tensor_scalar(zT[:, h * S:(h + 1) * S], psum[:, 4 + h // 2, (h % 2) * S:(h % 2 + 1) * S], b_decay[:, h:h + 1], None,
                                          ALU.add).then_inc(dve_prep, 1)
                    dve.wait_ge(act_prep, 2)
                    dve.scalar_tensor_tensor(zT, zT, 0.0, zA, ALU.min, ALU.subtract).then_inc(dve_prep, 1)
                    dve.wait_ge(dve_prep, 5)
                    for h in range(GLA_H):
                        dve.tensor_tensor_scan(bT[:, h, :], zT[:, h * S:(h + 1) * S], zT[:, h * S:(h + 1) * S], 0.0, ALU.add, ALU.bypass).then_inc(dve_prep, 1)
                if k == 2:
                    dve.wait_ge(kvc_in, 32)
                    rope(kv_c[:, 0, :, :].rearrange("p t (g d) -> p t g d", d=DH), rot_c, NSA_G).then_inc(dve_prep, 1)
                if k == 4:
                    dve.wait_ge(act_prep, 4)
                    for a in range(2):
                        for half in range(CMP_BLOCK // CMP_STRIDE):
                            o = half * CMP_STRIDE
                            ins = dve.tensor_tensor(blk_c[:, a, o:o + CMP_STRIDE, :, :],
                                                    kvT_c[:, a, :, o:o + NCMP * CMP_STRIDE].rearrange("p g (n b) -> p b g n", b=CMP_STRIDE),
                                                    posT[:, a, o:o + CMP_STRIDE, None, None].to_broadcast([P, CMP_STRIDE, NSA_G, NCMP]), ALU.add)
                    ins.then_inc(dve_prep, 1)
            with dve.Fori(2, A_BLOCKS // 2) as i:
                for k in range(2 * UPB):
                    lo(i * 8 + (k + AHEAD), k + AHEAD)

            def gla_slot(h, k):
                if k == 0:
                    dve.wait_ge(g_exp, h + 1)
                    dve.wait_ge(g_qe, h + 1)
                    dve.tensor_copy(kT_g[:, :], psum[:, 4, S:2 * S]).then_inc(g_ke, 1)
                    dve.wait_ge(g_ke, h + 1)
                    rest = NL - KL_POOL
                    dve.tensor_tensor(kL[:, KL_POOL:NL, :], dec[:, KL_POOL:NL, :], kT_g[:, None, :].to_broadcast([P, rest, S]), ALU.mult)
                    dve.tensor_tensor(qL[:, :, :], dec[:, :, :], qT_g[:, None, :].to_broadcast([P, NL, S]), ALU.mult).then_inc(g_ql, 1)
                if k in (1, 2):
                    t = k - 1
                    dve.wait_ge(g_lev, h * 2 + (t + 1))
                    step(dve.tensor_tensor(att_m[:, :, :], psum[:, 5:7, :].rearrange("p b (l t) -> p (b l) t", t=P), masks[:, :, :], ALU.mult))
                    dve.tensor_reduce(att_T[:, t, :], att_m[:, :, :].rearrange("p l t -> p t l"), AX.X, ALU.add).then_inc(g_att, 1)
                    dve.wait_ge(g_att, h * 2 + (t + 1) + FIRST)
                    if t == 0:
                        dve.tensor_copy(att_T[:, 2, :], psum[:, 4, 0:P]).then_inc(g_a01, 1)
            def gla_output(h):
                dve.wait_ge(g_rn, h + 1)
                step(dve.tensor_scalar(gst[:, 6:8], gst[:, 0:2], 1.0 / GLA_DV, EPS, ALU.mult, ALU.add))
                step(dve.reciprocal(gst[:, 4:6], gst[:, 2:4]))
                step(refine(gst[:, 4:6], gst[:, 6:8]))
                for t in range(NT):
                    ins = dve.scalar_tensor_tensor(y_g[:, t, :], psum[:, 7, t * GLA_DV:(t + 1) * GLA_DV], gst[:, 4 + t:5 + t], gnorm[:, :], ALU.mult, ALU.mult)
                step(ins)
                dve.wait_ge(g_silu, h + 1)
                dve.tensor_tensor(y_g[:, :, :], y_g[:, :, :], sig_g[:, :, :], ALU.mult).then_inc(g_y, 1)

            def gla_lower(h):
                up = ygT_hi[:, ds(h * 2, 2), :].rearrange("p c t -> p (c t)")
                dve.wait_ge(g_yhi, h + 1 + FIRST)
                dve.tensor_tensor(ygT_lo[:, ds(h * 2, 2), :].rearrange("p c t -> p (c t)"), psum[:, 4, :], up.bitcast(F32), ALU.subtract).then_inc(g_ylo, 1)

            dve.wait_ge(g_msk, 32)
            dve.memset(dec[:, LDIAG, :], 1.0).then_inc(g_one, 1)
            base = A_BLOCKS * UPB
            with dve.Fori(0, GLA_H // 2) as i:
                step.enter(i, 0, 2 * 9)
                for hp in range(2):
                    for k in range(UPB):
                        if k == 3:
                            gla_output(i * 2 + hp)
                        if k in (0, 2):
                            gla_slot(i * 2 + hp, k)
                        lo(i * 8 + (base + hp * 4 + k + AHEAD), k + AHEAD)
                        if k == 1:
                            gla_slot(i * 2 + hp, k)
                    gla_lower(i * 2 + hp)
                step.leave(GLA_H // 2)

            def scores_max(h, j):
                q = j % 2
                wait_alone(dve, s_done, h + 1)
                for t in range(NT):
                    n = (t + 1) * P
                    for b in range(2):
                        o = 2 * P * t + b * n
                        dve.tensor_tensor_reduce(sm[:, q, o:o + n], psum[:, 4 + t, b * n:(b + 1) * n], tri[:, S - n:S], 1.0, -3e38,
                                                 ALU.add, ALU.max, mx[:, q, t, b + 1:b + 2])
                    ins = dve.tensor_tensor_reduce(smc[:, q, t, :], psum[:, 4, S + 16 * t:S + 16 * t + NCMP], cmask[:, t, :], 1.0, -3e38,
                                                   ALU.add, ALU.max, mx[:, q, t, 0:1])
                step(ins)
                dve.tensor_scalar(nmx[:, q, :, :], mx[:, q, :, :], MASKED_MAX, -SCALE, ALU.max, ALU.mult).then_inc(mx_done, 1)

            def probs(h, j):
                q = j % 2
                dve.wait_ge(exp_done, h * 6 + 6)
                step(dve.tensor_scalar(wts[:, q, :, :], sums[:, q, :, :], 1e-30, None, ALU.max))
                step(dve.reciprocal(wts[:, q, :, :], wts[:, q, :, :]))
                step(dve.tensor_tensor(wts[:, q, :, :], wts[:, q, :, :], g_n[:, :, 3 * j:3 * j + 3], ALU.mult))
                for t in range(NT):
                    for b in range(3):
                        n = (t + 1) * P
                        o = 2 * P * t + b * n
                        w = (b + 1) % 3
                        x = smc[:, q, t, :] if b == 2 else sm[:, q, o:o + n]
                        ins = dve.tensor_scalar(x, x, wts[:, q, t, w:w + 1], None, ALU.mult)
                ins.then_inc(p_done, 1)

            base = (A_BLOCKS + 4) * UPB
            with dve.Fori(0, NSA_G) as g:
                step.enter(g, 0, 2 + 4 * 4)
                for k in range(8):
                    if 0 <= k - 3 < NSA_HPG:
                        probs(g * NSA_HPG + (k - 3), k - 3)
                    if k < 2:
                        lo(g * 8 + (base + k + AHEAD), k + AHEAD)
                    if k == 0:
                        step(dve.tensor_copy(g_n[:, :, :], gates[:, :, ds(g * 3 * NSA_HPG, 3 * NSA_HPG)]))
                        dve.wait_ge(nqk_in, g * 48 + 48)
                        rope(qk_n, rot_n, NSA_HPG + 2).then_inc(roped, 1)
                    if k == 1:
                        dve.wait_ge(qkt_done, g + 1 + FIRST)
                        dve.tensor_copy(qkT[:, 4:6, :].rearrange("p h t -> p (h t)"), psum[:, 6, :]).then_inc(qkt_v, 1)
                    if 0 <= k - 4 < NSA_HPG:
                        h = g * NSA_HPG + (k - 4)
                        up = ynT_hi[:, ds(h, 1), :].rearrange("p a t -> p (a t)")
                        dve.wait_ge(o_hi, h + 1 + FIRST)
                        dve.tensor_tensor(ynT_lo[:, ds(h, 1), :].rearrange("p a t -> p (a t)"), psum[:, 6, S:2 * S], up.bitcast(F32), ALU.subtract).then_inc(o_lo, 1)
                    if 0 <= k - 2 < NSA_HPG:
                        scores_max(g * NSA_HPG + (k - 2), k - 2)
                    if k >= 2:
                        lo(g * 8 + (base + k + AHEAD), k + AHEAD)
                    if 0 <= k - 3 < NSA_HPG:
                        dve.wait_ge(pt_done, g * NSA_HPG + (k - 3) + 1)
                        dve.tensor_copy(pT[:, :, P:S], psum[:, 7, :].rearrange("p (a t) -> p a t", t=P)).then_inc(pt_v, 1)
                step.leave(NSA_G)

            def merged_lower(nb):
                dve.wait_ge(m_hi, nb + 1 + FIRST)
                dve.tensor_tensor(mT_lo[:, ds(nb * 4, 4), :].rearrange("p c t -> p (c t)"), psum[:, 4:6, :].rearrange("p b n -> p (b n)"),
                                  mT_hi[:, ds(nb * 4, 4), :].rearrange("p c t -> p (c t)").bitcast(F32), ALU.subtract).then_inc(m_lo, 1)

            def x_lower(b):
                dve.wait_ge(x_hi, b + 1 + FIRST)
                dve.tensor_tensor(h2T_lo[:, ds(b * 4, 4), :].rearrange("p c t -> p (c t)"), psum[:, 4:6, :].rearrange("p b n -> p (b n)"),
                                  h2T_hi[:, ds(b * 4, 4), :].rearrange("p c t -> p (c t)").bitcast(F32), ALU.subtract).then_inc(x_lo, 1)

            base = PROJ_BLOCKS * UPB
            dve.wait_ge(stored[0], 16 * PROJ_BLOCKS // 2)
            dve.wait_ge(stored[1], 16 * PROJ_BLOCKS // 2)
            with dve.Fori(0, 2) as i:
                step.enter(i, 0, 2)
                for nbp in range(2):
                    nb = i * 2 + nbp
                    for k in range(6):
                        n = i * 12 + (base + nbp * 6 + k + 1)
                        if k == UPG - 1:
                            dve.wait_ge(gab_sig, nb + 1)
                            dve.wait_ge(unit_done, n)
                            dve.tensor_tensor(mrg[:, 0, :, :], psum[:, 0:2, :], gab[:, 0, :, :], ALU.mult).then_inc(m_done, 1)
                        if k == UPG + UPB - 1:
                            dve.wait_ge(unit_done, n)
                            step(dve.tensor_tensor(mrg[:, 1, :, :], psum[:, 2:4, :], gab[:, 1, :, :], ALU.mult))
                            dve.tensor_tensor(mrg[:, 1, :, :], mrg[:, 1, :, :], mrg[:, 0, :, :], ALU.add).then_inc(m_done, 1)
                        lo(i * 12 + (base + nbp * 6 + k + AHEAD), nbp * 6 + k + AHEAD)
                        if (nbp, k) == (1, 0):
                            merged_lower(nb - 1)
                merged_lower(nb)
                step.leave(2)

            base = PROJ_BLOCKS * UPB + 4 * (UPG + UPB)
            dve.wait_ge(xn_in, 32)
            dve.wait_ge(g2_in, 16)
            with dve.Fori(0, 2) as i:
                for par in range(2):
                    b = i * 2 + par
                    for k in range(UPB):
                        n = i * 8 + (base + par * 4 + k + 1)
                        if k == UPB - 1:
                            dve.wait_ge(unit_done, n)
                            x = x_nat[:, :, ds(b * NB, NB)]
                            dve.tensor_tensor(x, x, psum[:, 2 * par:2 * par + 2, :], ALU.add).then_inc(x1_done, 1)
                            dve.wait_ge(x1_done, b + 1 + FIRST)
                            for t in range(NT):
                                ins = dve.tensor_tensor(mrg[:, 1, t, :], x_nat[:, t, ds(b * NB, NB)], g2[:, ds(b * NB, NB)], ALU.mult)
                            ins.then_inc(xg2_done, 1)
                        lo(i * 8 + (base + par * 4 + k + AHEAD), k + AHEAD)
                        if (par, k) == (1, 0):
                            x_lower(b - 1)
                x_lower(b)

            base = PROJ_BLOCKS * UPB + 4 * (UPG + UPB) + 4 * UPB
            dve.wait_ge(sq2, 8)
            step(dve.tensor_reduce(stat[:, 6:8], sq_x1[:, :, :], AX.X, ALU.add))
            dve.tensor_scalar(stat[:, 8:10], stat[:, 6:8], 1.0 / D, EPS, ALU.mult, ALU.add).then_inc(ms2_done, 1)
            dve.memset(ones[:, :], 1.0).then_inc(rsd_done, 1)
            lo(base + AHEAD, AHEAD)
            dve.wait_ge(sq2_done, 1)
            step(dve.reciprocal(rstd2[:, :], stat[:, 10:12]))
            refine(rstd2[:, :], stat[:, 8:10]).then_inc(rs2_done, 1)
            dve.wait_ge(rs2_done, 1)
            for t in range(NT):
                ins = dve.tensor_scalar(rs_diag[:, t, :], ident[:, :], rstd2[:, t:t + 1], None, ALU.mult)
            ins.then_inc(rsd_done, 1)
            for n in range(base + AHEAD + 1, U0 + AHEAD - 1):
                lo(n, n % 4)
            dve.wait_ge(rs_row_done, 1)
            dve.tensor_copy(rs_row[:, :], psum[:, 0, 0:S]).then_inc(rs_row_out, 1)
            lo(U0 + AHEAD - 1, AHEAD - 1)

            ROUTE = 20
            def top16(values, cut, top, index):
                step(dve.max(top[:, 0:8], values), alone=True)
                dve.max_index(index[:, 0:8], top[:, 0:8], values)
                step(dve.match_replace(cut, top[:, 0:8], values, -3e38), alone=True)
                step(dve.max(top[:, 8:16], cut), alone=True)
                step(dve.max_index(index[:, 8:16], top[:, 8:16], cut), alone=True)

            def route(u, part):
                if part in (0, 1):
                    if part == 0:
                        step(dve.tensor_copy(s_now[:, :, :].rearrange("p a n -> p (a n)"), sc[:, ds(u, 1), :].rearrange("p a n -> p (a n)")), alone=True)
                    top16(s_now[:, part, :], s_cut[:, part, :], v_top[:, part, :], i_top[:, part, :])
                if part == 2:
                    dve.tensor_copy(if_top[:, :, :], i_top[:, :, :])
                    step(dve.tensor_tensor(cand[:, :, :], v_top[:, 0, :, None].to_broadcast([P, TOPK, TOPK]),
                                           v_top[:, 1, None, :].to_broadcast([P, TOPK, TOPK]), ALU.add), alone=True)
                    top16(cand[:, :, :].rearrange("p a b -> p (a b)"), cand_cut[:, :, :].rearrange("p a b -> p (a b)"), vals[:, :], flat[:, :])
                    dve.tensor_scalar(rst[:, 0:1], vals[:, 0:1], -1.0, None, ALU.mult).then_inc(r_vals, 1)
                if part == 3:
                    dve.tensor_scalar(ab[:, 0, :], flat[:, :], 4, None, ALU.logical_shift_right)
                    step(dve.tensor_scalar(ab[:, 1, :], flat[:, :], TOPK - 1, None, ALU.bitwise_and))
                    step(dve.tensor_copy(abf[:, :, :], ab[:, :, :]))
                    for a in range(2):
                        ins = dve.tensor_tensor(hot[:, a, :, :], abf[:, a, :, None].to_broadcast([P, TOPK, TOPK]),
                                                iota[:, None, 0:TOPK].to_broadcast([P, TOPK, TOPK]), ALU.is_equal)
                    step(ins)
                    for a in range(2):
                        ins = dve.tensor_tensor(hot[:, a, :, :], hot[:, a, :, :], if_top[:, a, None, :].to_broadcast([P, TOPK, TOPK]), ALU.mult)
                    step(ins)
                    step(dve.tensor_reduce(e12[:, :, :], hot[:, :, :, :], AX.X, ALU.add))
                    dve.tensor_copy(rt[:, 0:2, ds(u, 1), :].rearrange("p w u k -> p w (u k)"), e12[:, :, :])
                    dve.wait_ge(r_exp, u + 1)
                    step(dve.reciprocal(rst[:, 2:3], rst[:, 1:2]))
                    dve.tensor_scalar(rt[:, 2, ds(u, 1), :].rearrange("p u k -> p (u k)"), rexp[:, :], rst[:, 2:3], None, ALU.mult).then_inc(routed, 1)

            def picks_hot(tb, half, prior, parts=range(5)):
                hot1, hot2 = hots[half]
                for part in parts:
                    if part == 0:
                        if prior is not None:
                            dve.wait_ge(hot2_done, tb)
                            dve.wait_ge(tab_done, prior)
                        dve.tensor_copy(rt16[:, :, :], rtT[:, :, ds(tb * TB, TB)]).then_inc(rt16_done, 1)
                        dve.wait_ge(rt16_done, tb + 1)
                        dve.tensor_tensor(hot1[:, :, :], iota[:, None, :].to_broadcast([P, TB, PEER_NK]),
                                          rt16[:, 0, :, None].to_broadcast([P, TB, PEER_NK]), ALU.is_equal).then_inc(hot1_done, 1)
                    else:
                        for j in range((part - 1) * TB // 4, part * TB // 4):
                            ins = dve.tensor_scalar(hot2[:, j, :], iota[:, :], rt16[:, 1, j:j + 1], rt16[:, 2, j:j + 1], ALU.is_equal, ALU.mult)
                        if part == 4:
                            ins.then_inc(hot2_done, 1)

            def weights(m, half):
                x = h_in[:, half, :, :]
                dve.tensor_tensor(x.rearrange("p c (b t) -> p c b t", t=TB), x.rearrange("p c (b t) -> p c b t", t=TB),
                                  g_tab[:, :, half * VB:(half + 1) * VB, :].rearrange("p b c t -> p c b t"), ALU.mult).then_inc(prod_done, 1)
                dve.wait_ge(wup_done, m + 1)
                dve.tensor_tensor(w_low[:, half, :, :], x, w_up[:, half, :, :].bitcast(F32), ALU.subtract).then_inc(wlow_done, 1)

            def hidden(i, routes=False, one=False, two=False):
                for k in range(8):
                    if routes:
                        route(i * 2 + k // 4, k % 4)
                    if k < 5 and one:
                        first = isinstance(i, int) and i == I_T1
                        if first and k == 0:
                            dve.wait_ge(rt_out, 1)
                        picks_hot(i - I_T1, 0, None if first else i - I_T1, [k])
                    if k % 4 == 0 and two:
                        tb = i * 2 + (k // 4 - I_T2 - I_T1)
                        first = isinstance(i, int) and i == I_T2
                        if first and k == 0:
                            dve.wait_ge(rt_out, 2)
                        picks_hot(tb, k // 4, I_T2 - I_T1 if first else tb - 1)
                    lo(i * 8 + (U0 + k + AHEAD), k + AHEAD)
                    if k % 2 == 1:
                        m = i * 4 + k // 2
                        dve.wait_ge(unit_done, i * 8 + (U0 + k + 1))
                        if not (isinstance(i, int) and m < 2):
                            dve.wait_ge(hid_gelu, m - 1)
                        dve.tensor_tensor(hs[:, k // 2 % 2, :].rearrange("p (a t) -> p a t", a=2), psum[:, k // 2, :].rearrange("p (a t) -> p a t", a=2),
                                          rs_row[:, None, :].to_broadcast([P, 2, S]), ALU.mult).then_inc(hid_scaled, 1)
                    if k == 4 and isinstance(i, int) and i == U_IT - 1:
                        dve.wait_ge(v_in, 32)
                        weights(0, 0)

            dve.wait_ge(iota_in, 16)
            dve.wait_ge(rs_row_out, 1)
            dve.wait_ge(sc_out, 4)
            hidden(0, routes=True)
            with dve.Fori(1, I_T1) as i:
                step.enter(i, 1, 2 * ROUTE)
                hidden(i, routes=True)
                step.leave(I_T1 - 1)
            hidden(I_T1, routes=True, one=True)
            with dve.Fori(I_T1 + 1, I_T2) as i:
                step.enter(i, I_T1 + 1, 2 * ROUTE)
                hidden(i, routes=True, one=True)
                step.leave(I_T2 - I_T1 - 1)
            hidden(I_T2, two=True)
            with dve.Fori(I_T2 + 1, I_T3) as i:
                hidden(i, two=True)
            for i in range(I_T3, U_IT):
                hidden(i)

            def experts_out(i, last=False):
                for k in range(8):
                    if not (last and k + AHEAD >= 8):
                        lo(i * 8 + (V0 + k + AHEAD), k + AHEAD)
                    if k == 0:
                        dve.wait_ge(unit_done, i * 8 + V0)
                        weights(i * 2 + 1, 1)
                    if k == 4 and not last:
                        dve.wait_ge(unit_done, i * 8 + (V0 + 4))
                        dve.wait_ge(v_in, i * 32 + 64)
                        weights(i * 2 + 2, 0)

            experts_out(0)
            with dve.Fori(1, PEER_NK // 8 - 1) as i:
                experts_out(i)
            experts_out(PEER_NK // 8 - 1, True)

            dve.wait_ge(gf_in, 16)
            for t in range(NT):
                dve.wait_ge(acc_done, t + 1)
                dve.tensor_tensor(x_nat[:, t, :], x_nat[:, t, :], psum[:, 4 * t:4 * t + 4, :].rearrange("p b n -> p (b n)"), ALU.add).then_inc(x2_done, 1)
                dve.wait_ge(fsq, t + 1)
                dve.tensor_scalar(stat[:, 2 + t:3 + t], stat[:, t:t + 1], 1.0 / D, EPS, ALU.mult, ALU.add).then_inc(fms, 1)
                dve.wait_ge(frs, t + 1)
                step(dve.reciprocal(stat[:, 6 + t:7 + t], stat[:, 4 + t:5 + t]))
                step(refine(stat[:, 6 + t:7 + t], stat[:, 2 + t:3 + t], 1))
                dve.scalar_tensor_tensor(out_t[:, t, :], x_nat[:, t, :], stat[:, 6 + t:7 + t], gf[:, :], ALU.mult, ALU.mult).then_inc(out_done, 1)


ROUND = float(3 << 22)
TWO_PI = (6.28125, 0.0019350051879882812, float(2 * np.pi - 6.28125 - 0.0019350051879882812))


def _gla_masks():
    s, t = np.arange(P)[:, None], np.arange(P)[None, :]
    levels = [(s // (2 * m) == t // (2 * m)) & (s % (2 * m) < m) & (t % (2 * m) >= m) for m in LEVELS]
    return np.stack([*levels, s == t], axis=1).astype(np.float32)


def _shape_constants():
    t = np.arange(S)
    tri = np.zeros((P, S), np.float32)
    tri[:, P:] = np.where(np.arange(P)[None, :] <= np.arange(P)[:, None], 0.0, MASKED)
    end = np.arange(NCMP) * CMP_STRIDE + CMP_BLOCK - 1
    cmask = np.where(end[None, :] <= t[:, None], 0.0, MASKED).astype(np.float32)
    inv = np.power(np.float32(ROPE_THETA), -(np.arange(0, ROT, 2, dtype=np.float32) / np.float32(ROT)))
    return {
        "ident": np.eye(P, dtype=np.float32), "tri": tri, "cmask": cmask.reshape(NT, P, NCMP).transpose(1, 0, 2),
        "inv_f": inv.astype(np.float32)[None, :], "gla_masks": _gla_masks(),
        "iota": np.arange(PEER_NK, dtype=np.float32)[None, :],
    }


def _blocks(w):
    k, n = w.shape
    return w.reshape(k // (CU * P), CU, P, n // NB, NB).transpose(3, 0, 2, 1, 4).reshape(n // NB, k // (CU * P), P, UW)


def _layout(a):
    w = a["w_in"][0]
    gate, gqk, glr, gr, ga = 5120, 5168, 7216, 7232, 8256
    order = np.concatenate([w[:, 2048:3072], w[:, gqk:glr], w[:, gr:ga], w[:, 3072:5120], w[:, 0:2048], w[:, ga:]], axis=1)
    u = a["peer_u"][0].reshape(PEER_NK, PEER_NK, KC, P).transpose(1, 3, 2, 0)
    v = a["peer_v"][0].reshape(PEER_NK, PEER_NK, D).transpose(1, 0, 2)
    gla, nsa = _blocks(a["w_up_gla"][0]), _blocks(a["w_up_nsa"][0])
    merge = np.concatenate([gla, nsa], axis=1)
    units = np.concatenate([x.reshape(-1, P, UW) for x in (_blocks(order), merge, _blocks(a["w_out"][0]), _blocks(a["peer_w_q"][0]), u, v)])
    small = np.concatenate([w[:, glr:gr], w[:, gate:gqk]], axis=1).reshape(KC, P, 64).transpose(1, 0, 2)
    x = a["x"][0]
    keys = np.zeros((P, PEER_H, 2 * PEER_NK), np.float32)
    keys[:PEER_DK // 2, :, :PEER_NK] = a["peer_sub_k1"][0].transpose(2, 0, 1)
    keys[PEER_DK // 2:, :, PEER_NK:] = a["peer_sub_k2"][0].transpose(2, 0, 1)
    w1 = np.stack([a["nsa_cmp_k_w1"][0], a["nsa_cmp_v_w1"][0]]).reshape(2, 4, CMP_BLOCK // 4, DH, DH)
    return {
        "x": x.reshape(NT, P, D).transpose(1, 0, 2), "xT": x.T.reshape(KC, P, S).transpose(1, 0, 2),
        "positions": a["positions"].reshape(NT, P).T, "g1": a["norm1_g"][0].reshape(KC, P).T,
        "w_small": small, "w_units": units, "w_decay": a["gla_w_decay"][0], "b_decay": a["gla_b_decay"][0].reshape(GLA_H, P).T,
        "posT": np.stack([a["nsa_cmp_pos_k"][0], a["nsa_cmp_pos_v"][0]]).transpose(2, 0, 1),
        "w1": w1.transpose(0, 1, 3, 2, 4).reshape(8, DH, CMP_BLOCK // 4, DH),
        "w2": np.stack([a["nsa_cmp_k_w2"][0], a["nsa_cmp_v_w2"][0]], axis=1),
        "gla_g": a["gla_norm_g"], "g2": a["norm2_g"], "gf": a["final_g"][None, :], "keys": keys,
    }


def kernel(**inputs):
    import concourse.bacc as bacc
    from concourse.bass_utils import run_bass_kernel_spmd as run

    nc = bacc.Bacc("TRN2", target_bir_lowering=False, num_devices=1)
    laid = {**_layout({k: np.asarray(v) for k, v in inputs.items()}), **_shape_constants()}
    arrays = {f"in_{name}": np.ascontiguousarray(a) for name, a in laid.items()}
    io = {name: nc.dram_tensor(f"in_{name}", arrays[f"in_{name}"].shape, mybir.dt.from_np(arrays[f"in_{name}"].dtype), kind="ExternalInput").ap()
          for name in laid}
    io["out"] = nc.dram_tensor("out_0", (S, D), F32, kind="ExternalOutput").ap()
    hybrid_block(nc, io)
    r = run(nc, [arrays], core_ids=[0])
    return r.results[0]["out_0"].reshape(1, S, D)
```
